# Optimizing a Trainium2 kernel written in Bass

```python
import math
import jax
import jax.numpy as jnp
from jax import lax
import numpy as np

D_MODEL = 1024
BATCH = 1
SEQ = 512
DEPTH = 4
DEC_BATCH = 8
DEC_SEQ = 4
PAST_LEN = 256
PAGE_SIZE = 128

N_MIXERS = 3
N_HG_LAYERS = (DEPTH + 2) // 3
N_AT_LAYERS = (DEPTH + 1) // 3
N_RW_LAYERS = DEPTH // 3

HG_HEADS = 8
HG_DK = 128
HG_DV = D_MODEL // HG_HEADS
HG_FDIM = HG_HEADS * HG_DK
HG_CHUNK = 64
HG_F_MIN = 1e-30

AT_HEADS = 8
AT_HD = D_MODEL // AT_HEADS // 2
AT_QBLK = 128
SUBLN_EPS = 1e-5

RW_HEAD = 64
RW_HEADS = D_MODEL // RW_HEAD
RW_DECAY_LORA = 64
RW_AAA_LORA = 64
RW_GATE_LORA = 128
RW_GN_EPS = 64e-5

D_FF = 256 * ((8 * D_MODEL + 3 * 256 - 1) // (3 * 256))
RMS_EPS = 1e-6

kernel_name = 'hybrid_hgrn2_diffattn_rwkv7_decode_step'

def rms_norm(x, g, eps=RMS_EPS):
    xf = x.astype(jnp.float32)
    y = xf * lax.rsqrt(jnp.mean(xf * xf, axis=-1, keepdims=True) + eps)
    return (y * g.astype(jnp.float32)).astype(x.dtype)

def swiglu(x, w_in, w_out):
    gate, up = jnp.split(x @ w_in, 2, axis=-1)
    return (jax.nn.silu(gate) * up) @ w_out

def alibi_slopes(n_heads):
    return jnp.exp2(-8.0 * jnp.arange(1, n_heads + 1, dtype=jnp.float32) / n_heads)

def _hgrn2_chunked(q, k, v, log_f, S0):
    B, T, H, DK = q.shape
    DV = v.shape[-1]
    C = math.gcd(T, HG_CHUNK)
    N = T // C

    def to_chunks(a):
        return a.reshape(B, N, C, H, a.shape[-1]).transpose(1, 0, 3, 2, 4)

    causal = jnp.tril(jnp.ones((C, C), dtype=bool))[None, None, :, :, None]

    def step(S, xs):
        qc, kc, vc, gc = xs
        b = jnp.cumsum(gc, axis=2)
        rel = jnp.where(causal, b[:, :, :, None, :] - b[:, :, None, :, :], -jnp.inf)
        A = jnp.einsum('bhtk,bhtsk,bhsk->bhts', qc, jnp.exp(rel), kc)
        o = (jnp.einsum('bhtk,bhkv->bhtv', qc * jnp.exp(b), S)
             + jnp.einsum('bhts,bhsv->bhtv', A, vc))
        b_last = b[:, :, -1]
        S = (jnp.exp(b_last)[..., None] * S
             + jnp.einsum('bhsk,bhsv->bhkv', kc * jnp.exp(b_last[:, :, None, :] - b), vc))
        return S, o

    S, o = lax.scan(step, S0, (to_chunks(q), to_chunks(k), to_chunks(v), to_chunks(log_f)))
    return o.transpose(1, 0, 3, 2, 4).reshape(B, T, H, DV), S

def hgrn2_mixer(h, S0, w_in, lb, g_norm, w_out):
    B, T, _ = h.shape
    f32 = jnp.float32
    q, fz, i, g = jnp.split(h @ w_in, [HG_FDIM, 2 * HG_FDIM, 2 * HG_FDIM + D_MODEL], axis=-1)
    fz = fz.astype(f32)
    lb = lb.astype(f32)
    f = lb + (1.0 - lb) * jax.nn.sigmoid(fz)
    log_f = jnp.log(jnp.maximum(f, HG_F_MIN))
    k = (1.0 - lb) * jax.nn.sigmoid(-fz)
    q = jax.nn.silu(q.astype(f32))

    def heads(t, d):
        return t.reshape(B, T, HG_HEADS, d)

    o, S = _hgrn2_chunked(heads(q, HG_DK), heads(k, HG_DK), heads(i.astype(f32), HG_DV),
                          heads(log_f, HG_DK), S0.astype(f32))
    o = o.reshape(B, T, D_MODEL).astype(h.dtype) * jax.nn.sigmoid(g)
    return rms_norm(o, g_norm) @ w_out, S

def diff_attn_heads(q, k, v, q_pos, k_pos, lam, slopes):
    s = jnp.einsum('bqhcd,bkhcd->bhcqk', q, k).astype(jnp.float32) * (AT_HD ** -0.5)
    dist = q_pos[:, None] - k_pos[None, :]
    bias = -slopes[:, None, None] * dist.astype(jnp.float32)[None]
    s = jnp.where(dist >= 0, s + bias[None, :, None], -jnp.inf)
    p = jax.nn.softmax(s, axis=-1)
    attn = p[:, :, 0] - lam * p[:, :, 1]
    return jnp.einsum('bhqk,bkhe->bqhe', attn.astype(v.dtype), v)

def diff_attn_blocked(q, k, v, q_pos, k_pos, lam, slopes):
    B, Tq = q.shape[:2]
    QB = math.gcd(Tq, AT_QBLK)
    NB = Tq // QB
    qb = q.reshape(B, NB, QB, AT_HEADS, 2, AT_HD).swapaxes(0, 1)
    pb = q_pos.reshape(NB, QB)
    ob = lax.map(lambda a: diff_attn_heads(a[0], k, v, a[1], k_pos, lam, slopes), (qb, pb))
    return ob.swapaxes(0, 1).reshape(B, Tq, AT_HEADS, 2 * AT_HD)

def diff_attn_mixer(h, past_k, past_v, w_in, lam_vecs, subln, w_out, layer_idx):
    B, T, _ = h.shape
    q, k, v = jnp.split(h @ w_in, 3, axis=-1)
    q = q.reshape(B, T, AT_HEADS, 2, AT_HD)
    k = k.reshape(B, T, AT_HEADS, 2, AT_HD)
    v = v.reshape(B, T, AT_HEADS, 2 * AT_HD)
    if past_k is None:
        P, k_all, v_all = 0, k, v
    else:
        P = past_k.shape[1]
        k_all = jnp.concatenate([past_k.astype(k.dtype), k], axis=1)
        v_all = jnp.concatenate([past_v.astype(v.dtype), v], axis=1)
    lam_init = 0.8 - 0.6 * math.exp(-0.3 * layer_idx)
    lv = lam_vecs.astype(jnp.float32)
    lam = jnp.exp(jnp.sum(lv[0] * lv[1])) - jnp.exp(jnp.sum(lv[2] * lv[3])) + lam_init
    q_pos = P + jnp.arange(T, dtype=jnp.int32)
    k_pos = jnp.arange(P + T, dtype=jnp.int32)
    o = diff_attn_blocked(q, k_all, v_all, q_pos, k_pos, lam, alibi_slopes(AT_HEADS))
    o = rms_norm(o, subln, SUBLN_EPS) * (1.0 - lam_init)
    return o.reshape(B, T, D_MODEL) @ w_out, k.reshape(B, T, AT_HEADS, 2 * AT_HD), v

def _rwkv7_scan(r, decay, k, v, kk, a, S0):
    xs = tuple(t.swapaxes(0, 1) for t in (r, decay, k, v, kk, a))

    def step(S, inp):
        rt, wt, kt, vt, kkt, at = inp
        sk = jnp.einsum('bhij,bhj->bhi', S, kkt)
        S = (S * wt[:, :, None, :] - sk[..., None] * (kkt * at)[:, :, None, :]
             + vt[..., None] * kt[:, :, None, :])
        return S, jnp.einsum('bhij,bhj->bhi', S, rt)

    S, o = lax.scan(step, S0, xs)
    return o.swapaxes(0, 1), S

def rwkv7_mixer(h, h_last, S0, mix, w_rkv, w0, w1, w2, a0, a1, a2, g1, g2,
                k_k, k_a, r_k, ln_w, ln_b, w_o):
    B, T, _ = h.shape
    f32 = jnp.float32
    h_prev = jnp.concatenate([h_last[:, None].astype(h.dtype), h[:, :-1]], axis=1)
    xm = h[:, :, None] + (h_prev - h)[:, :, None] * mix
    rkv = jnp.einsum('btnd,nde->btne', xm[:, :, :3], w_rkv)
    r, k, v = rkv[:, :, 0], rkv[:, :, 1], rkv[:, :, 2]
    xw, xa, xg = xm[:, :, 3], xm[:, :, 4], xm[:, :, 5]
    w = -jax.nn.softplus(-(w0 + jnp.tanh(xw @ w1) @ w2).astype(f32)) - 0.5
    decay = jnp.exp(-jnp.exp(w))
    a = jax.nn.sigmoid((a0 + (xa @ a1) @ a2).astype(f32))
    g = jax.nn.sigmoid(xg @ g1) @ g2

    def heads(t):
        return t.astype(f32).reshape(B, T, RW_HEADS, RW_HEAD)

    kk = heads(k * k_k)
    kk = kk / jnp.maximum(jnp.sqrt(jnp.sum(kk * kk, axis=-1, keepdims=True)), 1e-12)
    r, k, v, decay, a = heads(r), heads(k), heads(v), heads(decay), heads(a)
    k = k * (1.0 + (a - 1.0) * k_a.astype(f32).reshape(RW_HEADS, RW_HEAD))
    o, S = _rwkv7_scan(r, decay, k, v, kk, a, S0.astype(f32))
    mu = jnp.mean(o, axis=-1, keepdims=True)
    var = jnp.mean(jnp.square(o - mu), axis=-1, keepdims=True)
    o = (o - mu) * lax.rsqrt(var + RW_GN_EPS)
    o = (o * ln_w.astype(f32).reshape(RW_HEADS, RW_HEAD)
         + ln_b.astype(f32).reshape(RW_HEADS, RW_HEAD))
    o = o + jnp.sum(r * k * r_k.astype(f32), axis=-1, keepdims=True) * v
    o = o.reshape(B, T, D_MODEL).astype(h.dtype)
    return (o * g) @ w_o, S, h[:, -1]

def _trunk(x, hg_S0, rw_S0, rw_shift0, past_kv, W):
    sm = jax.nn.softmax(W['hg_lb_raw'].astype(jnp.float32), axis=0)
    lb_all = jnp.cumsum(sm, axis=0) - sm[0]
    hg_out, k_out, v_out, rw_out, sh_out = [], [], [], [], []
    for i in range(DEPTH):
        kind, j = i % N_MIXERS, i // N_MIXERS
        h = rms_norm(x, W['norm_mix'][i])
        if kind == 0:
            mixed, S = hgrn2_mixer(h, hg_S0[j], W['hg_w_in'][j], lb_all[i],
                                   W['hg_norm'][j], W['hg_w_out'][j])
            hg_out.append(S.astype(x.dtype))
        elif kind == 1:
            if past_kv is None:
                pk = pv = None
            else:
                cache_k, cache_v, page_table = past_kv
                nb = page_table.shape[0]
                pk = cache_k[j, page_table].reshape(nb, -1, AT_HEADS, 2, AT_HD)
                pv = cache_v[j, page_table].reshape(nb, -1, AT_HEADS, 2 * AT_HD)
            mixed, k_rows, v_rows = diff_attn_mixer(h, pk, pv, W['at_w_in'][j], W['at_lam'][j],
                                                    W['at_subln'][j], W['at_w_out'][j], i)
            k_out.append(k_rows)
            v_out.append(v_rows)
        else:
            mixed, S, last = rwkv7_mixer(
                h, rw_shift0[j], rw_S0[j], W['rw_mix'][j], W['rw_w_rkv'][j],
                W['rw_w0'][j], W['rw_w1'][j], W['rw_w2'][j],
                W['rw_a0'][j], W['rw_a1'][j], W['rw_a2'][j],
                W['rw_g1'][j], W['rw_g2'][j], W['rw_k_k'][j], W['rw_k_a'][j],
                W['rw_r_k'][j], W['rw_ln_w'][j], W['rw_ln_b'][j], W['rw_w_o'][j])
            rw_out.append(S.astype(x.dtype))
            sh_out.append(last)
        x = x + mixed
        x = x + swiglu(rms_norm(x, W['norm_ffn'][i]), W['ffn_w_in'][i], W['ffn_w_out'][i])
    y = rms_norm(x, W['final_norm'])
    return y, jnp.stack(hg_out), jnp.stack(k_out), jnp.stack(v_out), jnp.stack(rw_out), jnp.stack(sh_out)

def setup_inputs(seed: int = 0) -> dict:
    key = jax.random.key(seed)
    keys = iter(jax.random.split(key, 64))

    def nrm(shape, scale):
        return scale * jax.random.normal(next(keys), shape, jnp.float32)

    def unif(shape, lo, hi):
        return jax.random.uniform(next(keys), shape, jnp.float32, lo, hi)

    D = D_MODEL
    n_pages = PAST_LEN // PAGE_SIZE
    n_used = DEC_BATCH * n_pages
    n_pool = n_used + (n_used + 3) // 4
    perm = jax.random.permutation(next(keys), n_pool)
    page_table = perm[:n_used].reshape(DEC_BATCH, n_pages).astype(jnp.int32)
    return {
        'x_prompt': nrm((BATCH, SEQ, D), 1.0),
        'x_sample': nrm((DEC_BATCH, DEC_SEQ, D), 1.0),
        'cache_k': nrm((N_AT_LAYERS, n_pool, PAGE_SIZE, AT_HEADS, 2 * AT_HD), 1.0),
        'cache_v': nrm((N_AT_LAYERS, n_pool, PAGE_SIZE, AT_HEADS, 2 * AT_HD), 1.0),
        'page_table': page_table,
        'state_hgrn': nrm((N_HG_LAYERS, DEC_BATCH, HG_HEADS, HG_DK, HG_DV), 0.5),
        'state_rwkv': nrm((N_RW_LAYERS, DEC_BATCH, RW_HEADS, RW_HEAD, RW_HEAD), 0.1),
        'state_shift': nrm((N_RW_LAYERS, DEC_BATCH, D), 1.0),
        'norm_mix': 1.0 + nrm((DEPTH, D), 0.02),
        'norm_ffn': 1.0 + nrm((DEPTH, D), 0.02),
        'final_norm': 1.0 + nrm((D,), 0.02),
        'ffn_w_in': nrm((DEPTH, D, 2 * D_FF), D ** -0.5),
        'ffn_w_out': nrm((DEPTH, D_FF, D), D_FF ** -0.5),
        'hg_w_in': nrm((N_HG_LAYERS, D, 2 * HG_FDIM + 2 * D), D ** -0.5),
        'hg_lb_raw': nrm((DEPTH, HG_FDIM), 1.0),
        'hg_norm': 1.0 + nrm((N_HG_LAYERS, D), 0.02),
        'hg_w_out': nrm((N_HG_LAYERS, D, D), D ** -0.5),
        'at_w_in': nrm((N_AT_LAYERS, D, 3 * D), D ** -0.5),
        'at_lam': nrm((N_AT_LAYERS, 4, AT_HD), 0.1),
        'at_subln': 1.0 + nrm((N_AT_LAYERS, 2 * AT_HD), 0.02),
        'at_w_out': nrm((N_AT_LAYERS, D, D), D ** -0.5),
        'rw_mix': unif((N_RW_LAYERS, 6, D), 0.0, 1.0),
        'rw_w_rkv': nrm((N_RW_LAYERS, 3, D, D), D ** -0.5),
        'rw_w0': unif((N_RW_LAYERS, D), -6.5, -0.5),
        'rw_w1': nrm((N_RW_LAYERS, D, RW_DECAY_LORA), D ** -0.5),
        'rw_w2': nrm((N_RW_LAYERS, RW_DECAY_LORA, D), 0.1 * RW_DECAY_LORA ** -0.5),
        'rw_a0': nrm((N_RW_LAYERS, D), 0.1),
        'rw_a1': nrm((N_RW_LAYERS, D, RW_AAA_LORA), D ** -0.5),
        'rw_a2': nrm((N_RW_LAYERS, RW_AAA_LORA, D), 0.1 * RW_AAA_LORA ** -0.5),
        'rw_g1': nrm((N_RW_LAYERS, D, RW_GATE_LORA), D ** -0.5),
        'rw_g2': nrm((N_RW_LAYERS, RW_GATE_LORA, D), RW_GATE_LORA ** -0.5),
        'rw_k_k': unif((N_RW_LAYERS, D), 0.7, 1.0),
        'rw_k_a': unif((N_RW_LAYERS, D), 0.8, 1.2),
        'rw_r_k': nrm((N_RW_LAYERS, RW_HEADS, RW_HEAD), 0.1),
        'rw_ln_w': 1.0 + nrm((N_RW_LAYERS, D), 0.02),
        'rw_ln_b': nrm((N_RW_LAYERS, D), 0.01),
        'rw_w_o': nrm((N_RW_LAYERS, D, D), D ** -0.5),
    }

def reference(x_prompt, x_sample, cache_k, cache_v, page_table, state_hgrn, state_rwkv, state_shift,
              norm_mix, norm_ffn, final_norm, ffn_w_in, ffn_w_out,
              hg_w_in, hg_lb_raw, hg_norm, hg_w_out,
              at_w_in, at_lam, at_subln, at_w_out,
              rw_mix, rw_w_rkv, rw_w0, rw_w1, rw_w2, rw_a0, rw_a1, rw_a2, rw_g1, rw_g2,
              rw_k_k, rw_k_a, rw_r_k, rw_ln_w, rw_ln_b, rw_w_o):
    W = dict(norm_mix=norm_mix, norm_ffn=norm_ffn, final_norm=final_norm,
             ffn_w_in=ffn_w_in, ffn_w_out=ffn_w_out,
             hg_w_in=hg_w_in, hg_lb_raw=hg_lb_raw, hg_norm=hg_norm, hg_w_out=hg_w_out,
             at_w_in=at_w_in, at_lam=at_lam, at_subln=at_subln, at_w_out=at_w_out,
             rw_mix=rw_mix, rw_w_rkv=rw_w_rkv, rw_w0=rw_w0, rw_w1=rw_w1, rw_w2=rw_w2,
             rw_a0=rw_a0, rw_a1=rw_a1, rw_a2=rw_a2, rw_g1=rw_g1, rw_g2=rw_g2,
             rw_k_k=rw_k_k, rw_k_a=rw_k_a, rw_r_k=rw_r_k, rw_ln_w=rw_ln_w, rw_ln_b=rw_ln_b,
             rw_w_o=rw_w_o)
    B = x_prompt.shape[0]
    dt = x_prompt.dtype
    hg0 = jnp.zeros((N_HG_LAYERS, B, HG_HEADS, HG_DK, HG_DV), dt)
    rw0 = jnp.zeros((N_RW_LAYERS, B, RW_HEADS, RW_HEAD, RW_HEAD), dt)
    sh0 = jnp.zeros((N_RW_LAYERS, B, D_MODEL), dt)
    y_prompt, hg_p, k_p, v_p, rw_p, sh_p = _trunk(x_prompt, hg0, rw0, sh0, None, W)
    y_sample, hg_s, k_s, v_s, rw_s, sh_s = _trunk(
        x_sample, state_hgrn, state_rwkv, state_shift, (cache_k, cache_v, page_table), W)
    return (y_prompt, y_sample, hg_p, hg_s, k_p, v_p, k_s, v_s, rw_p, sh_p, rw_s, sh_s)


_drawn_inputs = setup_inputs


def setup_inputs(seed=0):
    import zlib

    import numpy as np

    out = dict(_drawn_inputs(seed))
    spreads = {}
    factors = {'final_norm': 2.907,
     'at_subln': 4.811,
     'rw_w1': 8.0,
     'rw_w2': 8.0,
     'rw_ln_w': 8.0,
     'rw_ln_b': 8.0}
    for name, (base, spread) in spreads.items():
        noise = np.random.default_rng([zlib.crc32(name.encode()), seed]).standard_normal(out[name].shape)
        drawn = base * np.exp(spread * noise) if base else spread * noise
        out[name] = jnp.asarray(drawn.astype(out[name].dtype))
    for name, factor in factors.items():
        out[name] = (out[name] * factor).astype(out[name].dtype)
    return out
```

```python
import math
from contextlib import ExitStack

import numpy as np

import concourse.bass as bass
from concourse import mybir

F32 = mybir.dt.float32
I32 = mybir.dt.int32
ALU = mybir.AluOpType
ACT = mybir.ActivationFunctionType
AX = mybir.AxisListType

D = 1024
P = 128
KC = D // P
NP_TOK = 512
NB, TB = 8, 4
NS_TOK = NB * TB
NT = NP_TOK + NS_TOK
HALF = NT // 2
DEPTH = 4
DFF = 2816
FC = DFF // P
FU = FC // 2
SLOTS = 4
SLOT = FU * P
HEADS = 8
CH = 128
NCH = NP_TOK // CH
LEVELS = 8
RMS_EPS = 1e-6
SUBLN_EPS = 1e-5
GN_EPS = 64e-5
F_MIN = 1e-30
HD = 64
C2 = 64
N2 = NP_TOK // C2
PAST = 256
PAGES = 2
NPOOL = 20
NEG = -1e30
LAYER_AT, LAYER_RW = 1, 2
LAM_INIT = 0.8 - 0.6 * math.exp(-0.3 * LAYER_AT)

V_MIX, V_FFN, V_FIN, V_HG, V_RWMIX = 0, 4, 8, 9, 11
V_W0, V_A0, V_KK, V_KA, V_RK, V_LNW, V_LNB, V_LB, V_SHIFT = 17, 18, 19, 20, 21, 22, 23, 24, 28
NV = 36

CONSTS = [("ident", P), ("ones", P), ("blocks", P), ("slopes", HEADS), ("bmask", NB),
          ("reset", NT), ("strict", C2), ("incl", C2), ("bs", PAST + NS_TOK), ("sel", NS_TOK),
          ("dist", NP_TOK), ("lvl64", 6 * 2 * C2), ("low", C2), ("eye64", C2), ("masks32", 5 * NS_TOK)]
CO = {}
_o = 0
for _n, _w in CONSTS:
    CO[_n] = (_o, _w)
    _o += _w
NCONST = _o


def constants():
    c = np.zeros((P, NCONST), np.float32)

    def put(name, a):
        o, w = CO[name]
        a = np.asarray(a, np.float32).reshape(-1, w)
        c[:a.shape[0], o:o + w] = a

    i = np.arange(P)
    put("ident", np.eye(P))
    put("ones", np.ones((P, P)))
    put("blocks", (i[:, None] // HD == i[None] // HD))
    put("slopes", np.tile(np.exp2(-8.0 * np.arange(1, HEADS + 1) / HEADS), (P, 1)))
    t = np.arange(NS_TOK)
    put("bmask", t[:, None] // TB == np.arange(NB)[None])
    r = np.ones(NT)
    r[:NP_TOK:C2] = 0
    r[NP_TOK::TB] = 0
    put("reset", np.tile(r, (P, 1)))
    s, u = np.arange(P)[:, None] % C2, np.arange(C2)[None]
    put("strict", s < u)
    put("incl", s <= u)
    row, key = np.arange(64)[:, None] % NS_TOK, np.arange(PAST + NS_TOK)[None]
    b, tt, new = row // TB, row % TB, key - PAST
    past = -(PAST + tt - key).astype(np.float64)
    fresh = np.where((new // TB == b) & (new % TB <= tt), -(tt - new % TB).astype(np.float64), NEG)
    put("bs", np.where(key < PAST, past, fresh))
    put("sel", (np.arange(64)[:, None] % NS_TOK == t[None]))
    j = np.arange(NP_TOK)[None] - (NP_TOK - P)
    q = np.arange(P)[:, None]
    put("dist", np.where(j <= q, -(q - j).astype(np.float64), NEG))
    lv = np.zeros((P, 6, 2, C2))
    for n in range(6):
        off = (s >> (n + 1) == u >> (n + 1)) & (s >> n != u >> n)
        lv[:, n, 0] = off & (s > u)
        lv[:, n, 1] = off & (s < u)
    put("lvl64", lv.reshape(P, -1))
    put("low", s > u)
    put("eye64", s == u)
    sb_, sa = t[:, None], t[None]
    same = sb_ // TB == sa // TB
    up, low, inc = same & (sb_ < sa), same & (sb_ > sa), same & (sb_ <= sa)
    put("masks32", np.stack([up, low, up, inc, inc], 1).reshape(NS_TOK, -1))
    m = np.zeros((P, LEVELS, P), np.int32)
    a, z = i[:, None], i[None]
    m[:, 0] = a == z
    for n in range(1, LEVELS):
        m[:, n] = (a >> n == z >> n) & (a >> (n - 1) != z >> (n - 1)) & (a < z)
    return c, m.reshape(P, -1)


CREDITS = {"hg_x": 4, "ff_glu": 2, "ff_x": 2}
CREDITS.update({n: 1 for n in (
    "hg_ev_v", "hg_ev_g", "hg_state", "hg_raw_used", "hg_vt_mm", "hg_out", "hg_st_free",
    "at_x", "at_st_mm", "at_ev_v", "at_scored", "at_o_ev", "at_kv_free", "at_ob", "rw_x", "rw_st", "rw_st_free", "rw_ob")})


class Semaphores:

    def __init__(self, nc, ctx):
        self.nc, self.ctx, self.known = nc, ctx, {}

    def __call__(self, name):
        if name not in self.known:
            self.known[name] = self.ctx.enter_context(self.nc.semaphore(name))
        return self.known[name]


class Arena:

    def __init__(self, tensor, size):
        self.tensor, self.size, self.at = tensor, size, 0

    def take(self, n):
        a = self.tensor[:, self.at:self.at + n]
        self.at += n
        assert self.at <= self.size, (self.at, self.size)
        return a


def unit_bases(depth):
    base, at = {}, 0
    for layer in range(depth):
        base[layer, "mix"] = at
        at += 4 * HEADS
        if layer % 3 == 0:
            base[layer, "out"] = at
            at += KC
        base[layer, "up"] = at
        at += 2 * FC
        base[layer, "down"] = at
        at += 2 * KC
    return base


def build(nc, T, depth=DEPTH):
    UB = unit_bases(depth)
    with ExitStack() as ctx:
        def sb(name, shape, dt=F32):
            return ctx.enter_context(nc.sbuf_tensor(name, shape, dt))

        S = Semaphores(nc, ctx)
        X = sb("x", [P, KC * NT])
        H = sb("h", [P, KC * NT])
        O = sb("o", [P, KC * NT])
        ring = sb("ring", [P, SLOTS * SLOT])
        rstd = sb("rstd", [P, NT])
        vec = sb("vec", [P, NV * KC])
        lbs = sb("lbs", [P, 4 * KC])
        lbt = sb("lbt", [P, 6 * KC])
        consts = sb("consts", [P, NCONST])
        subln = sb("subln", [P, 1])
        scratch = sb("scratch", [P, 4])
        hg_mask_t = sb("hg_mask", [P, LEVELS * P], I32)
        hg_mask = hg_mask_t[:, :]
        ARENA = 28560
        arena_t = sb("arena", [P, ARENA])
        PS = ctx.enter_context(nc.psum_tensor("ps", [P, 8, 512], F32))

        x3 = X[:, :].rearrange("p (c t) -> p c t", c=KC)
        h3 = H[:, :].rearrange("p (c t) -> p c t", c=KC)
        o3 = O[:, :].rearrange("p (c t) -> p c t", c=KC)
        vec3 = vec[:, :].rearrange("p (v c) -> p v c", v=NV)

        def const(name, rows=P):
            o, w = CO[name]
            return consts[0:rows, o:o + w]

        def slot(k, c):
            return ring[:, k * SLOT + c * P:k * SLOT + (c + 1) * P]

        def acc(k):
            return PS[:, 2 * k:2 * k + 2, 0:HALF]

        def halves(ap):
            return ap.rearrange("p (a t) -> p a t", a=2)

        NCONST_LOADS = 7
        lamv = sb("lamv", [P, 4 * HD])
        pages = sb("pages", [1, NB * PAGES], I32)
        cell = sb("cell", [P, 64])

        ar = Arena(arena_t, ARENA)
        ff_act = ar.take(FC * NT)
        ff_gate = [ar.take(NT) for _ in range(2)]

        ar = Arena(arena_t, ARENA)
        hg_sgp, hg_sgn, hg_qs, hg_qr, hg_v, hg_gs = (ar.take(NT) for _ in range(6))
        hg_f, hg_q, hg_qp, hg_ks = (ar.take(NT) for _ in range(4))
        hg_d = ar.take(NT)
        hg_at, hg_ats = ar.take(NP_TOK), ar.take(NS_TOK)
        hg_vt, hg_vts = ar.take(NP_TOK), ar.take(P)
        hg_kt, hg_kts = ar.take(NP_TOK), ar.take(P)
        hg_vx = ar.take(NB * P)
        hg_s = ar.take(NCH * P)
        hg_s0 = ar.take(NB * P)

        ar = Arena(arena_t, ARENA)
        at_q, at_k, at_v = (ar.take(NT) for _ in range(3))
        at_vt, at_vts = ar.take(NP_TOK), ar.take(P)
        at_kc, at_vc = ar.take(NB * PAGES * P), ar.take(NB * PAGES * P)
        at_sb = [[ar.take(NP_TOK) for _ in range(2)] for _ in range(2)]
        at_p = [[ar.take(NP_TOK) for _ in range(2)] for _ in range(2)]
        at_diag = [[ar.take(P) for _ in range(2)] for _ in range(2)]
        at_at = ar.take(NP_TOK)
        at_o, at_sq, at_rs, at_ob = (ar.take(NT) for _ in range(4))
        at_st, at_stn = ar.take(PAGES * 64), ar.take(64)
        at_ss, at_sp = ar.take(PAST + NS_TOK), ar.take(PAST + NS_TOK)
        at_selc = ar.take(NS_TOK)
        at_att, at_atn = ar.take(PAGES * NS_TOK), ar.take(NS_TOK)
        c_nm, c_ls, c_rl = ([cell[:, o + 2 * n:o + 2 * n + 2] for n in range(2)] for o in (20, 24, 28))
        c_snm, c_sls, c_srl, c_sco = cell[:, 6:7], cell[:, 7:8], cell[:, 8:9], cell[:, 9:10]
        c_slope, c_gain, c_sign, c_nlam = cell[:, 10:11], cell[:, 11:12], cell[:, 12:13], cell[:, 13:14]
        c_lam, c_sub, c_gn = cell[:, 14:18], cell[:, 18:19], cell[:, 19:20]

        ar = Arena(arena_t, ARENA)
        rw_xk, rw_xv = ar.take(KC * NT), ar.take(KC * NT)
        rw_hw, rw_ha, rw_hg = (ar.take(NT) for _ in range(3))
        rw_ls = ar.take(3 * P)
        rw_cur = ar.take(NV)
        rw_sh = ar.take(KC * 9)
        rw_r, rw_k, rw_v, rw_sg, rw_a, rw_g = (ar.take(NT) for _ in range(6))
        rw_bc, rw_p, rw_pi, rw_pp, rw_kn, rw_rn, rw_k2, rw_be = (O[:, n * NT:(n + 1) * NT] for n in range(8))
        rw_o, rw_oc = ar.take(NT), ar.take(NT)
        mats_at = ar.at
        MW = N2 * C2
        rw_mt, rw_m, rw_zkt, rw_rbt, rw_rkt, rw_x, rw_xt, rw_ml, rw_y, rw_hv, rw_wt = (ar.take(MW) for _ in range(11))
        rw_vtm, rw_ztm, rw_kptm, rw_bptm, rw_nu, rw_tmp = (ar.take(MW) for _ in range(6))
        rw_ms = ar.take(5 * 2 * NS_TOK)
        rw_xs, rw_xts, rw_mls, rw_ys, rw_tmps = (ar.take(2 * NS_TOK) for _ in range(5))
        rw_tms = ar.take(4 * P)
        rw_hvs, rw_wts, rw_ufm, rw_nutm = ar.take(P), ar.take(NS_TOK), ar.take(2 * NS_TOK), ar.take(P)
        rw_vxs, rw_nux = ar.take(NB * P), ar.take(NB * P)
        rw_st0 = ar.take(NB * HD)
        rw_st = ar.take((N2 + 1) * HD)
        rw_lw = arena_t[:, mats_at:mats_at + KC * 256]
        KAPPA = math.exp(-0.5)

        block = ctx.enter_context(nc.Block())

        norms = []
        for layer in range(depth):
            norms += [f"n{layer}m"] + [f"n{layer}o"] * (layer % 3 == 0) + [f"n{layer}f"]
        norms += ["nfin"]

        def norm_name(layer, which):
            return f"n{layer}{which}"

        def nth(name):
            return norms.index(name)

        @block.sync
        def _(sp):
            sp.dma_start(consts[:, :], T["consts"]).then_inc(S("consts_in"), 16)
            sp.dma_start(vec[:, :], T["vec"]).then_inc(S("consts_in"), 16)
            sp.dma_start(subln[:, :], T["subln"]).then_inc(S("consts_in"), 16)
            sp.dma_start(X[:, :], T["x"]).then_inc(S("consts_in"), 16)
            sp.dma_start(lamv[:, :], T["lam"]).then_inc(S("consts_in"), 16)
            sp.dma_start(pages[:, :], T["pages"]).then_inc(S("consts_in"), 16)

            def units(src, width, ubase, groups, first):
                if first:
                    for k in range(SLOTS):
                        sp.dma_start(ring[:, k * SLOT:k * SLOT + width],
                                     src[k]).then_inc(S(f"slot_in{k}"), 16)
                with sp.Fori(1 if first else 0, groups) as i:
                    for k in range(SLOTS):
                        sp.wait_ge(S("unit_done"), i * 4 + (ubase + k - 3))
                        sp.dma_start(ring[:, k * SLOT:k * SLOT + width],
                                     src[bass.ds(i * 4 + k, 1), :, :].rearrange("a p n -> (a p) n"))\
                          .then_inc(S(f"slot_in{k}"), 16)

            for layer in range(depth):
                kind = layer % 3
                units(T[f"w_mix{layer}"], D, UB[layer, "mix"], HEADS, layer == 0)
                if kind == 0:
                    units(T[f"w_hgout{layer}"], D, UB[layer, "out"], KC // 4, False)
                units(T[f"w_up{layer}"], D, UB[layer, "up"], 2 * FC // 4, False)
                units(T[f"w_down{layer}"], SLOT, UB[layer, "down"], 2 * KC // 4, False)
            sp.wait_ge(S("norm_h"), KC * len(norms))
            sp.dma_start(T["y"], H[:, :]).then_inc(S("y_out"), 16)
            sp.wait_ge(S("y_out"), 16)

        @block.tensor
        def _(pe):
            def settle():
                pe.sem_inc(S("pe_settled"), 1)

            def unit(k, a, rhs, blocks=KC, start=True, stop=True):
                for c in range(blocks):
                    for hf in range(2):
                        mm = pe.matmul(PS[:, 2 * a + hf, 0:HALF], slot(k, c), rhs(c, hf),
                                       start=start and c == 0, stop=stop and c == blocks - 1)
                return mm

            def from_h(c, hf):
                return h3[:, c, hf * HALF:(hf + 1) * HALF]

            def loaded(k, i, ubase):
                pe.wait_ge(S(f"slot_in{k}"), i * 16 + 16 * (ubase // 4 + 1))

            def norm(name):
                for c in range(KC):
                    pe.wait_ge(S("norm_sq"), nth(name) * KC + c + 1)
                    for hf in range(2):
                        mm = pe.matmul(PS[:, hf, 0:HALF], const("ones"), from_h(c, hf),
                                       start=c == 0, stop=c == KC - 1)
                mm.then_inc(S("norm_ssq"), 1)

            def feed_forward(layer):
                n, base = norm_name(layer, "f"), UB[layer, "up"]
                norm(n)
                pe.wait_ge(S("norm_h"), KC * (nth(n) + 1))
                with pe.Fori(0, FC // 2) as i:
                    for par in range(2):
                        for g in range(2):
                            k = 2 * par + g
                            if g == 0:
                                pe.wait_ge(S("ff_glu"), i * 2 + (par + FC * layer) + 1)
                            loaded(k, i, base)
                            unit(k, k, from_h).then_inc(S("unit_done"), 1)
                base = UB[layer, "down"]
                pe.wait_ge(S("ff_glu"), FC * (layer + 1) + 1 + 1)
                with pe.Fori(0, KC // 2) as i:
                    for par in range(2):
                        for g in range(2):
                            k = 2 * par + g
                            if g == 0:
                                pe.wait_ge(S("ff_x"), i * 2 + (par + KC * layer) + 1)
                            loaded(k, i, base)

                            def rhs(c, hf, g=g):
                                o = (g * FU + c) * NT + hf * HALF
                                return ff_act[:, o:o + HALF]
                            unit(k, par, rhs, FU, start=g == 0, stop=g == 1).then_inc(S("unit_done"), 1)

            def hgrn(layer):
                L = "hg_"
                j = layer // 3
                base = UB[layer, "mix"] - 4 * HEADS * j
                norm(norm_name(layer, "m"))
                pe.wait_ge(S("norm_h"), KC * (nth(norm_name(layer, "m")) + 1))
                before = ("ev_v", "ev_g", "ev_f", "ev_q")

                def project(h, first, last):
                    for n in range(first, last):
                        k, c = n // KC, n % KC
                        if c == 0:
                            pe.wait_ge(S(L + before[k]), h + 1)
                            loaded(k, h, base)
                        for hf in range(2):
                            mm = pe.matmul(PS[:, 2 * (k % 2) + hf, 0:HALF], slot(k, c), from_h(c, hf),
                                           start=c == 0, stop=c == KC - 1)
                        if c == KC - 1:
                            mm.then_inc(S("unit_done"), 1)

                def mix(h, more):
                    done = [0]

                    def ahead(n):
                        if more:
                            project(h + 1, done[0], done[0] + n)
                            done[0] += n

                    ahead(3)
                    pe.wait_ge(S(L + "ev_v"), h + 1 + 1)
                    pe.wait_ge(S(L + "state"), h + 1)
                    for c in range(NCH):
                        pe.transpose(PS[:, 6, c * P:(c + 1) * P], hg_v[:, c * P:(c + 1) * P], const("ident"))
                    pe.transpose(PS[0:NS_TOK, 7, 0:P], hg_v[:, NP_TOK:NT], const("ident")).then_inc(S(L + "vt_mm"), 1)
                    ahead(3)
                    pe.wait_ge(S(L + "vt_ev"), h + 1)
                    for n in range(LEVELS):
                        if n:
                            ahead(2)
                        pe.wait_ge(S(L + "lvl"), h * (LEVELS + 1) + n + 1)
                        q = hg_q if n == 0 else hg_qp
                        for c in range(NCH):
                            mm = pe.matmul(PS[:, 4 + n % 2, c * P:(c + 1) * P], hg_ks[:, c * P:(c + 1) * P],
                                           q[:, c * P:(c + 1) * P], start=True, stop=True)
                        if n <= 2:
                            mm = pe.matmul(PS[0:NS_TOK, 7 - n % 2, 0:NS_TOK], hg_ks[:, NP_TOK:NT],
                                           q[:, NP_TOK:NT], start=True, stop=True)
                        mm.then_inc(S(L + "lvl_mm"), 1)
                    ahead(2)
                    pe.wait_ge(S(L + "lvl"), (h + 1) * (LEVELS + 1))
                    for c in range(NCH):
                        pe.transpose(PS[:, 6, c * P:(c + 1) * P], hg_ks[:, c * P:(c + 1) * P], const("ident"))
                    pe.transpose(PS[0:NS_TOK, 7, 0:P], hg_ks[:, NP_TOK:NT], const("ident")).then_inc(S(L + "kt_mm"), 1)
                    ahead(1)
                    pe.wait_ge(S(L + "kt_ev"), h + 1)
                    pe.wait_ge(S(L + "at"), h + 1)
                    for c in range(NCH):
                        mm = pe.matmul(PS[:, 5, c * P:(c + 1) * P], hg_kt[:, c * P:(c + 1) * P],
                                       hg_vt[:, c * P:(c + 1) * P], start=True, stop=True)
                    mm.then_inc(S(L + "kv_mm"), 1)
                    pe.wait_ge(S(L + "vx"), h + 1)
                    for g in range(2):
                        mm = pe.matmul(PS[:, 6 + g, :], hg_kts[0:NS_TOK, :], hg_vx[0:NS_TOK, g * 512:(g + 1) * 512],
                                       start=True, stop=True)
                    mm.then_inc(S(L + "kvs_mm"), 1)
                    ahead(3)
                    pe.wait_ge(S(L + "s"), h + 1)
                    for c in range(NCH):
                        cs = slice(c * P, (c + 1) * P)
                        pe.matmul(PS[:, 4, cs], hg_vt[:, cs], hg_at[:, cs], start=True, stop=c == 0)
                        if c:
                            pe.matmul(PS[:, 4, cs], hg_s[:, (c - 1) * P:c * P], hg_qp[:, cs], start=False, stop=True)
                    pe.wait_ge(S(L + "s0_in"), h * 16 + 16)
                    pe.matmul(PS[:, 5, 0:NS_TOK], hg_vts[0:NS_TOK, :], hg_ats[0:NS_TOK, :], start=True, stop=False,
                              skip_group_check=True)
                    for b in range(NB):
                        bs = slice(b * TB, (b + 1) * TB)
                        mm = pe.matmul(PS[:, 5, bs], hg_s0[:, b * P:(b + 1) * P], hg_qp[:, NP_TOK + b * TB:NP_TOK + (b + 1) * TB],
                                       start=False, stop=b == NB - 1, skip_group_check=True)
                    mm.then_inc(S(L + "o_mm"), 1)
                    ahead(6)

                project(j * HEADS, 0, 4 * KC)
                with pe.Fori(j * HEADS, (j + 1) * HEADS - 1) as h:
                    mix(h, True)
                mix((j + 1) * HEADS - 1, False)
                norm(norm_name(layer, "o"))
                pe.wait_ge(S("norm_h"), KC * (nth(norm_name(layer, "o")) + 1))
                base = UB[layer, "out"]
                with pe.Fori(0, KC // 4) as i:
                    for k in range(4):
                        pe.wait_ge(S(L + "x"), i * 4 + (k + KC * j) + 1)
                        loaded(k, i, base)
                        unit(k, k, from_h).then_inc(S("unit_done"), 1)

            def out_rows(L, h, base, rhs, d, accs):
                for m in range(KC):
                    if m >= len(accs):
                        pe.wait_ge(S(L + "x"), h * KC + (m - len(accs) + 1) + 1)
                    if m == 0:
                        loaded(d % 4, h, base + d - d % 4)
                    for hf in range(2):
                        mm = pe.matmul(PS[:, 2 * accs[m % len(accs)] + hf, 0:HALF], slot(d % 4, m),
                                       rhs[:, hf * HALF:(hf + 1) * HALF], start=True, stop=True)
                    mm.then_inc(S(L + "out_mm") if m < KC - 1 else S("unit_done"), 1)

            def attention(layer):
                L = "at_"
                base = UB[layer, "mix"]
                norm(norm_name(layer, "m"))
                pe.wait_ge(S("norm_h"), KC * (nth(norm_name(layer, "m")) + 1))
                ident = const("ident")
                def project(h, first, last, d):
                    for n in range(first, last):
                        k, c = n // KC, n % KC
                        s = (d + k) % 4
                        if c == 0:
                            if k == 0:
                                pe.wait_ge(S(L + "ev_v"), h + 1)
                            if k == 2:
                                pe.wait_ge(S(L + "ev_q"), h + 1)
                            loaded(s, h, base + d + k - s)
                        for hf in range(2):
                            mm = pe.matmul(PS[:, 2 * (k % 2) + hf, 0:HALF], slot(s, c), from_h(c, hf),
                                           start=c == 0, stop=c == KC - 1)
                        if c == KC - 1:
                            mm.then_inc(S("unit_done"), 1)

                def mix(h, more):
                    done = [0]

                    def ahead(n):
                        if more:
                            project(h + 1, done[0], done[0] + n, -1)
                            done[0] += n

                    def scores(qb):
                        keys = (qb + 1) * P
                        pe.wait_ge(S(L + "scored"), h * NCH + qb + 1)
                        for c in range(2):
                            mm = pe.matmul(PS[:, 4 + c, 0:keys], at_q[c * HD:(c + 1) * HD, qb * P:keys],
                                           at_k[c * HD:(c + 1) * HD, 0:keys], start=True, stop=True)
                        mm.then_inc(S(L + "score_mm"), 1)

                    ahead(1)
                    pe.wait_ge(S(L + "x"), h * KC + 1)
                    pe.wait_ge(S(L + "ev_k"), h + 1)
                    scores(0)
                    pe.wait_ge(S(L + "ev_v"), h + 1 + 1)
                    for c in range(NCH):
                        pe.transpose(PS[:, 6, c * P:(c + 1) * P], at_v[:, c * P:(c + 1) * P], ident)
                    pe.transpose(PS[0:NS_TOK, 7, 0:P], at_v[:, NP_TOK:NT], ident).then_inc(S(L + "vt_mm"), 1)
                    for qb in range(NCH):
                        n = h * NCH + qb
                        if qb < NCH - 1:
                            scores(qb + 1)
                        ahead(2 if qb == 0 else 3)
                        pe.wait_ge(S(L + "probs"), n + 1)
                        pe.wait_ge(S(L + "diag"), n + 1)
                        pe.wait_ge(S(L + "vt_ev"), h + 1)
                        for kb in range(qb + 1):
                            for c in range(2):
                                mm = pe.matmul(PS[:, 6, kb * P:(kb + 1) * P], at_p[qb % 2][c][:, kb * P:(kb + 1) * P],
                                               at_diag[qb % 2][c], start=c == 0, stop=c == 1)
                        mm.then_inc(S(L + "at_mm"), 1)
                        ahead(1)
                        pe.wait_ge(S(L + "at_ev"), n + 1)
                        pe.wait_ge(S(L + "o_ev"), h * (NCH + 1) + qb + 1)
                        for kb in range(qb + 1):
                            mm = pe.matmul(PS[:, 7, 0:P], at_vt[:, kb * P:(kb + 1) * P], at_at[:, kb * P:(kb + 1) * P],
                                           start=kb == 0, stop=kb == qb)
                        mm.then_inc(S(L + "o_mm"), 1)
                    pe.wait_ge(S(L + "kc_in"), (h + 1) * (16 * NB * PAGES))
                    pe.wait_ge(S(L + "scored"), (h + 1) * NCH + 1)
                    for c in range(2):
                        rows = slice(c * HD, (c + 1) * HD)
                        for b in range(NB):
                            for pg in range(PAGES):
                                k0 = (b * PAGES + pg) * P
                                o = pg * NS_TOK + b * TB
                                pe.matmul(PS[:, 4 + c, o:o + TB], at_kc[rows, k0:k0 + P],
                                          at_q[rows, NP_TOK + b * TB:NP_TOK + (b + 1) * TB], start=True, stop=True)
                        mm = pe.matmul(PS[0:NS_TOK, 4 + c, 64:64 + NS_TOK], at_k[rows, NP_TOK:NT],
                                       at_q[rows, NP_TOK:NT], start=True, stop=True)
                    mm.then_inc(S(L + "st_mm"), 1)
                    pe.wait_ge(S(L + "st_ev"), h + 1)
                    settle()
                    for pg in range(PAGES):
                        pe.transpose(PS[0:64, 5, pg * P:(pg + 1) * P], at_st[:, pg * 64:(pg + 1) * 64], ident)
                    pe.transpose(PS[0:64, 5, PAST:PAST + NS_TOK], at_stn[0:NS_TOK, :], ident[0:NS_TOK, 0:NS_TOK])\
                        .then_inc(S(L + "ss_mm"), 1)
                    ahead(3)
                    pe.wait_ge(S(L + "sprobs"), h + 1)
                    pe.wait_ge(S(L + "selc"), h + 1)
                    for pg in range(PAGES):
                        pe.matmul(PS[:, 6, pg * NS_TOK:(pg + 1) * NS_TOK], at_sp[0:64, pg * P:(pg + 1) * P],
                                  at_selc[0:64, :], start=True, stop=True)
                    pe.matmul(PS[0:NS_TOK, 6, 64:64 + NS_TOK], at_sp[0:64, PAST:PAST + NS_TOK],
                              at_selc[0:64, :], start=True, stop=True).then_inc(S(L + "sat_mm"), 1)
                    ahead(1)
                    pe.wait_ge(S(L + "sat_ev"), h + 1)
                    pe.wait_ge(S(L + "vc_in"), (h + 1) * (16 * NB * PAGES))
                    pe.wait_ge(S(L + "o_ev"), h * (NCH + 1) + NCH + 1)
                    pe.matmul(PS[:, 7, 0:NS_TOK], at_vts[0:NS_TOK, :], at_atn[0:NS_TOK, :], start=True, stop=False,
                              skip_group_check=True)
                    for b in range(NB):
                        for pg in range(PAGES):
                            k0 = (b * PAGES + pg) * P
                            o = pg * NS_TOK + b * TB
                            mm = pe.matmul(PS[:, 7, b * TB:(b + 1) * TB], at_vc[:, k0:k0 + P], at_att[:, o:o + TB],
                                           start=False, stop=b == NB - 1 and pg == PAGES - 1, skip_group_check=True)
                    mm.then_inc(S(L + "o_mm"), 1)
                    ahead(2)
                    pe.wait_ge(S(L + "osq"), h + 1)
                    for hf in range(2):
                        mm = pe.matmul(PS[:, 4 + hf, 0:HALF], const("ones"), at_sq[:, hf * HALF:(hf + 1) * HALF],
                                       start=True, stop=True)
                    mm.then_inc(S(L + "ossq"), 1)
                    ahead(2)
                    pe.wait_ge(S(L + "ob"), h + 1 + 1)
                    out_rows(L, h, base, at_ob, 6 if more else 3, (1, 2, 3))

                project(0, 0, 3 * KC, 0)
                with pe.Fori(0, HEADS - 1) as h:
                    mix(h, True)
                mix(HEADS - 1, False)

            def rwkv(layer):
                L = "rw_"
                base = UB[layer, "mix"]
                norm(norm_name(layer, "m"))
                for n, (lo, w, buf) in enumerate(((0, 64, rw_xk), (64, 64, rw_xv), (128, 128, rw_xk))):
                    pe.wait_ge(S(L + "xm"), n + 1)
                    if n == 0:
                        pe.wait_ge(S(L + "lw_in"), 16)
                    for c in range(KC):
                        for hf in range(2):
                            mm = pe.matmul(PS[0:w, 2 * n + hf, 0:HALF], rw_lw[:, c * 256 + lo:c * 256 + lo + w],
                                           buf[:, c * NT + hf * HALF:c * NT + (hf + 1) * HALF],
                                           start=c == 0, stop=c == KC - 1)
                    mm.then_inc(S(L + "lora_mm"), 1)
                pe.wait_ge(S(L + "hidden"), 3)
                pe.wait_ge(S(L + "xm"), 6)
                ident = const("ident")
                heads = (slice(0, HD), slice(HD, P))

                def rhs_of(buf):
                    return lambda c, hf: buf[:, c * NT + hf * HALF:c * NT + (hf + 1) * HALF]

                with pe.Fori(0, HEADS) as h:
                    pe.wait_ge(S(L + "x"), h * KC + 1)
                    loaded(0, h, base)
                    unit(0, 0, rhs_of(H)).then_inc(S("unit_done"), 1)
                    loaded(1, h, base)
                    unit(1, 1, rhs_of(rw_xk)).then_inc(S("unit_done"), 1)
                    pe.wait_ge(S(L + "ev_r"), h + 1)
                    loaded(2, h, base)
                    unit(2, 0, rhs_of(rw_xv)).then_inc(S("unit_done"), 1)
                    for n, (rows, hid, a, before) in enumerate(((HD, rw_hw, 1, "ev_k"), (HD, rw_ha, 0, "ev_v"), (P, rw_hg, 1, "ev_w"))):
                        pe.wait_ge(S(L + before), h + 1)
                        pe.wait_ge(S(L + "ls_in"), h * 48 + 48)
                        pe.wait_ge(S(L + "lw_in"), 16)
                        for hf in range(2):
                            mm = pe.matmul(PS[:, 2 * a + hf, 0:HALF], rw_ls[0:rows, n * P:(n + 1) * P],
                                           hid[0:rows, hf * HALF:(hf + 1) * HALF], start=True, stop=True)
                        mm.then_inc(S(L + "lora2_mm"), 1)
                    pe.wait_ge(S(L + "kn_sq"), h + 1)
                    for hf in range(2):
                        mm = pe.matmul(PS[:, 4 + hf, 0:HALF], const("blocks"), rw_rn[:, hf * HALF:(hf + 1) * HALF],
                                       start=True, stop=True)
                    mm.then_inc(S(L + "kn_mm"), 1)
                    pe.wait_ge(S(L + "rk"), h + 1)
                    for hf in range(2):
                        mm = pe.matmul(PS[:, 6 + hf, 0:HALF], const("blocks"), rw_k[:, hf * HALF:(hf + 1) * HALF],
                                       start=True, stop=True)
                    mm.then_inc(S(L + "bonus_mm"), 1)
                    pe.wait_ge(S(L + "ops"), h + 1)
                    pe.wait_ge(S(L + "bonus"), h + 1)
                    settle()
                    for bank, src in enumerate((rw_v, rw_pp, rw_bc, rw_kn)):
                        for n in range(N2):
                            for hd in heads:
                                pe.matmul(PS[hd, 4 + bank, n * C2:(n + 1) * C2], src[hd, n * C2:(n + 1) * C2],
                                          ident[hd, hd], start=True, stop=True)
                        mm = pe.transpose(PS[0:NS_TOK, 0, bank * P:(bank + 1) * P], src[:, NP_TOK:NT], ident)
                    mm.then_inc(S(L + "tm_mm"), 1)
                    pe.wait_ge(S(L + "tm_ev"), h + 1)
                    settle()
                    pairs = ((rw_be, rw_pp), (rw_pp, rw_be), (rw_k2, rw_pp), (rw_be, rw_r), (rw_k2, rw_r))
                    for n_, (a, b) in enumerate(pairs):
                        bank = (4, 5, 6, 7, 0)[n_]
                        for n in range(N2):
                            cs = slice(n * C2, (n + 1) * C2)
                            for hd in heads:
                                pe.matmul(PS[hd, bank, cs], a[hd, cs], b[hd, cs], start=True, stop=True)
                        for i, hd in enumerate(heads):
                            o = n_ * NS_TOK
                            mm = pe.matmul(PS[0:NS_TOK, 1 + i, o:o + NS_TOK], a[hd, NP_TOK:NT], b[hd, NP_TOK:NT],
                                           start=True, stop=True)
                    mm.then_inc(S(L + "mat_mm"), 1)
                    for lv in range(1, 6):
                        pe.wait_ge(S(L + "inv"), h * 6 + lv)
                        settle()
                        for n in range(N2):
                            cs = slice(n * C2, (n + 1) * C2)
                            for hd in heads:
                                mm = pe.matmul(PS[hd, 4, cs], rw_ml[hd, cs], rw_x[hd, cs], start=True, stop=True)
                        if lv == 1:
                            for i in range(2):
                                ss = slice(i * NS_TOK, (i + 1) * NS_TOK)
                                mm = pe.matmul(PS[0:NS_TOK, 5, ss], rw_mls[0:NS_TOK, ss], rw_xs[0:NS_TOK, ss], start=True, stop=True)
                        mm.then_inc(S(L + "y_mm"), 1)
                        pe.wait_ge(S(L + "y_ev"), h * 5 + lv)
                        settle()
                        for n in range(N2):
                            cs = slice(n * C2, (n + 1) * C2)
                            for hd in heads:
                                pe.matmul(PS[hd, 6, cs], rw_xt[hd, cs], rw_y[hd, cs], start=True, stop=True)
                                mm = pe.matmul(PS[hd, 7, cs], rw_y[hd, cs], rw_xt[hd, cs], start=True, stop=True)
                        if lv == 1:
                            for i in range(2):
                                ss = slice(i * NS_TOK, (i + 1) * NS_TOK)
                                s2 = slice(128 + i * NS_TOK, 128 + (i + 1) * NS_TOK)
                                s3 = slice(256 + i * NS_TOK, 256 + (i + 1) * NS_TOK)
                                pe.matmul(PS[0:NS_TOK, 5, s2], rw_xts[0:NS_TOK, ss], rw_ys[0:NS_TOK, ss], start=True, stop=True)
                                mm = pe.matmul(PS[0:NS_TOK, 5, s3], rw_ys[0:NS_TOK, ss], rw_xts[0:NS_TOK, ss], start=True, stop=True)
                        mm.then_inc(S(L + "xy_mm"), 1)
                    pe.wait_ge(S(L + "inv"), h * 6 + 6)
                    settle()
                    for n in range(N2):
                        cs = slice(n * C2, (n + 1) * C2)
                        for hd in heads:
                            pe.matmul(PS[hd, 4, cs], rw_zkt[hd, cs], rw_vtm[hd, cs], start=True, stop=True)
                            pe.matmul(PS[hd, 5, cs], rw_ztm[hd, cs], rw_xt[hd, cs], start=True, stop=True)
                    for i, hd in enumerate(heads):
                        tm = slice(i * HD, (i + 1) * HD)
                        ss = slice(i * NS_TOK, (i + 1) * NS_TOK)
                        pe.matmul(PS[0:NS_TOK, 6, tm], rw_ms[0:NS_TOK, (4 + i) * NS_TOK:(5 + i) * NS_TOK],
                                  rw_tms[0:NS_TOK, tm], start=True, stop=True)
                        mm = pe.matmul(PS[hd, 7, 0:NS_TOK], rw_tms[0:NS_TOK, P + i * HD:P + (i + 1) * HD], rw_xts[0:NS_TOK, ss],
                                       start=True, stop=True)
                    mm.then_inc(S(L + "hw_mm"), 1)
                    pe.wait_ge(S(L + "hw_ev"), h + 1)
                    settle()
                    for n in range(N2):
                        cs = slice(n * C2, (n + 1) * C2)
                        pe.wait_ge(S(L + "st"), h * N2 + n + 1)
                        settle()
                        for hd in heads:
                            pe.matmul(PS[hd, 4 + n % 2, 0:HD], rw_xt[hd, cs], rw_hv[hd, cs], start=True, stop=False)
                            mm = pe.matmul(PS[hd, 4 + n % 2, 0:HD], rw_wt[hd, cs], rw_st[hd, n * HD:(n + 1) * HD],
                                           start=False, stop=True)
                        mm.then_inc(S(L + "u_mm"), 1)
                        pe.wait_ge(S(L + "nu"), h * N2 + n + 1)
                        settle()
                        for hd in heads:
                            pe.matmul(PS[hd, 6 + n % 2, 0:HD], rw_kptm[hd, cs], rw_vtm[hd, cs], start=True, stop=False)
                            mm = pe.matmul(PS[hd, 6 + n % 2, 0:HD], rw_bptm[hd, cs], rw_nu[hd, cs], start=False, stop=True)
                        mm.then_inc(S(L + "ds_mm"), 1)
                    for n in range(N2):
                        cs = slice(n * C2, (n + 1) * C2)
                        for hd in heads:
                            pe.matmul(PS[hd, 0, cs], rw_st[hd, n * HD:(n + 1) * HD], rw_r[hd, cs], start=True, stop=False)
                            pe.matmul(PS[hd, 0, cs], rw_vtm[hd, cs], rw_rkt[hd, cs], start=False, stop=False)
                            pe.matmul(PS[hd, 0, cs], rw_nu[hd, cs], rw_rbt[hd, cs], start=False, stop=True)
                    pe.wait_ge(S(L + "s0_in"), h * 16 + 16)
                    pe.wait_ge(S(L + "nu"), (h + 1) * N2)
                    settle()
                    for i, hd in enumerate(heads):
                        ss = slice(i * NS_TOK, (i + 1) * NS_TOK)
                        pe.matmul(PS[hd, 4, 0:NS_TOK], rw_hvs[0:NS_TOK, i * HD:(i + 1) * HD], rw_xts[0:NS_TOK, ss],
                                  start=True, stop=True)
                    for b in range(NB):
                        for hd in heads:
                            mm = pe.matmul(PS[hd, 5, b * TB:(b + 1) * TB], rw_st0[hd, b * HD:(b + 1) * HD],
                                           rw_wts[hd, b * TB:(b + 1) * TB], start=True, stop=True)
                    mm.then_inc(S(L + "us_mm"), 1)
                    pe.wait_ge(S(L + "us_ev"), h + 1)
                    settle()
                    for n in range(2):
                        mm = pe.matmul(PS[0:NS_TOK, 5, 0:P], rw_ufm[:, n * NS_TOK:(n + 1) * NS_TOK], ident, start=n == 0, stop=n == 1)
                    mm.then_inc(S(L + "ut_mm"), 1)
                    pe.wait_ge(S(L + "ut_ev"), h + 1)
                    for i, hd in enumerate(heads):
                        tm = slice(i * HD, (i + 1) * HD)
                        rk = slice((8 + i) * NS_TOK, (9 + i) * NS_TOK)
                        rb = slice((6 + i) * NS_TOK, (7 + i) * NS_TOK)
                        pe.matmul(PS[hd, 1, 0:NS_TOK], rw_tms[0:NS_TOK, tm], rw_ms[0:NS_TOK, rk], start=True, stop=False,
                                  skip_group_check=True)
                        pe.matmul(PS[hd, 1, 0:NS_TOK], rw_nutm[0:NS_TOK, tm], rw_ms[0:NS_TOK, rb], start=False, stop=True,
                                  skip_group_check=True)
                    for b in range(NB):
                        for hd in heads:
                            mm = pe.matmul(PS[hd, 2, b * TB:(b + 1) * TB], rw_st0[hd, b * HD:(b + 1) * HD],
                                           rw_r[hd, NP_TOK + b * TB:NP_TOK + (b + 1) * TB], start=True, stop=True)
                    mm.then_inc(S(L + "o_mm"), 1)
                    pe.wait_ge(S(L + "nux"), h + 1)
                    pe.wait_ge(S(L + "st"), (h + 1) * N2 + 1)
                    for i, hd in enumerate(heads):
                        vx = rw_vxs[0:NS_TOK, :].rearrange("p (b v) -> p b v", b=NB)[:, :, i * HD:(i + 1) * HD]
                        nx = rw_nux[0:NS_TOK, :].rearrange("p (b v) -> p b v", b=NB)[:, :, i * HD:(i + 1) * HD]
                        ps = PS[hd, 6, :].rearrange("p (b v) -> p b v", b=NB)
                        pe.matmul(ps, rw_tms[0:NS_TOK, 2 * P + i * HD:2 * P + (i + 1) * HD], vx, start=True, stop=False)
                        mm = pe.matmul(ps, rw_tms[0:NS_TOK, 3 * P + i * HD:3 * P + (i + 1) * HD], nx, start=False, stop=True)
                    mm.then_inc(S(L + "dss_mm"), 1)
                    pe.wait_ge(S(L + "o_sum"), h + 1)
                    for hf in range(2):
                        mm = pe.matmul(PS[:, 4 + hf, 0:HALF], const("blocks"), rw_o[:, hf * HALF:(hf + 1) * HALF],
                                       start=True, stop=True)
                    mm.then_inc(S(L + "mu_mm"), 1)
                    pe.wait_ge(S(L + "oc_sq"), h + 1)
                    for hf in range(2):
                        mm = pe.matmul(PS[:, 4 + hf, 0:HALF], const("blocks"), rw_o[:, hf * HALF:(hf + 1) * HALF],
                                       start=True, stop=True)
                    mm.then_inc(S(L + "var_mm"), 1)
                    pe.wait_ge(S(L + "ob"), h + 1 + 1)
                    pe.wait_ge(S(L + "state"), h + 1)
                    out_rows(L, h, base, rw_oc, 3, (0, 1, 2, 3))

            pe.wait_ge(S("consts_in"), 16 * NCONST_LOADS)
            for layer in range(depth):
                (hgrn, attention, rwkv)[layer % 3](layer)
                feed_forward(layer)
            norm("nfin")

        @block.scalar
        def _(act):
            act.dma_start(hg_mask, T["mask"]).then_inc(S("consts_in"), 16)

            def norm(name, src, ready, count):
                act.wait_ge(S(ready), count)
                for c in range(KC):
                    act.activation(h3[:, c, :], src[:, c, :], ACT.Square).then_inc(S("norm_sq"), 1)
                act.wait_ge(S("norm_ssq"), nth(name) + 1)
                act.activation(halves(rstd[:, :]), acc(0), ACT.Sqrt, scale=1.0 / D, bias=scratch[:, 0:1])\
                   .then_inc(S("norm_rms"), 1)

            def done(ubase, i, k):
                act.wait_ge(S("unit_done"), i * 4 + (ubase + k + 1))

            def feed_forward(layer, ready, count):
                norm(norm_name(layer, "f"), x3, ready, count)
                base = UB[layer, "up"]
                with act.Fori(0, FC // 2) as i:
                    for par in range(2):
                        act.wait_ge(S("ff_glu"), i * 2 + (par + FC * layer) + 1)
                        done(base, i, 2 * par)
                        act.activation(halves(ff_gate[par]), acc(2 * par), ACT.Silu).then_inc(S("ff_silu"), 1)

            def hgrn(layer, ready, count):
                L = "hg_"
                j = layer // 3
                base = UB[layer, "mix"] - 4 * HEADS * j
                norm(norm_name(layer, "m"), x3, ready, count)

                def raw(h, k):
                    done(base, h, k)
                    if k == 0:
                        act.wait_ge(S(L + "raw_used"), h + 1)
                        act.activation(halves(hg_sgp), acc(0), ACT.Sigmoid)
                        act.activation(halves(hg_sgn), acc(0), ACT.Sigmoid, scale=-1.0).then_inc(S(L + "ev_f"), 1)
                    if k == 1:
                        act.activation(halves(hg_qs), acc(1), ACT.Sigmoid)
                        act.activation(halves(hg_qr), acc(1), ACT.Copy).then_inc(S(L + "ev_q"), 1)
                    if k == 2:
                        act.wait_ge(S(L + "vt_mm"), h + 1)
                        act.activation(halves(hg_v), acc(0), ACT.Copy).then_inc(S(L + "ev_v"), 1)
                    if k == 3:
                        act.wait_ge(S(L + "out"), h + 1)
                        act.activation(halves(hg_gs), acc(1), ACT.Sigmoid).then_inc(S(L + "ev_g"), 1)

                def mix(h, more):
                    act.wait_ge(S(L + "vt_mm"), h + 1 + 1)
                    act.activation(hg_vt, PS[:, 6, :], ACT.Copy)
                    act.activation(hg_vts[0:NS_TOK, :], PS[0:NS_TOK, 7, 0:P], ACT.Copy).then_inc(S(L + "vt_ev"), 1)
                    if more:
                        raw(h + 1, 0)
                        raw(h + 1, 1)
                    act.wait_ge(S(L + "kt_mm"), h + 1)
                    act.activation(hg_kt, PS[:, 6, :], ACT.Copy)
                    act.activation(hg_kts[0:NS_TOK, :], PS[0:NS_TOK, 7, 0:P], ACT.Copy).then_inc(S(L + "kt_ev"), 1)
                    if more:
                        raw(h + 1, 2)
                        raw(h + 1, 3)

                for k in range(4):
                    raw(j * HEADS, k)
                with act.Fori(j * HEADS, (j + 1) * HEADS - 1) as h:
                    mix(h, True)
                mix((j + 1) * HEADS - 1, False)
                norm(norm_name(layer, "o"), o3, L + "out", HEADS * (j + 1) + 1)

            def attention(layer, ready, count):
                L = "at_"
                base = UB[layer, "mix"]
                act.wait_ge(S(L + "lam_sum"), 1)
                act.activation(c_lam[:, 2:4], c_lam[:, 0:2], ACT.Exp).then_inc(S(L + "lam_exp"), 1)
                norm(norm_name(layer, "m"), x3, ready, count)

                def raw(h, k, d):
                    if k == 0:
                        act.wait_ge(S(L + "kv_free"), h + 1)
                    act.wait_ge(S("unit_done"), h * 4 + (base + d + k + 1))
                    if k == 0:
                        act.activation(halves(at_q), acc(0), ACT.Copy, scale=HD ** -0.5).then_inc(S(L + "ev_q"), 1)
                    if k == 1:
                        act.activation(halves(at_k), acc(1), ACT.Copy).then_inc(S(L + "ev_k"), 1)
                    if k == 2:
                        act.activation(halves(at_v), acc(0), ACT.Copy).then_inc(S(L + "ev_v"), 1)

                def mix(h, more):
                    act.wait_ge(S(L + "vt_mm"), h + 1)
                    act.activation(at_vt, PS[:, 6, :], ACT.Copy)
                    act.activation(at_vts[0:NS_TOK, :], PS[0:NS_TOK, 7, 0:P], ACT.Copy).then_inc(S(L + "vt_ev"), 1)

                    def probs(qb):
                        keys = (qb + 1) * P
                        act.wait_ge(S(L + "maxed"), h * NCH + qb + 1)
                        for c in range(2):
                            last = act.activation(at_p[qb % 2][c][:, 0:keys], at_sb[qb % 2][c][:, 0:keys], ACT.Exp,
                                                  bias=c_nm[qb % 2][:, c:c + 1], accum_out=c_ls[qb % 2][:, c:c + 1])
                        last.then_inc(S(L + "probs"), 1)

                    probs(0)
                    for qb in range(NCH):
                        keys = (qb + 1) * P
                        if qb < NCH - 1:
                            probs(qb + 1)
                        act.wait_ge(S(L + "at_mm"), h * NCH + qb + 1)
                        act.activation(at_at[:, 0:keys], PS[:, 6, 0:keys], ACT.Copy).then_inc(S(L + "at_ev"), 1)
                    act.wait_ge(S(L + "st_mm"), h + 1 + 1)
                    for pg in range(PAGES):
                        act.activation(at_st[:, pg * 64:(pg + 1) * 64].rearrange("p (c t) -> p c t", c=2),
                                       PS[:, 4:6, pg * NS_TOK:(pg + 1) * NS_TOK], ACT.Copy)
                    act.activation(at_stn[0:NS_TOK, :].rearrange("p (c t) -> p c t", c=2),
                                   PS[0:NS_TOK, 4:6, 64:64 + NS_TOK], ACT.Copy).then_inc(S(L + "st_ev"), 1)
                    if more:
                        raw(h + 1, 0, -1)
                        raw(h + 1, 1, -1)
                    act.wait_ge(S(L + "smaxed"), h + 1)
                    act.activation(at_sp[0:64, :], at_ss[0:64, :], ACT.Exp, bias=c_snm[0:64, :],
                                   accum_out=c_sls[0:64, :]).then_inc(S(L + "sprobs"), 1)
                    act.wait_ge(S(L + "sat_mm"), h + 1)
                    act.activation(at_att, PS[:, 6, 0:64], ACT.Copy)
                    act.activation(at_atn[0:NS_TOK, :], PS[0:NS_TOK, 6, 64:96], ACT.Copy).then_inc(S(L + "sat_ev"), 1)
                    act.wait_ge(S(L + "o_ev"), (h + 1) * (NCH + 1) + 1)
                    act.activation(at_sq, at_o, ACT.Square).then_inc(S(L + "osq"), 1)
                    act.wait_ge(S(L + "ossq"), h + 1)
                    act.activation(halves(at_rs), acc(2), ACT.Sqrt, scale=1.0 / P, bias=c_sub).then_inc(S(L + "orms"), 1)
                    if more:
                        raw(h + 1, 2, -1)

                for k in range(3):
                    raw(0, k, 0)
                with act.Fori(0, HEADS - 1) as h:
                    mix(h, True)
                mix(HEADS - 1, False)

            def rwkv(layer, ready, count):
                L = "rw_"
                base = UB[layer, "mix"]
                norm(norm_name(layer, "m"), x3, ready, count)
                act.wait_ge(S(L + "lora_mm"), 1)
                act.activation(halves(rw_hw[0:HD, :]), PS[0:HD, 0:2, 0:HALF], ACT.Tanh).then_inc(S(L + "hidden"), 1)
                act.wait_ge(S(L + "lora_mm"), 2)
                act.activation(halves(rw_ha[0:HD, :]), PS[0:HD, 2:4, 0:HALF], ACT.Copy).then_inc(S(L + "hidden"), 1)
                act.wait_ge(S(L + "lora_mm"), 3)
                act.activation(halves(rw_hg), acc(2), ACT.Sigmoid).then_inc(S(L + "hidden"), 1)
                cur = lambda v: rw_cur[:, v:v + 1]
                with act.Fori(0, HEADS) as h:
                    act.wait_ge(S(L + "ob"), h + 1)
                    done(base, h, 0)
                    act.activation(halves(rw_r), acc(0), ACT.Copy).then_inc(S(L + "ev_r"), 1)
                    done(base, h, 1)
                    act.activation(halves(rw_k), acc(1), ACT.Copy).then_inc(S(L + "ev_k"), 1)
                    done(base, h, 2)
                    act.activation(halves(rw_v), acc(0), ACT.Copy).then_inc(S(L + "ev_v"), 1)
                    act.wait_ge(S(L + "cur"), h + 1)
                    act.wait_ge(S(L + "lora2_mm"), h * 3 + 1)
                    act.activation(halves(rw_sg), acc(1), ACT.Sigmoid, bias=cur(V_W0)).then_inc(S(L + "ev_w"), 1)
                    act.wait_ge(S(L + "lora2_mm"), h * 3 + 2)
                    act.activation(halves(rw_a), acc(0), ACT.Sigmoid, bias=cur(V_A0)).then_inc(S(L + "ev_a"), 1)
                    act.wait_ge(S(L + "lora2_mm"), h * 3 + 3)
                    act.activation(halves(rw_g), acc(1), ACT.Copy).then_inc(S(L + "ev_g"), 1)
                    act.wait_ge(S(L + "bc"), h + 1)
                    act.activation(rw_p, rw_bc, ACT.Exp, scale=-KAPPA)
                    act.activation(rw_pi, rw_bc, ACT.Exp, scale=KAPPA)
                    act.drain()
                    act.activation(rw_pp, rw_pp, ACT.Exp, scale=-KAPPA).then_inc(S(L + "exps"), 1)
                    act.wait_ge(S(L + "kn"), h + 1)
                    act.activation(rw_rn, rw_kn, ACT.Square).then_inc(S(L + "kn_sq"), 1)
                    act.wait_ge(S(L + "kn_mm"), h + 1)
                    act.activation(halves(rw_rn), acc(2), ACT.Sqrt).then_inc(S(L + "kn_rt"), 1)
                    act.wait_ge(S(L + "tm_mm"), h + 1)
                    act.activation(rw_vtm, PS[:, 4, :], ACT.Copy)
                    act.activation(rw_ztm, PS[:, 5, :], ACT.Copy)
                    act.activation(rw_kptm, PS[:, 6, :], ACT.Copy)
                    act.activation(rw_bptm, PS[:, 7, :], ACT.Copy)
                    act.activation(rw_tms[0:NS_TOK, :], PS[0:NS_TOK, 0, :], ACT.Copy).then_inc(S(L + "tm_ev"), 1)
                    for lv in range(1, 6):
                        act.wait_ge(S(L + "y_mm"), h * 5 + lv)
                        y = act.activation(rw_y, PS[:, 4, :], ACT.Copy)
                        if lv == 1:
                            y = act.activation(rw_ys[0:NS_TOK, :], PS[0:NS_TOK, 5, 0:2 * NS_TOK], ACT.Copy)
                        y.then_inc(S(L + "y_ev"), 1)
                    act.wait_ge(S(L + "hw_mm"), h + 1)
                    act.activation(rw_hv, PS[:, 4, :], ACT.Copy)
                    act.activation(rw_wt, PS[:, 5, :], ACT.Copy)
                    act.activation(rw_hvs[0:NS_TOK, :], PS[0:NS_TOK, 6, 0:P], ACT.Copy)
                    act.activation(rw_wts, PS[:, 7, 0:NS_TOK], ACT.Copy).then_inc(S(L + "hw_ev"), 1)
                    for n in range(N2):
                        act.wait_ge(S(L + "u_mm"), h * N2 + n + 1)
                        act.activation(rw_nu[:, n * C2:(n + 1) * C2], PS[:, 4 + n % 2, 0:HD], ACT.Copy, scale=-1.0)\
                            .then_inc(S(L + "nu"), 1)
                    act.wait_ge(S(L + "us_mm"), h + 1)
                    act.activation(rw_ufm.rearrange("p (n t) -> p n t", n=2), PS[:, 4:6, 0:NS_TOK], ACT.Copy)\
                        .then_inc(S(L + "us_ev"), 1)
                    act.wait_ge(S(L + "ut_mm"), h + 1)
                    act.activation(rw_nutm[0:NS_TOK, :], PS[0:NS_TOK, 5, 0:P], ACT.Copy, scale=-1.0).then_inc(S(L + "ut_ev"), 1)
                    act.wait_ge(S(L + "o_mm"), h + 1)
                    act.activation(rw_o[:, 0:NP_TOK], PS[:, 0, :], ACT.Copy)
                    act.activation(rw_o[:, NP_TOK:NT], PS[:, 1, 0:NS_TOK], ACT.Copy).then_inc(S(L + "o_ev"), 1)
                    act.wait_ge(S(L + "oc"), h + 1)
                    act.activation(rw_o, rw_oc, ACT.Square).then_inc(S(L + "oc_sq"), 1)
                    act.wait_ge(S(L + "var_mm"), h + 1)
                    act.activation(halves(rw_rn), acc(2), ACT.Sqrt, scale=1.0 / HD, bias=c_gn).then_inc(S(L + "gn_rt"), 1)

            act.wait_ge(S("setup"), 1)
            act.wait_ge(S("lb_sub"), 1)
            act.activation(lbs[:, :], lbs[:, :], ACT.Exp).then_inc(S("lb_exp"), 1)
            ready, count = "consts_in", 16 * NCONST_LOADS
            for layer in range(depth):
                (hgrn, attention, rwkv)[layer % 3](layer, ready, count)
                ready, count = (("hg_x", KC * (layer // 3 + 1) + CREDITS["hg_x"]), ("at_x", KC * HEADS + 1), ("rw_x", KC * HEADS + 1))[layer % 3]
                feed_forward(layer, ready, count)
                ready, count = "ff_x", KC * (layer + 1) + CREDITS["ff_x"]
            norm("nfin", x3, ready, count)

        @block.vector
        def _(dve):
            def norm(name, src, gain):
                dve.wait_ge(S("norm_rms"), nth(name) + 1)
                dve.reciprocal(rstd[:, :], rstd[:, :])
                dve.drain()
                for c in range(KC):
                    dve.scalar_tensor_tensor(h3[:, c, :], src[:, c, :], vec3[:, gain, c:c + 1], rstd[:, :],
                                             ALU.mult, ALU.mult).then_inc(S("norm_h"), 1)

            def feed_forward(layer):
                norm(norm_name(layer, "f"), x3, V_FFN + layer)
                base = UB[layer, "up"]
                with dve.Fori(0, FC // 2) as i:
                    for par in range(2):
                        dve.wait_ge(S("ff_silu"), i * 2 + (par + 1 + FC * layer))
                        dve.wait_ge(S("unit_done"), i * 4 + (base + 2 * par + 2))
                        dve.tensor_tensor(halves(ff_act[:, bass.ds((i * 2 + par) * NT, NT)]), halves(ff_gate[par]),
                                          acc(2 * par + 1), ALU.mult).then_inc(S("ff_glu"), 1)
                base = UB[layer, "down"]
                with dve.Fori(0, KC // 2) as i:
                    for par in range(2):
                        dve.wait_ge(S("unit_done"), i * 4 + (base + 2 * par + 2))
                        xm = halves(X[:, bass.ds((i * 2 + par) * NT, NT)])
                        dve.tensor_tensor(xm, xm, acc(par), ALU.add).then_inc(S("ff_x"), 1)

            def hgrn(layer):
                L = "hg_"
                j = layer // 3
                norm(norm_name(layer, "m"), x3, V_MIX + layer)
                dve.memset(hg_at, 0.0)
                dve.memset(hg_ats, 0.0)
                lb = lbs[:, layer * KC:(layer + 1) * KC]
                oml = lbt[:, 0:KC]
                dve.tensor_scalar(oml, lb, -1.0, 1.0, ALU.mult, ALU.add)
                dve.drain()
                with dve.Fori(j * HEADS, (j + 1) * HEADS) as h:
                    dve.tensor_copy(scratch[:, 1:2], lbt[:, bass.ds(h - j * HEADS, 1)])
                    dve.tensor_copy(scratch[:, 3:4], lbs[:, bass.ds(h + (layer - j) * KC, 1)])
                    dve.drain()
                    dve.wait_ge(S(L + "ev_f"), h + 1)
                    dve.wait_ge(S(L + "ev_q"), h + 1)
                    dve.tensor_scalar(hg_f, hg_sgp, scratch[:, 1:2], scratch[:, 3:4], ALU.mult, ALU.add)
                    dve.tensor_scalar(hg_ks, hg_sgn, scratch[:, 1:2], None, ALU.mult)
                    dve.tensor_tensor(hg_q, hg_qs, hg_qr, ALU.mult).then_inc(S(L + "raw_used"), 1)
                    dve.drain()
                    dve.tensor_scalar(hg_f, hg_f, F_MIN, None, ALU.max).then_inc(S(L + "lvl"), 1)
                    dve.wait_ge(S(L + "vt_ev"), h + 1)
                    dve.tensor_tensor(
                        hg_vx[0:NS_TOK, :].rearrange("p (b v) -> p b v", b=NB),
                        hg_vts[0:NS_TOK, :].unsqueeze(1).to_broadcast([NS_TOK, NB, P]),
                        const("bmask", NS_TOK).unsqueeze(2).to_broadcast([NS_TOK, NB, P]),
                        ALU.mult).then_inc(S(L + "vx"), 1)
                    dprev, doff = hg_f, 0
                    for n in range(LEVELS):
                        dve.drain()
                        dve.wait_ge(S(L + "lvl_mm"), h * LEVELS + n + 1)
                        if n == 0:
                            dve.tensor_tensor(hg_qp, hg_q, hg_f, ALU.mult).then_inc(S(L + "lvl"), 1)
                        else:
                            size = NT if n <= 2 else NP_TOK
                            blk = 1 << (n - 1)
                            m = size // (2 * blk)
                            qv = hg_qp[:, 0:size].rearrange("p (m a b) -> p m a b", a=2, b=blk)
                            kv = hg_ks[:, 0:size].rearrange("p (m a b) -> p m a b", a=2, b=blk)
                            dv = dprev[:, 0:size // blk].rearrange("p (m a) -> p m a", a=2)
                            if n < LEVELS - 1 or True:
                                dn = hg_d[:, doff:doff + m]
                                doff += m
                                dve.tensor_tensor(dn, dv[:, :, 0], dv[:, :, 1], ALU.mult)
                            dve.tensor_tensor(qv[:, :, 1, :], qv[:, :, 1, :],
                                              dv[:, :, 0:1].to_broadcast([P, m, blk]), ALU.mult)
                            dve.tensor_tensor(kv[:, :, 0, :], kv[:, :, 0, :],
                                              dv[:, :, 1:2].to_broadcast([P, m, blk]), ALU.mult).then_inc(S(L + "lvl"), 1)
                            if n == 2:
                                ds_ = dn[:, NP_TOK // 4:NT // 4]
                            dprev = dn
                        if n <= 2:
                            dve.copy_predicated(hg_ats[0:NS_TOK, :], hg_mask[0:NS_TOK, n * P:n * P + NS_TOK],
                                                PS[0:NS_TOK, 7 - n % 2, 0:NS_TOK])
                        cp = dve.copy_predicated(
                            hg_at.rearrange("p (c t) -> p c t", c=NCH),
                            hg_mask[:, n * P:(n + 1) * P].unsqueeze(1).to_broadcast([P, NCH, P]),
                            PS[:, 4 + n % 2, :].rearrange("p (c t) -> p c t", c=NCH))
                    cp.then_inc(S(L + "at"), 1)
                    dve.wait_ge(S(L + "kv_mm"), h + 1)
                    dve.wait_ge(S(L + "st_free"), h + 1)
                    st = dve.tensor_copy(hg_s[:, 0:P], PS[:, 5, 0:P])
                    for c in range(1, NCH):
                        dve.drain()
                        st = dve.scalar_tensor_tensor(hg_s[:, c * P:(c + 1) * P], hg_s[:, (c - 1) * P:c * P],
                                                      dprev[:, c:c + 1], PS[:, 5, c * P:(c + 1) * P], ALU.mult, ALU.add)
                    st.then_inc(S(L + "s"), 1)
                    dve.wait_ge(S(L + "ev_g"), h + 1 + 1)
                    dve.wait_ge(S(L + "o_mm"), h + 1)
                    dve.tensor_tensor(O[:, bass.ds((h - j * HEADS) * NT, NP_TOK)], PS[:, 4, :], hg_gs[:, 0:NP_TOK], ALU.mult)
                    dve.tensor_tensor(O[:, bass.ds((h - j * HEADS) * NT + NP_TOK, NS_TOK)], PS[:, 5, 0:NS_TOK],
                                      hg_gs[:, NP_TOK:NT], ALU.mult).then_inc(S(L + "out"), 1)
                    for b in range(NB):
                        bs = slice(b * P, (b + 1) * P)
                        st = dve.scalar_tensor_tensor(hg_s0[:, bs], hg_s0[:, bs], ds_[:, b:b + 1],
                                                      PS[:, 6 + b // 4, (b % 4) * P:(b % 4 + 1) * P], ALU.mult, ALU.add)
                    st.then_inc(S(L + "state"), 1)
                norm(norm_name(layer, "o"), o3, V_HG + layer // 3)
                dve.wait_ge(S(L + "st_free"), HEADS * (j + 1) + 1)
                base = UB[layer, "out"]
                with dve.Fori(0, KC // 4) as i:
                    for k in range(4):
                        dve.wait_ge(S("unit_done"), i * 4 + (base + k + 1))
                        xm = halves(X[:, bass.ds((i * 4 + k) * NT, NT)])
                        dve.tensor_tensor(xm, xm, acc(k), ALU.add).then_inc(S(L + "x"), 1)

            def add_rows(L, h, base, d, accs):
                for m in range(KC):
                    if m < KC - 1:
                        dve.wait_ge(S(L + "out_mm"), h * (KC - 1) + m + 1)
                    else:
                        dve.wait_ge(S("unit_done"), h * 4 + (base + d + 1))
                    xm = halves(X[:, m * NT:(m + 1) * NT])
                    dve.tensor_tensor(xm, xm, acc(accs[m % len(accs)]), ALU.add).then_inc(S(L + "x"), 1)

            def attention(layer):
                L = "at_"
                base = UB[layer, "mix"]
                lv = lamv[:, :].rearrange("p (n e) -> p n e", n=4)
                for n in range(2):
                    dve.tensor_tensor(lv[:, 2 * n, :], lv[:, 2 * n, :], lv[:, 2 * n + 1, :], ALU.mult)
                dve.drain()
                dve.reduce_sum(c_lam[:, 0:1], lv[:, 0, :], AX.X)
                dve.reduce_sum(c_lam[:, 1:2], lv[:, 2, :], AX.X).then_inc(S(L + "lam_sum"), 1)
                dve.memset(c_sub, SUBLN_EPS)
                dve.tensor_scalar(c_gain, subln[:, :], 1.0 - LAM_INIT, None, ALU.mult)
                dve.wait_ge(S(L + "lam_exp"), 1)
                dve.tensor_tensor(c_nlam, c_lam[:, 3:4], c_lam[:, 2:3], ALU.subtract)
                dve.drain()
                dve.tensor_scalar(c_nlam, c_nlam, -LAM_INIT, None, ALU.add)
                dve.memset(c_sign, 1.0)
                dve.drain()
                dve.tensor_copy(c_sign[NS_TOK:2 * NS_TOK, :], c_nlam[NS_TOK:2 * NS_TOK, :])
                norm(norm_name(layer, "m"), x3, V_MIX + layer)
                dist = const("dist")

                def mix(h, more):
                    dve.tensor_copy(c_slope, consts[:, bass.ds(h + CO["slopes"][0], 1)])

                    def biased(qb):
                        keys, par = (qb + 1) * P, qb % 2
                        dve.drain()
                        dve.wait_ge(S(L + "score_mm"), h * NCH + qb + 1)
                        for c in range(2):
                            last = dve.scalar_tensor_tensor(at_sb[par][c][:, 0:keys], dist[:, NP_TOK - keys:], c_slope,
                                                            PS[:, 4 + c, 0:keys], ALU.mult, ALU.add)
                        last.then_inc(S(L + "scored"), 1)
                        dve.drain()
                        for c in range(2):
                            dve.reduce_max(c_nm[par][:, c:c + 1], at_sb[par][c][:, 0:keys], AX.X)
                        dve.drain()
                        dve.tensor_scalar(c_nm[par], c_nm[par], -1.0, None, ALU.mult).then_inc(S(L + "maxed"), 1)

                    biased(0)
                    for qb in range(NCH):
                        par = qb % 2
                        if qb < NCH - 1:
                            biased(qb + 1)
                        dve.wait_ge(S(L + "probs"), h * NCH + qb + 1)
                        dve.reciprocal(c_rl[par], c_ls[par])
                        dve.drain()
                        dve.tensor_tensor(c_rl[par][:, 1:2], c_rl[par][:, 1:2], c_nlam, ALU.mult)
                        dve.drain()
                        for c in range(2):
                            last = dve.tensor_scalar(at_diag[par][c], const("ident"), c_rl[par][:, c:c + 1], None, ALU.mult)
                        last.then_inc(S(L + "diag"), 1)
                        dve.wait_ge(S(L + "o_mm"), h * (NCH + 1) + qb + 1)
                        dve.tensor_copy(at_o[:, qb * P:(qb + 1) * P], PS[:, 7, 0:P]).then_inc(S(L + "o_ev"), 1)
                    dve.wait_ge(S(L + "ss_mm"), h + 1)
                    dve.scalar_tensor_tensor(at_ss[0:64, :], const("bs", 64), c_slope[0:64, :], PS[0:64, 5, 0:PAST + NS_TOK],
                                             ALU.mult, ALU.add)
                    dve.drain()
                    dve.reduce_max(c_snm[0:64, :], at_ss[0:64, :], AX.X)
                    dve.drain()
                    dve.tensor_scalar(c_snm[0:64, :], c_snm[0:64, :], -1.0, None, ALU.mult).then_inc(S(L + "smaxed"), 1)
                    dve.wait_ge(S(L + "sprobs"), h + 1)
                    dve.reciprocal(c_srl[0:64, :], c_sls[0:64, :])
                    dve.drain()
                    dve.tensor_tensor(c_sco[0:64, :], c_srl[0:64, :], c_sign[0:64, :], ALU.mult)
                    dve.drain()
                    dve.tensor_scalar(at_selc[0:64, :], const("sel", 64), c_sco[0:64, :], None, ALU.mult)\
                        .then_inc(S(L + "selc"), 1)
                    dve.wait_ge(S(L + "o_mm"), (h + 1) * (NCH + 1))
                    dve.tensor_copy(at_o[:, NP_TOK:NT], PS[:, 7, 0:NS_TOK]).then_inc(S(L + "o_ev"), 1)
                    dve.wait_ge(S(L + "orms"), h + 1)
                    dve.reciprocal(at_rs, at_rs)
                    dve.drain()
                    dve.scalar_tensor_tensor(at_ob, at_o, c_gain, at_rs, ALU.mult, ALU.mult).then_inc(S(L + "ob"), 1)
                    add_rows(L, h, base, 6 if more else 3, (1, 2, 3))

                with dve.Fori(0, HEADS - 1) as h:
                    mix(h, True)
                mix(HEADS - 1, False)
                dve.wait_ge(S(L + "kv_free"), HEADS + 1)

            def rwkv(layer):
                L = "rw_"
                base = UB[layer, "mix"]
                dve.memset(c_gn, GN_EPS)
                norm(norm_name(layer, "m"), x3, V_MIX + layer)
                dve.drain()
                dve.tensor_tensor(o3[:, :, 1:NP_TOK], h3[:, :, 0:NP_TOK - 1], h3[:, :, 1:NP_TOK], ALU.subtract)
                dve.tensor_scalar(o3[:, :, 0:1], h3[:, :, 0:1], -1.0, None, ALU.mult)
                for c in range(KC):
                    hs = h3[:, c, NP_TOK:NT].rearrange("p (b t) -> p b t", t=TB)
                    os_ = o3[:, c, NP_TOK:NT].rearrange("p (b t) -> p b t", t=TB)
                    dve.tensor_tensor(os_[:, :, 1:TB], hs[:, :, 0:TB - 1], hs[:, :, 1:TB], ALU.subtract)
                    dve.tensor_tensor(os_[:, :, 0], vec3[:, V_SHIFT:V_SHIFT + NB, c], hs[:, :, 0], ALU.subtract)
                sh = rw_sh.rearrange("p (c n) -> p c n", c=KC)
                dve.tensor_copy(sh[:, :, 0:1], h3[:, :, NP_TOK - 1:NP_TOK])
                dve.tensor_copy(sh[:, :, 1:9], h3[:, :, NP_TOK + TB - 1:NT:TB]).then_inc(S(L + "shift"), 1)
                dve.drain()
                for n, (mix, dst, mm) in enumerate(((3, rw_xk, 0), (4, rw_xv, 0), (5, rw_xk, 1), (1, rw_xk, 3),
                                                    (2, rw_xv, 3), (0, H, 3))):
                    if mm:
                        dve.wait_ge(S(L + "lora_mm"), mm)
                    for c in range(KC):
                        last = dve.scalar_tensor_tensor(dst[:, c * NT:(c + 1) * NT], o3[:, c, :],
                                                        vec3[:, V_RWMIX + mix, c:c + 1], h3[:, c, :], ALU.mult, ALU.add)
                    last.then_inc(S(L + "xm"), 1)
                dve.wait_ge(S(L + "hidden"), 3)
                dve.memset(rw_st[:, 0:HD], 0.0)
                cur = lambda v: rw_cur[:, v:v + 1]

                def chunks(ap, n, c):
                    return ap.rearrange("p (n c) -> p n c", c=c)

                def pair(mask):
                    return mask.unsqueeze(1).to_broadcast([P, N2, C2])

                def pair32(mask):
                    return mask.unsqueeze(1).to_broadcast([NS_TOK, 2, NS_TOK])

                def mat(ap):
                    return ap.rearrange("p (n c) -> p n c", c=C2)

                def mat32(ap):
                    return ap[0:NS_TOK].rearrange("p (n c) -> p n c", c=NS_TOK)

                def level(n, upper):
                    o = CO["lvl64"][0] + (2 * n + upper) * C2
                    return consts[:, o:o + C2], consts[0:NS_TOK, o:o + NS_TOK]

                with dve.Fori(0, HEADS) as h:
                    dve.drain()
                    dve.tensor_copy(rw_cur.unsqueeze(2), vec3[:, :, bass.ds(h, 1)]).then_inc(S(L + "cur"), 1)
                    dve.drain()
                    dve.wait_ge(S(L + "ev_k"), h + 1)
                    dve.tensor_scalar(rw_kn, rw_k, cur(V_KK), None, ALU.mult).then_inc(S(L + "kn"), 1)
                    dve.wait_ge(S(L + "ev_w"), h + 1)
                    dve.tensor_tensor_scan(rw_bc, const("reset"), rw_sg, 0.0, ALU.mult, ALU.add)
                    dve.drain()
                    dve.tensor_tensor(rw_pp, rw_bc, rw_sg, ALU.subtract).then_inc(S(L + "bc"), 1)
                    dve.wait_ge(S(L + "ev_a"), h + 1)
                    dve.tensor_scalar(rw_be, rw_a, -1.0, cur(V_KA), ALU.add, ALU.mult)
                    dve.drain()
                    dve.scalar_tensor_tensor(rw_k2, rw_be, 1.0, rw_k, ALU.add, ALU.mult)
                    dve.drain()
                    dve.scalar_tensor_tensor(rw_k, rw_r, cur(V_RK), rw_k2, ALU.mult, ALU.mult).then_inc(S(L + "rk"), 1)
                    dve.wait_ge(S(L + "kn_rt"), h + 1)
                    dve.tensor_scalar(rw_rn, rw_rn, 1e-12, None, ALU.max)
                    dve.drain()
                    dve.reciprocal(rw_rn, rw_rn)
                    dve.drain()
                    dve.tensor_tensor(rw_kn, rw_kn, rw_rn, ALU.mult)
                    dve.drain()
                    dve.tensor_tensor(rw_be, rw_kn, rw_a, ALU.mult)
                    dve.wait_ge(S(L + "exps"), h + 1)
                    dve.tensor_tensor(rw_pp, rw_pp, rw_kn, ALU.mult)
                    dve.tensor_tensor(rw_k2, rw_k2, rw_pi, ALU.mult)
                    dve.tensor_tensor(rw_r, rw_r, rw_p, ALU.mult)
                    dve.drain()
                    dve.tensor_tensor(rw_be, rw_be, rw_pi, ALU.mult)
                    dve.drain()
                    pc = chunks(rw_p[:, 0:NP_TOK], N2, C2)[:, :, C2 - 1:C2]
                    pcs = chunks(rw_p[:, NP_TOK:NT], NB, TB)[:, :, TB - 1:TB]
                    for dst, src in ((rw_bc, rw_k2), (rw_kn, rw_be)):
                        dve.tensor_tensor(chunks(dst[:, 0:NP_TOK], N2, C2), chunks(src[:, 0:NP_TOK], N2, C2),
                                          pc.to_broadcast([P, N2, C2]), ALU.mult)
                        last = dve.tensor_tensor(chunks(dst[:, NP_TOK:NT], NB, TB), chunks(src[:, NP_TOK:NT], NB, TB),
                                                 pcs.to_broadcast([P, NB, TB]), ALU.mult)
                    last.then_inc(S(L + "ops"), 1)
                    dve.wait_ge(S(L + "bonus_mm"), h + 1)
                    dve.wait_ge(S(L + "ev_v"), h + 1)
                    dve.tensor_tensor(halves(rw_pi), acc(3), halves(rw_v), ALU.mult).then_inc(S(L + "bonus"), 1)
                    dve.wait_ge(S(L + "mat_mm"), h + 1)
                    for bank, dst, mask in ((4, rw_mt, "strict"), (5, rw_m, "low"), (6, rw_zkt, "strict"),
                                            (7, rw_rbt, "incl"), (0, rw_rkt, "incl")):
                        dve.tensor_tensor(mat(dst), mat(PS[:, bank, :]), pair(const(mask)), ALU.mult)
                    for i in range(2):
                        dve.tensor_tensor(rw_ms[0:NS_TOK, :].rearrange("p (m i c) -> p m i c", m=5, i=2)[:, :, i, :],
                                          PS[0:NS_TOK, 1 + i, 0:5 * NS_TOK].rearrange("p (m c) -> p m c", m=5),
                                          const("masks32", NS_TOK).rearrange("p (m c) -> p m c", m=5), ALU.mult)
                    dve.drain()
                    mts, ms = rw_ms[0:NS_TOK, 0:2 * NS_TOK], rw_ms[0:NS_TOK, 2 * NS_TOK:4 * NS_TOK]
                    for src, src32, dst, dst32, upper in ((rw_m, ms, rw_x, rw_xs, 0), (rw_mt, mts, rw_xt, rw_xts, 1)):
                        big, small = level(0, upper)
                        dve.tensor_tensor(mat(rw_tmp), mat(src), pair(big), ALU.mult)
                        dve.tensor_tensor(mat32(rw_tmps), mat32(src32), pair32(small), ALU.mult)
                        dve.drain()
                        dve.tensor_tensor(mat(dst), pair(const("eye64")), mat(rw_tmp), ALU.subtract)
                        dve.tensor_tensor(mat32(dst32), pair32(const("eye64", NS_TOK)[:, 0:NS_TOK]), mat32(rw_tmps), ALU.subtract)
                        dve.drain()
                    for lv in range(1, 6):
                        big, small = level(lv, 1)
                        if lv == 1:
                            dve.tensor_tensor(mat32(rw_mls), mat32(mts), pair32(small), ALU.mult)
                        dve.tensor_tensor(mat(rw_ml), mat(rw_mt), pair(big), ALU.mult).then_inc(S(L + "inv"), 1)
                        dve.wait_ge(S(L + "xy_mm"), h * 5 + lv)
                        if lv == 1:
                            dve.tensor_tensor(rw_xs[0:NS_TOK, :], rw_xs[0:NS_TOK, :], PS[0:NS_TOK, 5, 128:128 + 2 * NS_TOK], ALU.subtract)
                            dve.tensor_tensor(rw_xts[0:NS_TOK, :], rw_xts[0:NS_TOK, :], PS[0:NS_TOK, 5, 256:256 + 2 * NS_TOK], ALU.subtract)
                        dve.tensor_tensor(rw_x, rw_x, PS[:, 6, :], ALU.subtract)
                        last = dve.tensor_tensor(rw_xt, rw_xt, PS[:, 7, :], ALU.subtract)
                    last.then_inc(S(L + "inv"), 1)
                    def spread(dst, src):
                        return dve.tensor_tensor(dst[0:NS_TOK, :].rearrange("p (b v) -> p b v", b=NB),
                                                 src[0:NS_TOK, 0:P].unsqueeze(1).to_broadcast([NS_TOK, NB, P]),
                                                 const("bmask", NS_TOK).unsqueeze(2).to_broadcast([NS_TOK, NB, P]), ALU.mult)
                    spread(rw_vxs, rw_tms)
                    dve.drain()
                    dve.wait_ge(S(L + "st_free"), h + 1)
                    for n in range(N2):
                        if n:
                            dve.drain()
                        dve.wait_ge(S(L + "ds_mm"), h * N2 + n + 1)
                        dve.scalar_tensor_tensor(rw_st[:, (n + 1) * HD:(n + 2) * HD], rw_st[:, n * HD:(n + 1) * HD],
                                                 rw_p[:, n * C2 + C2 - 1:n * C2 + C2], PS[:, 6 + n % 2, 0:HD],
                                                 ALU.mult, ALU.add).then_inc(S(L + "st"), 1)
                    dve.wait_ge(S(L + "ut_ev"), h + 1)
                    spread(rw_nux, rw_nutm).then_inc(S(L + "nux"), 1)
                    dve.wait_ge(S(L + "o_ev"), h + 1)
                    dve.tensor_tensor(rw_o[:, NP_TOK:NT], rw_o[:, NP_TOK:NT], PS[:, 2, 0:NS_TOK], ALU.add)\
                        .then_inc(S(L + "o_sum"), 1)
                    dve.wait_ge(S(L + "dss_mm"), h + 1)
                    st3 = rw_st0.rearrange("p (b v) -> p b v", b=NB)
                    dve.tensor_tensor(st3, st3, pcs.to_broadcast([P, NB, HD]), ALU.mult)
                    dve.drain()
                    dve.tensor_tensor(rw_st0, rw_st0, PS[:, 6, :], ALU.add).then_inc(S(L + "state"), 1)
                    dve.wait_ge(S(L + "mu_mm"), h + 1)
                    dve.scalar_tensor_tensor(halves(rw_oc), acc(2), -1.0 / HD, halves(rw_o), ALU.mult, ALU.add)\
                        .then_inc(S(L + "oc"), 1)
                    dve.wait_ge(S(L + "gn_rt"), h + 1)
                    dve.reciprocal(rw_rn, rw_rn)
                    dve.drain()
                    dve.tensor_tensor(rw_oc, rw_oc, rw_rn, ALU.mult)
                    dve.drain()
                    dve.tensor_scalar(rw_oc, rw_oc, cur(V_LNW), cur(V_LNB), ALU.mult, ALU.add)
                    dve.drain()
                    dve.tensor_tensor(rw_oc, rw_oc, rw_pi, ALU.add)
                    dve.drain()
                    dve.wait_ge(S(L + "ev_g"), h + 1)
                    dve.tensor_tensor(rw_oc, rw_oc, rw_g, ALU.mult).then_inc(S(L + "ob"), 1)
                    add_rows(L, h, base, 3, (0, 1, 2, 3))
                dve.wait_ge(S(L + "st_free"), HEADS + 1)
                dve.wait_ge(S(L + "sh_out"), 16)

            def lower_bounds():
                raw = vec[:, V_LB * KC:(V_LB + 4) * KC]
                mx, sm, rs = lbt[:, 0:KC], lbt[:, KC:2 * KC], lbt[:, 2 * KC:3 * KC]
                dve.tensor_tensor(mx, raw[:, 0:KC], raw[:, KC:2 * KC], ALU.max)
                for n in (2, 3):
                    dve.drain()
                    dve.tensor_tensor(mx, mx, raw[:, n * KC:(n + 1) * KC], ALU.max)
                dve.drain()
                dve.tensor_tensor(lbs[:, :].rearrange("p (l c) -> p l c", l=4), raw.rearrange("p (l c) -> p l c", l=4),
                                  mx.unsqueeze(1).to_broadcast([P, 4, KC]), ALU.subtract).then_inc(S("lb_sub"), 1)
                dve.wait_ge(S("lb_exp"), 1)
                dve.tensor_tensor(sm, lbs[:, 0:KC], lbs[:, KC:2 * KC], ALU.add)
                for n in (2, 3):
                    dve.drain()
                    dve.tensor_tensor(sm, sm, lbs[:, n * KC:(n + 1) * KC], ALU.add)
                dve.drain()
                dve.reciprocal(rs, sm)
                dve.drain()
                dve.tensor_tensor(lbs[:, :].rearrange("p (l c) -> p l c", l=4), lbs[:, :].rearrange("p (l c) -> p l c", l=4),
                                  rs.unsqueeze(1).to_broadcast([P, 4, KC]), ALU.mult)
                dve.drain()
                dve.memset(lbs[:, 0:KC], 0.0)
                for n in (2, 3):
                    dve.drain()
                    dve.tensor_tensor(lbs[:, n * KC:(n + 1) * KC], lbs[:, n * KC:(n + 1) * KC],
                                      lbs[:, (n - 1) * KC:n * KC], ALU.add)
                dve.drain()

            dve.memset(scratch[:, 0:1], RMS_EPS).then_inc(S("setup"), 1)
            dve.wait_ge(S("consts_in"), 16 * NCONST_LOADS)
            lower_bounds()
            for layer in range(depth):
                (hgrn, attention, rwkv)[layer % 3](layer)
                feed_forward(layer)
            norm("nfin", x3, V_FIN)

        @block.gpsimd
        def _(pool):
            for name, count in CREDITS.items():
                pool.sem_inc(S(name), count)

            def settle():
                pool.sem_inc(S("pool_settled"), 1)

            def hgrn(layer):
                L = "hg_"
                j = layer // 3
                with pool.Fori(j * HEADS, (j + 1) * HEADS) as h:
                    pool.dma_start(hg_s0, T["hg_s0"][bass.ds(h, 1), :, :].rearrange("a p n -> (a p) n"))\
                        .then_inc(S(L + "s0_in"), 16)
                    pool.wait_ge(S(L + "state"), h + 1 + 1)
                    settle()
                    pool.dma_start(T["hg_so"][bass.ds(h, 1), :, :].rearrange("a p n -> (a p) n"), hg_s0)\
                        .then_inc(S(L + "st_out"), 16)
                    pool.dma_start(T["hg_po"][bass.ds(h, 1), :, :].rearrange("a p n -> (a p) n"),
                                   hg_s[:, (NCH - 1) * P:NCH * P]).then_inc(S(L + "st_out"), 16)
                    pool.wait_ge(S(L + "st_out"), h * 32 + 32)
                    pool.sem_inc(S(L + "st_free"), 1)

            def head(t, i):
                return t[bass.ds(i, 1), :, :].rearrange("a p n -> (a p) n")

            def attention(layer):
                L = "at_"
                with pool.Fori(0, HEADS) as h:
                    pool.wait_ge(S(L + "st_mm"), h + 1)
                    settle()
                    for n in range(NB * PAGES):
                        page = pool.value_load(pages[0:1, n:n + 1], min_val=0, max_val=NPOOL - 1)
                        pool.dma_start(at_kc[:, n * P:(n + 1) * P], head(T["cache_k"], page * HEADS + h)).then_inc(S(L + "kc_in"), 16)
                    pool.wait_ge(S(L + "ob"), h + 1)
                    settle()
                    for n in range(NB * PAGES):
                        page = pool.value_load(pages[0:1, n:n + 1], min_val=0, max_val=NPOOL - 1)
                        pool.dma_start(at_vc[:, n * P:(n + 1) * P], head(T["cache_v"], page * HEADS + h)).then_inc(S(L + "vc_in"), 16)
                    pool.wait_ge(S(L + "ev_k"), h + 1)
                    settle()
                    pool.dma_start(head(T["k_out"], h), at_k).then_inc(S(L + "kv_out"), 16)
                    pool.wait_ge(S(L + "ev_v"), h + 1 + 1)
                    settle()
                    pool.dma_start(head(T["v_out"], h), at_v).then_inc(S(L + "kv_out"), 16)
                    pool.wait_ge(S(L + "kv_out"), h * 32 + 32)
                    pool.sem_inc(S(L + "kv_free"), 1)

            def rwkv(layer):
                L = "rw_"
                pool.wait_ge(S("norm_sq"), nth(norm_name(layer, "m")) * KC + 1)
                pool.dma_start(rw_lw, T["lora1"]).then_inc(S(L + "lw_in"), 16)
                pool.wait_ge(S(L + "shift"), 1)
                pool.dma_start(T["sh_out"], rw_sh).then_inc(S(L + "sh_out"), 16)
                with pool.Fori(0, HEADS) as h:
                    pool.wait_ge(S(L + "ob"), h + 1)
                    settle()
                    pool.dma_start(rw_ls[0:HD, 0:P], head(T["rw_w2"], h)).then_inc(S(L + "ls_in"), 16)
                    pool.dma_start(rw_ls[0:HD, P:2 * P], head(T["rw_a2"], h)).then_inc(S(L + "ls_in"), 16)
                    pool.dma_start(rw_ls[:, 2 * P:3 * P], head(T["rw_g2"], h)).then_inc(S(L + "ls_in"), 16)
                    pool.wait_ge(S(L + "lora_mm"), 3)
                    pool.dma_start(rw_st0, head(T["rw_s0"], h)).then_inc(S(L + "s0_in"), 16)
                    pool.wait_ge(S(L + "state"), h + 1)
                    settle()
                    pool.dma_start(head(T["rw_so"], h), rw_st0).then_inc(S(L + "st_out"), 16)
                    pool.dma_start(head(T["rw_po"], h), rw_st[:, N2 * HD:(N2 + 1) * HD]).then_inc(S(L + "st_out"), 16)
                    pool.wait_ge(S(L + "st_out"), h * 32 + 32)
                    pool.sem_inc(S(L + "st_free"), 1)
                pool.wait_ge(S(L + "sh_out"), 16)

            for layer in range(depth):
                if layer == 1:
                    pool.wait_ge(S("ff_x"), KC * layer + 1 + 1)
                    attention(layer)
                if layer == 2:
                    pool.wait_ge(S("ff_x"), KC * layer + 1 + 1)
                    rwkv(layer)
                if layer == 3:
                    pool.wait_ge(S("ff_x"), KC * layer + 1 + 1)
                if layer % 3 == 0:
                    hgrn(layer)


def column_units(w):
    k, m = w.shape
    return w.reshape(k // P, P, m // P, P).transpose(2, 1, 0, 3).reshape(m // P, P, k)


AHEAD_ORDER = [0, 1, 2] + [4 * h + n for h in range(1, HEADS) for n in (0, 1, 2, -1)] + [4 * HEADS - 1]


def layout(a, depth):
    arr = {}
    x = np.concatenate([a["x_prompt"].reshape(-1, D), a["x_sample"].reshape(-1, D)])
    arr["x"] = x.T.reshape(KC, P, NT).transpose(1, 0, 2).reshape(P, -1)
    rows = [a["norm_mix"], a["norm_ffn"], a["final_norm"][None], a["hg_norm"], a["rw_mix"][0]]
    rows += [a[n].reshape(1, D) for n in ("rw_w0", "rw_a0", "rw_k_k", "rw_k_a", "rw_r_k", "rw_ln_w", "rw_ln_b")]
    rows += [a["hg_lb_raw"], a["state_shift"][0]]
    v = np.concatenate(rows)
    assert v.shape[0] == NV
    arr["vec"] = v.reshape(NV, KC, P).transpose(2, 0, 1).reshape(P, -1)
    arr["subln"] = a["at_subln"].reshape(P, 1)
    arr["consts"], arr["mask"] = constants()
    for layer in range(depth):
        kind, j = layer % 3, layer // 3
        if kind == 0:
            u = column_units(a["hg_w_in"][j]).reshape(4, HEADS, P, D)
            arr[f"w_mix{layer}"] = u[[1, 0, 2, 3]].transpose(1, 0, 2, 3).reshape(4 * HEADS, P, D)
            arr[f"w_hgout{layer}"] = column_units(a["hg_w_out"][j])
        if kind == 1:
            u = column_units(a["at_w_in"][j]).reshape(3, HEADS, P, D)
            u = np.concatenate([u, a["at_w_out"][j].reshape(1, HEADS, P, D)])
            u = u.transpose(1, 0, 2, 3).reshape(4 * HEADS, P, D)
            arr[f"w_mix{layer}"] = u[AHEAD_ORDER]
        if kind == 2:
            u = np.stack([column_units(w) for w in a["rw_w_rkv"][j]] + [a["rw_w_o"][j].reshape(HEADS, P, D)])
            arr[f"w_mix{layer}"] = u.transpose(1, 0, 2, 3).reshape(4 * HEADS, P, D)
        up = column_units(a["ffn_w_in"][layer]).reshape(2, FC, P, D).transpose(1, 0, 2, 3)
        arr[f"w_up{layer}"] = up.reshape(2 * FC, P, D)
        down = column_units(a["ffn_w_out"][layer]).reshape(KC, P, 2, SLOT).transpose(0, 2, 1, 3)
        arr[f"w_down{layer}"] = down.reshape(2 * KC, P, SLOT)
    nh = len(a["state_hgrn"])
    arr["hg_s0"] = a["state_hgrn"].transpose(0, 2, 3, 1, 4).reshape(nh * HEADS, P, NB * P)
    arr["lam"] = np.tile(a["at_lam"].reshape(1, -1), (P, 1))
    arr["pages"] = a["page_table"].reshape(1, -1).astype(np.int32)
    arr["cache_k"] = a["cache_k"][0].transpose(0, 2, 3, 1).reshape(NPOOL * HEADS, P, P)
    arr["cache_v"] = a["cache_v"][0].transpose(0, 2, 1, 3).reshape(NPOOL * HEADS, P, P)
    lora = np.concatenate([a["rw_w1"][0], a["rw_a1"][0], a["rw_g1"][0]], 1)
    arr["lora1"] = lora.reshape(KC, P, 256).transpose(1, 0, 2).reshape(P, -1)
    for n in ("w2", "a2", "g2"):
        w = a[f"rw_{n}"][0]
        arr[f"rw_{n}"] = w.reshape(len(w), KC, P).transpose(1, 0, 2)
    st = a["state_rwkv"][0].reshape(NB, HEADS, 2, HD, HD)
    arr["rw_s0"] = st.transpose(1, 2, 4, 0, 3).reshape(HEADS, P, NB * HD)
    return arr


OUTS = {"y": (P, KC * NT), "hg_so": (2 * HEADS, P, NB * P), "hg_po": (2 * HEADS, P, P),
        "k_out": (HEADS, P, NT), "v_out": (HEADS, P, NT), "rw_so": (HEADS, P, NB * HD), "rw_po": (HEADS, P, HD),
        "sh_out": (P, KC * 9)}


def unpack(o):
    y = o["y"].reshape(P, KC, NT).transpose(2, 1, 0).reshape(NT, D)
    so = o["hg_so"].reshape(2, HEADS, P, NB, P).transpose(0, 3, 1, 2, 4)
    po = o["hg_po"].reshape(2, 1, HEADS, P, P)
    k, v = (o[n].transpose(2, 0, 1) for n in ("k_out", "v_out"))
    rs = o["rw_so"].reshape(HEADS, 2, HD, NB, HD).transpose(3, 0, 1, 4, 2).reshape(1, NB, 2 * HEADS, HD, HD)
    rp = o["rw_po"].reshape(HEADS, 2, HD, HD).transpose(0, 1, 3, 2).reshape(1, 1, 2 * HEADS, HD, HD)
    sh = o["sh_out"].reshape(P, KC, 9).transpose(2, 1, 0).reshape(9, D)
    sample = (1, NB, TB, HEADS, P)
    return (y[None, :NP_TOK], y[NP_TOK:].reshape(NB, TB, D), po, so, k[None, None, :NP_TOK], v[None, None, :NP_TOK],
            k[NP_TOK:].reshape(sample), v[NP_TOK:].reshape(sample), rp, sh[None, 0:1], rs, sh[None, 1:])


def kernel(**inputs):
    import concourse.bacc as bacc
    from concourse.bass_utils import run_bass_kernel_spmd

    a = {k: np.asarray(v) for k, v in inputs.items()}
    nc = bacc.Bacc("TRN2", target_bir_lowering=False, num_devices=1)
    arrays = {f"in_{k}": np.ascontiguousarray(v) for k, v in layout(a, DEPTH).items()}
    T = {k[3:]: nc.dram_tensor(k, v.shape, mybir.dt.from_np(v.dtype), kind="ExternalInput").ap()
         for k, v in arrays.items()}
    for k, shape in OUTS.items():
        T[k] = nc.dram_tensor(f"out_{k}", shape, F32, kind="ExternalOutput").ap()
    build(nc, T, DEPTH)
    r = run_bass_kernel_spmd(nc, [arrays], core_ids=[0]).results[0]
    return unpack({k: r[f"out_{k}"] for k in OUTS})
```

```python
import math
from contextlib import ExitStack

import numpy as np

import concourse.bass as bass
from concourse import mybir

F32 = mybir.dt.float32
I32 = mybir.dt.int32
F32R = mybir.dt.float32r
ALU = mybir.AluOpType
ACT = mybir.ActivationFunctionType
AX = mybir.AxisListType

D = 1024
P = 128
KC = D // P
NP_TOK = 512
NB, TB = 8, 4
NS_TOK = NB * TB
NT = NP_TOK + NS_TOK
HALF = NT // 2
DEPTH = 4
DFF = 2816
FC = DFF // P
FU = FC // 2
HU = 2 * FU + KC
SLOTS = 4
SLOT = FU * P
HEADS = 8
CH = 128
NCH = NP_TOK // CH
LEVELS = 8
RMS_EPS = 1e-6
SUBLN_EPS = 1e-5
GN_EPS = 64e-5
F_MIN = 1e-30
HD = 64
C2 = 64
N2 = NP_TOK // C2
PAST = 256
PAGES = 2
NPOOL = 20
NEG = -1e30
LAYER_AT, LAYER_RW = 1, 2
LAM_INIT = 0.8 - 0.6 * math.exp(-0.3 * LAYER_AT)

V_MIX, V_FFN, V_FIN, V_HG, V_RWMIX = 0, 4, 8, 9, 11
V_W0, V_A0, V_KK, V_KA, V_RK, V_LNW, V_LNB, V_LB, V_SHIFT = 17, 18, 19, 20, 21, 22, 23, 24, 28
NV = 36

CONSTS = [("ident", P), ("ones", P), ("blocks", P), ("slopes", HEADS), ("bmask", NB),
          ("reset", NT), ("strict", C2), ("incl", C2), ("bs", PAST + NS_TOK), ("sel", NS_TOK),
          ("dist", NP_TOK), ("lvl64", 6 * 2 * C2), ("low", C2), ("eye64", C2), ("masks32", 5 * NS_TOK)]
CO = {}
_o = 0
for _n, _w in CONSTS:
    CO[_n] = (_o, _w)
    _o += _w
NCONST = _o


def constants():
    c = np.zeros((P, NCONST), np.float32)

    def put(name, a):
        o, w = CO[name]
        a = np.asarray(a, np.float32).reshape(-1, w)
        c[:a.shape[0], o:o + w] = a

    i = np.arange(P)
    put("ident", np.eye(P))
    put("ones", np.ones((P, P)))
    put("blocks", (i[:, None] // HD == i[None] // HD))
    put("slopes", np.tile(np.exp2(-8.0 * np.arange(1, HEADS + 1) / HEADS), (P, 1)))
    t = np.arange(NS_TOK)
    put("bmask", t[:, None] // TB == np.arange(NB)[None])
    r = np.ones(NT)
    r[:NP_TOK:C2] = 0
    r[NP_TOK::TB] = 0
    put("reset", np.tile(r, (P, 1)))
    s, u = np.arange(P)[:, None] % C2, np.arange(C2)[None]
    put("strict", s < u)
    put("incl", s <= u)
    row, key = np.arange(64)[:, None] % NS_TOK, np.arange(PAST + NS_TOK)[None]
    b, tt, new = row // TB, row % TB, key - PAST
    past = -(PAST + tt - key).astype(np.float64)
    fresh = np.where((new // TB == b) & (new % TB <= tt), -(tt - new % TB).astype(np.float64), NEG)
    put("bs", np.where(key < PAST, past, fresh))
    put("sel", (np.arange(64)[:, None] % NS_TOK == t[None]))
    j = np.arange(NP_TOK)[None] - (NP_TOK - P)
    q = np.arange(P)[:, None]
    put("dist", np.where(j <= q, -(q - j).astype(np.float64), NEG))
    lv = np.zeros((P, 6, 2, C2))
    for n in range(6):
        off = (s >> (n + 1) == u >> (n + 1)) & (s >> n != u >> n)
        lv[:, n, 0] = off & (s > u)
        lv[:, n, 1] = off & (s < u)
    put("lvl64", lv.reshape(P, -1))
    put("low", s > u)
    put("eye64", s == u)
    sb_, sa = t[:, None], t[None]
    same = sb_ // TB == sa // TB
    up, low, inc = same & (sb_ < sa), same & (sb_ > sa), same & (sb_ <= sa)
    put("masks32", np.stack([up, low, up, inc, inc], 1).reshape(NS_TOK, -1))
    m = np.zeros((P, LEVELS, P), np.int32)
    a, z = i[:, None], i[None]
    m[:, 0] = a == z
    for n in range(1, LEVELS):
        m[:, n] = (a >> n == z >> n) & (a >> (n - 1) != z >> (n - 1)) & (a < z)
    return c, m.reshape(P, -1)


CREDITS = {"hg_x": 4, "ff_glu": 2, "ff_x": 2}
CREDITS.update({n: 1 for n in (
    "hg_ev_v", "hg_ev_g", "hg_state", "hg_raw_used", "hg_vt_mm", "hg_out", "hg_st_free",
    "at_x", "at_st_mm", "at_ev_v", "at_scored", "at_o_ev", "at_kv_free", "at_ob", "rw_x", "rw_ev_a", "rw_ev_g", "rw_st", "rw_st_free", "rw_ob")})


class Semaphores:

    def __init__(self, nc, ctx):
        self.nc, self.ctx, self.known = nc, ctx, {}

    def __call__(self, name):
        if name not in self.known:
            self.known[name] = self.ctx.enter_context(self.nc.semaphore(name))
        return self.known[name]


class Arena:

    def __init__(self, tensor, size):
        self.tensor, self.size, self.at = tensor, size, 0

    def take(self, n):
        a = self.tensor[:, self.at:self.at + n]
        self.at += n
        assert self.at <= self.size, (self.at, self.size)
        return a


def unit_bases(depth):
    base, at = {}, 0
    for layer in range(depth):
        base[layer, "mix"] = at
        at += 4 * HEADS
        if layer % 3 == 0:
            base[layer, "out"] = at
            at += KC
        base[layer, "ff"] = at
        at += 2 * HU
    return base


def build(nc, T, depth=DEPTH):
    UB = unit_bases(depth)
    with ExitStack() as ctx:
        def sb(name, shape, dt=F32):
            return ctx.enter_context(nc.sbuf_tensor(name, shape, dt))

        S = Semaphores(nc, ctx)
        X = sb("x", [P, KC * NT])
        H = sb("h", [P, KC * NT])
        O = sb("o", [P, KC * NT])
        ring = sb("ring", [P, SLOTS * SLOT])
        rstd = sb("rstd", [P, NT])
        vec = sb("vec", [P, NV * KC])
        lbs = sb("lbs", [P, 4 * KC])
        lbt = sb("lbt", [P, 6 * KC])
        consts = sb("consts", [P, NCONST])
        subln = sb("subln", [P, 1])
        scratch = sb("scratch", [P, 4])
        hg_mask_t = sb("hg_mask", [P, LEVELS * P], I32)
        hg_mask = hg_mask_t[:, :]
        ARENA = 29104
        SPLIT = 2 * (KC + FU) * NT + 4 * SLOT
        with nc.sbuf_tensor("arena_r", [P, SPLIT], F32R) as arena_r:
            pass
        arena_t = sb("arena", [P, ARENA])
        PS = ctx.enter_context(nc.psum_tensor("ps", [P, 8, 512], F32))

        x3 = X[:, :].rearrange("p (c t) -> p c t", c=KC)
        h3 = H[:, :].rearrange("p (c t) -> p c t", c=KC)
        o3 = O[:, :].rearrange("p (c t) -> p c t", c=KC)
        vec3 = vec[:, :].rearrange("p (v c) -> p v c", v=NV)

        def const(name, rows=P):
            o, w = CO[name]
            return consts[0:rows, o:o + w]

        def slot(k, c):
            return ring[:, k * SLOT + c * P:k * SLOT + (c + 1) * P]

        def acc(k):
            return PS[:, 2 * k:2 * k + 2, 0:HALF]

        def halves(ap):
            return ap.rearrange("p (a t) -> p a t", a=2)

        NCONST_LOADS = 7
        lamv = sb("lamv", [P, 4 * HD])
        pages = sb("pages", [1, NB * PAGES], I32)
        cell = sb("cell", [P, 64])

        ar = Arena(arena_r, SPLIT)
        hh, hl = (ar.take(KC * NT) for _ in range(2))
        wh = [ar.take(SLOT) for _ in range(2)]
        wl = [ar.take(SLOT) for _ in range(2)]
        shared = ar.at
        ff_ah, ff_al = (ar.take(FU * NT) for _ in range(2))
        ff_gate = [O[:, n * NT:(n + 1) * NT] for n in range(2)]

        ar = Arena(arena_t, ARENA)
        ar.take(shared)
        hg_sgp, hg_sgn, hg_qs, hg_qr, hg_v, hg_gs = (ar.take(NT) for _ in range(6))
        hg_f, hg_q, hg_qp, hg_ks = (ar.take(NT) for _ in range(4))
        hg_d = ar.take(NT)
        hg_at, hg_ats = ar.take(NP_TOK), ar.take(NS_TOK)
        hg_vt, hg_vts = ar.take(NP_TOK), ar.take(P)
        hg_kt, hg_kts = ar.take(NP_TOK), ar.take(P)
        hg_vx = ar.take(NB * P)
        hg_s = ar.take(NCH * P)
        hg_s0 = ar.take(NB * P)

        ar = Arena(arena_t, ARENA)
        at_q, at_k, at_v = (ar.take(NT) for _ in range(3))
        at_vt, at_vts = ar.take(NP_TOK), ar.take(P)
        at_kc, at_vc = ar.take(NB * PAGES * P), ar.take(NB * PAGES * P)
        at_sb = [[ar.take(NP_TOK) for _ in range(2)] for _ in range(2)]
        at_p = [[ar.take(NP_TOK) for _ in range(2)] for _ in range(2)]
        at_diag = [[ar.take(P) for _ in range(2)] for _ in range(2)]
        at_at = ar.take(NP_TOK)
        at_o, at_sq, at_rs, at_ob = (ar.take(NT) for _ in range(4))
        at_st, at_stn = ar.take(PAGES * 64), ar.take(64)
        at_ss, at_sp = ar.take(PAST + NS_TOK), ar.take(PAST + NS_TOK)
        at_selc = ar.take(NS_TOK)
        at_att, at_atn = ar.take(PAGES * NS_TOK), ar.take(NS_TOK)
        c_nm, c_ls, c_rl = ([cell[:, o + 2 * n:o + 2 * n + 2] for n in range(2)] for o in (20, 24, 28))
        c_snm, c_sls, c_srl, c_sco = cell[:, 6:7], cell[:, 7:8], cell[:, 8:9], cell[:, 9:10]
        c_slope, c_gain, c_sign, c_nlam = cell[:, 10:11], cell[:, 11:12], cell[:, 12:13], cell[:, 13:14]
        c_w0a0, c_w0, c_a0 = cell[:, 32:34], cell[:, 32:33], cell[:, 33:34]
        c_lam, c_sub, c_gn = cell[:, 14:18], cell[:, 18:19], cell[:, 19:20]

        ar = Arena(arena_t, ARENA)
        rw_xk, rw_xv = ar.take(KC * NT), ar.take(KC * NT)
        rw_hw, rw_ha, rw_hg = (ar.take(NT) for _ in range(3))
        rw_ls = ar.take(3 * P)
        rw_cur = ar.take(NV)
        rw_sh = ar.take(KC * 9)
        rw_rr, rw_r, rw_k, rw_v, rw_sg, rw_a, rw_g = (ar.take(NT) for _ in range(7))
        rw_bc, rw_p, rw_pi, rw_pp, rw_kn, rw_rn, rw_k2, rw_be = (O[:, n * NT:(n + 1) * NT] for n in range(8))
        rw_o, rw_oc = ar.take(NT), ar.take(NT)
        mats_at = ar.at
        MW = N2 * C2
        rw_mt, rw_m, rw_zkt, rw_rbt, rw_rkt, rw_x, rw_xt, rw_ml, rw_y, rw_hv, rw_wt = (ar.take(MW) for _ in range(11))
        rw_vtm, rw_ztm, rw_kptm, rw_bptm, rw_nu, rw_tmp = (ar.take(MW) for _ in range(6))
        rw_ms = ar.take(5 * 2 * NS_TOK)
        rw_xs, rw_xts, rw_mls, rw_ys, rw_tmps = (ar.take(2 * NS_TOK) for _ in range(5))
        rw_tms = ar.take(4 * P)
        rw_hvs, rw_wts, rw_ufm, rw_nutm = ar.take(P), ar.take(NS_TOK), ar.take(2 * NS_TOK), ar.take(P)
        rw_vxs, rw_nux = ar.take(NB * P), ar.take(NB * P)
        rw_st0 = ar.take(NB * HD)
        rw_st = ar.take((N2 + 1) * HD)
        rw_lw = arena_t[:, mats_at:mats_at + KC * 256]
        KAPPA = math.exp(-0.5)

        block = ctx.enter_context(nc.Block())

        norms = []
        for layer in range(depth):
            norms += [f"n{layer}m"] + [f"n{layer}o"] * (layer % 3 == 0) + [f"n{layer}f"]
        norms += ["nfin"]

        def norm_name(layer, which):
            return f"n{layer}{which}"

        def nth(name):
            return norms.index(name)

        @block.sync
        def _(sp):
            sp.dma_start(consts[:, :], T["consts"]).then_inc(S("consts_in"), 16)
            sp.dma_start(vec[:, :], T["vec"]).then_inc(S("consts_in"), 16)
            sp.dma_start(subln[:, :], T["subln"]).then_inc(S("consts_in"), 16)
            sp.dma_start(X[:, :], T["x"]).then_inc(S("consts_in"), 16)
            sp.dma_start(lamv[:, :], T["lam"]).then_inc(S("consts_in"), 16)
            sp.dma_start(pages[:, :], T["pages"]).then_inc(S("consts_in"), 16)

            def units(src, width, ubase, off, count, first=False):
                def load(i, k, free):
                    u = ubase + k
                    if free:
                        sp.wait_ge(S("unit_done"), i * 4 + (u - 3))
                    sp.dma_start(ring[:, u % 4 * SLOT:u % 4 * SLOT + width],
                                 src[bass.ds(i * 4 + (off + k), 1), :, :].rearrange("a p n -> (a p) n"))\
                      .then_inc(S(f"slot_in{u % 4}"), 16)

                if first:
                    for k in range(SLOTS):
                        load(0, k, False)
                with sp.Fori(1 if first else 0, count // 4) as i:
                    for k in range(SLOTS):
                        load(i, k, True)
                for k in range(count % 4):
                    load(count // 4, k, True)

            for layer in range(depth):
                kind = layer % 3
                units(T[f"w_mix{layer}"], D, UB[layer, "mix"], 0, 4 * HEADS, layer == 0)
                if kind == 0:
                    units(T[f"w_hgout{layer}"], D, UB[layer, "out"], 0, KC)
                for s in range(2):
                    base = UB[layer, "ff"] + HU * s
                    units(T[f"w_up{layer}"], D, base, 2 * FU * s, 2 * FU)
                    units(T[f"w_down{layer}"], SLOT, base + 2 * FU, KC * s, KC)
            sp.wait_ge(S("norm_h"), KC * len(norms))
            sp.dma_start(T["y"], H[:, :]).then_inc(S("y_out"), 16)
            sp.wait_ge(S("y_out"), 16)

        @block.tensor
        def _(pe):
            def settle():
                pe.sem_inc(S("pe_settled"), 1)

            def unit(k, a, rhs, blocks=KC, start=True, stop=True):
                for c in range(blocks):
                    for hf in range(2):
                        mm = pe.matmul(PS[:, 2 * a + hf, 0:HALF], slot(k, c), rhs(c, hf),
                                       start=start and c == 0, stop=stop and c == blocks - 1)
                return mm

            def from_h(c, hf):
                return h3[:, c, hf * HALF:(hf + 1) * HALF]

            def loaded(k, i, ubase):
                pe.wait_ge(S(f"slot_in{k}"), i * 16 + 16 * (ubase // 4 + 1))

            def norm(name):
                for c in range(KC):
                    pe.wait_ge(S("norm_sq"), nth(name) * KC + c + 1)
                    for hf in range(2):
                        mm = pe.matmul(PS[:, hf, 0:HALF], const("ones"), from_h(c, hf),
                                       start=c == 0, stop=c == KC - 1)
                mm.then_inc(S("norm_ssq"), 1)

            def block_product(a, w, c, hi, lo, start, stop):
                ws = slice(c * P, (c + 1) * P)
                for n, (part, rhs) in enumerate(((wh[w], hi), (wh[w], lo), (wl[w], hi))):
                    for hf in range(2):
                        o = c * NT + hf * HALF
                        mm = pe.matmul(PS[:, 2 * a + hf, 0:HALF], part[:, ws], rhs[:, o:o + HALF],
                                       start=start and n == 0, stop=stop and n == 2)
                return mm

            def feed_forward(layer):
                norm(norm_name(layer, "f"))

                def product(a, w, hi, lo, blocks, first=False):
                    for c in range(blocks):
                        if first:
                            pe.wait_ge(S("ff_hl"), KC * layer + c + 1)
                        mm = block_product(a, w, c, hi, lo, c == 0, c == blocks - 1)
                    mm.then_inc(S("unit_done"), 1)

                for s in range(2):
                    unit0, block0 = 2 * HU * layer + HU * s, FC * layer + FU * s

                    def up(i, par):
                        pe.wait_ge(S("ff_glu"), i * 2 + (par + block0) + 1)
                        for g in range(2):
                            pe.wait_ge(S("ff_wl"), i * 4 + (unit0 + 2 * par + g + 1))
                            product(2 * ((s + par) % 2) + g, g, hh, hl, KC, first=par == 0 and g == 0)

                    if s:
                        pe.wait_ge(S("ff_x"), 2 * KC * layer + KC + CREDITS["ff_x"])
                    with pe.Fori(0, FU // 2) as i:
                        for par in range(2):
                            up(i, par)
                    up(FU // 2, 0)
                    pe.wait_ge(S("ff_al"), block0 + FU)
                    with pe.Fori(0, KC // 2) as i:
                        for par in range(2):
                            pe.wait_ge(S("ff_x"), i * 2 + (par + 2 * KC * layer + KC * s) + 1)
                            pe.wait_ge(S("ff_wl"), i * 2 + (unit0 + 2 * FU + par + 1))
                            product(par, par, ff_ah, ff_al, FU)

            def hgrn(layer):
                L = "hg_"
                j = layer // 3
                norm(norm_name(layer, "m"))
                before = ("ev_v", "ev_g", "ev_f", "ev_q")

                def project(h, first, last, head0=False):
                    for n in range(first, last):
                        k, c = n // KC, n % KC
                        if c == 0:
                            pe.wait_ge(S(L + before[k]), h + 1)
                            pe.wait_ge(S(L + "wl"), h * 4 + (KC * j + k + 1))
                        if head0 and k == 0:
                            pe.wait_ge(S(L + "hl"), 2 * KC * j + c + 1)
                        mm = block_product(k % 2, k % 2, c, hh, hl, c == 0, c == KC - 1)
                        if c == KC - 1:
                            mm.then_inc(S("unit_done"), 1)

                def mix(h, more):
                    done = [0]

                    def ahead(n):
                        if more:
                            project(h + 1, done[0], done[0] + n)
                            done[0] += n

                    ahead(3)
                    pe.wait_ge(S(L + "ev_v"), h + 1 + 1)
                    pe.wait_ge(S(L + "state"), h + 1)
                    for c in range(NCH):
                        pe.transpose(PS[:, 6, c * P:(c + 1) * P], hg_v[:, c * P:(c + 1) * P], const("ident"))
                    pe.transpose(PS[0:NS_TOK, 7, 0:P], hg_v[:, NP_TOK:NT], const("ident")).then_inc(S(L + "vt_mm"), 1)
                    ahead(3)
                    pe.wait_ge(S(L + "vt_ev"), h + 1)
                    for n in range(LEVELS):
                        if n:
                            ahead(2)
                        pe.wait_ge(S(L + "lvl"), h * (LEVELS + 1) + n + 1)
                        q = hg_q if n == 0 else hg_qp
                        for c in range(NCH):
                            mm = pe.matmul(PS[:, 4 + n % 2, c * P:(c + 1) * P], hg_ks[:, c * P:(c + 1) * P],
                                           q[:, c * P:(c + 1) * P], start=True, stop=True)
                        if n <= 2:
                            mm = pe.matmul(PS[0:NS_TOK, 7 - n % 2, 0:NS_TOK], hg_ks[:, NP_TOK:NT],
                                           q[:, NP_TOK:NT], start=True, stop=True)
                        mm.then_inc(S(L + "lvl_mm"), 1)
                    ahead(2)
                    pe.wait_ge(S(L + "lvl"), (h + 1) * (LEVELS + 1))
                    for c in range(NCH):
                        pe.transpose(PS[:, 6, c * P:(c + 1) * P], hg_ks[:, c * P:(c + 1) * P], const("ident"))
                    pe.transpose(PS[0:NS_TOK, 7, 0:P], hg_ks[:, NP_TOK:NT], const("ident")).then_inc(S(L + "kt_mm"), 1)
                    ahead(1)
                    pe.wait_ge(S(L + "kt_ev"), h + 1)
                    pe.wait_ge(S(L + "at"), h + 1)
                    for c in range(NCH):
                        mm = pe.matmul(PS[:, 5, c * P:(c + 1) * P], hg_kt[:, c * P:(c + 1) * P],
                                       hg_vt[:, c * P:(c + 1) * P], start=True, stop=True)
                    mm.then_inc(S(L + "kv_mm"), 1)
                    pe.wait_ge(S(L + "vx"), h + 1)
                    for g in range(2):
                        mm = pe.matmul(PS[:, 6 + g, :], hg_kts[0:NS_TOK, :], hg_vx[0:NS_TOK, g * 512:(g + 1) * 512],
                                       start=True, stop=True)
                    mm.then_inc(S(L + "kvs_mm"), 1)
                    ahead(3)
                    pe.wait_ge(S(L + "s"), h + 1)
                    for c in range(NCH):
                        cs = slice(c * P, (c + 1) * P)
                        pe.matmul(PS[:, 4, cs], hg_vt[:, cs], hg_at[:, cs], start=True, stop=c == 0)
                        if c:
                            pe.matmul(PS[:, 4, cs], hg_s[:, (c - 1) * P:c * P], hg_qp[:, cs], start=False, stop=True)
                    pe.wait_ge(S(L + "s0_in"), h * 16 + 16)
                    pe.matmul(PS[:, 5, 0:NS_TOK], hg_vts[0:NS_TOK, :], hg_ats[0:NS_TOK, :], start=True, stop=False,
                              skip_group_check=True)
                    for b in range(NB):
                        bs = slice(b * TB, (b + 1) * TB)
                        mm = pe.matmul(PS[:, 5, bs], hg_s0[:, b * P:(b + 1) * P], hg_qp[:, NP_TOK + b * TB:NP_TOK + (b + 1) * TB],
                                       start=False, stop=b == NB - 1, skip_group_check=True)
                    mm.then_inc(S(L + "o_mm"), 1)
                    ahead(6)

                project(j * HEADS, 0, 4 * KC, head0=True)
                with pe.Fori(j * HEADS, (j + 1) * HEADS - 1) as h:
                    mix(h, True)
                mix((j + 1) * HEADS - 1, False)
                norm(norm_name(layer, "o"))
                with pe.Fori(0, KC // 4) as i:
                    for k in range(4):
                        pe.wait_ge(S(L + "x"), i * 4 + (k + KC * j) + 1)
                        pe.wait_ge(S(L + "wl"), i * 4 + (4 * HEADS * (j + 1) + KC * j + k + 1))
                        for c in range(KC):
                            if k == 0:
                                pe.wait_ge(S(L + "hl"), 2 * KC * j + KC + c + 1)
                            mm = block_product(k, k % 2, c, hh, hl, c == 0, c == KC - 1)
                        mm.then_inc(S("unit_done"), 1)

            def out_rows(L, h, base, rhs, d, accs):
                for m in range(KC):
                    if m >= len(accs):
                        pe.wait_ge(S(L + "x"), h * KC + (m - len(accs) + 1) + 1)
                    if m == 0:
                        loaded(d % 4, h, base + d - d % 4)
                    for hf in range(2):
                        mm = pe.matmul(PS[:, 2 * accs[m % len(accs)] + hf, 0:HALF], slot(d % 4, m),
                                       rhs[:, hf * HALF:(hf + 1) * HALF], start=True, stop=True)
                    mm.then_inc(S(L + "out_mm") if m < KC - 1 else S("unit_done"), 1)

            def attention(layer):
                L = "at_"
                base = UB[layer, "mix"]
                norm(norm_name(layer, "m"))
                pe.wait_ge(S("norm_h"), KC * (nth(norm_name(layer, "m")) + 1))
                ident = const("ident")
                def project(h, first, last, d):
                    for n in range(first, last):
                        k, c = n // KC, n % KC
                        s = (d + k) % 4
                        if c == 0:
                            if k == 0:
                                pe.wait_ge(S(L + "ev_v"), h + 1)
                            if k == 2:
                                pe.wait_ge(S(L + "ev_q"), h + 1)
                            loaded(s, h, base + d + k - s)
                        for hf in range(2):
                            mm = pe.matmul(PS[:, 2 * (k % 2) + hf, 0:HALF], slot(s, c), from_h(c, hf),
                                           start=c == 0, stop=c == KC - 1)
                        if c == KC - 1:
                            mm.then_inc(S("unit_done"), 1)

                def mix(h, more):
                    done = [0]

                    def ahead(n):
                        if more:
                            project(h + 1, done[0], done[0] + n, -1)
                            done[0] += n

                    def scores(qb):
                        keys = (qb + 1) * P
                        pe.wait_ge(S(L + "scored"), h * NCH + qb + 1)
                        for c in range(2):
                            mm = pe.matmul(PS[:, 4 + c, 0:keys], at_q[c * HD:(c + 1) * HD, qb * P:keys],
                                           at_k[c * HD:(c + 1) * HD, 0:keys], start=True, stop=True)
                        mm.then_inc(S(L + "score_mm"), 1)

                    ahead(1)
                    pe.wait_ge(S(L + "x"), h * KC + 1)
                    pe.wait_ge(S(L + "ev_k"), h + 1)
                    scores(0)
                    pe.wait_ge(S(L + "ev_v"), h + 1 + 1)
                    for c in range(NCH):
                        pe.transpose(PS[:, 6, c * P:(c + 1) * P], at_v[:, c * P:(c + 1) * P], ident)
                    pe.transpose(PS[0:NS_TOK, 7, 0:P], at_v[:, NP_TOK:NT], ident).then_inc(S(L + "vt_mm"), 1)
                    for qb in range(NCH):
                        n = h * NCH + qb
                        if qb < NCH - 1:
                            scores(qb + 1)
                        ahead(2 if qb == 0 else 3)
                        pe.wait_ge(S(L + "probs"), n + 1)
                        pe.wait_ge(S(L + "diag"), n + 1)
                        pe.wait_ge(S(L + "vt_ev"), h + 1)
                        for kb in range(qb + 1):
                            for c in range(2):
                                mm = pe.matmul(PS[:, 6, kb * P:(kb + 1) * P], at_p[qb % 2][c][:, kb * P:(kb + 1) * P],
                                               at_diag[qb % 2][c], start=c == 0, stop=c == 1)
                        mm.then_inc(S(L + "at_mm"), 1)
                        ahead(1)
                        pe.wait_ge(S(L + "at_ev"), n + 1)
                        pe.wait_ge(S(L + "o_ev"), h * (NCH + 1) + qb + 1)
                        for kb in range(qb + 1):
                            mm = pe.matmul(PS[:, 7, 0:P], at_vt[:, kb * P:(kb + 1) * P], at_at[:, kb * P:(kb + 1) * P],
                                           start=kb == 0, stop=kb == qb)
                        mm.then_inc(S(L + "o_mm"), 1)
                    pe.wait_ge(S(L + "kc_in"), (h + 1) * (16 * NB * PAGES))
                    pe.wait_ge(S(L + "scored"), (h + 1) * NCH + 1)
                    for c in range(2):
                        rows = slice(c * HD, (c + 1) * HD)
                        for b in range(NB):
                            for pg in range(PAGES):
                                k0 = (b * PAGES + pg) * P
                                o = pg * NS_TOK + b * TB
                                pe.matmul(PS[:, 4 + c, o:o + TB], at_kc[rows, k0:k0 + P],
                                          at_q[rows, NP_TOK + b * TB:NP_TOK + (b + 1) * TB], start=True, stop=True)
                        mm = pe.matmul(PS[0:NS_TOK, 4 + c, 64:64 + NS_TOK], at_k[rows, NP_TOK:NT],
                                       at_q[rows, NP_TOK:NT], start=True, stop=True)
                    mm.then_inc(S(L + "st_mm"), 1)
                    pe.wait_ge(S(L + "st_ev"), h + 1)
                    settle()
                    for pg in range(PAGES):
                        pe.transpose(PS[0:64, 5, pg * P:(pg + 1) * P], at_st[:, pg * 64:(pg + 1) * 64], ident)
                    pe.transpose(PS[0:64, 5, PAST:PAST + NS_TOK], at_stn[0:NS_TOK, :], ident[0:NS_TOK, 0:NS_TOK])\
                        .then_inc(S(L + "ss_mm"), 1)
                    ahead(3)
                    pe.wait_ge(S(L + "sprobs"), h + 1)
                    pe.wait_ge(S(L + "selc"), h + 1)
                    for pg in range(PAGES):
                        pe.matmul(PS[:, 6, pg * NS_TOK:(pg + 1) * NS_TOK], at_sp[0:64, pg * P:(pg + 1) * P],
                                  at_selc[0:64, :], start=True, stop=True)
                    pe.matmul(PS[0:NS_TOK, 6, 64:64 + NS_TOK], at_sp[0:64, PAST:PAST + NS_TOK],
                              at_selc[0:64, :], start=True, stop=True).then_inc(S(L + "sat_mm"), 1)
                    ahead(1)
                    pe.wait_ge(S(L + "sat_ev"), h + 1)
                    pe.wait_ge(S(L + "vc_in"), (h + 1) * (16 * NB * PAGES))
                    pe.wait_ge(S(L + "o_ev"), h * (NCH + 1) + NCH + 1)
                    pe.matmul(PS[:, 7, 0:NS_TOK], at_vts[0:NS_TOK, :], at_atn[0:NS_TOK, :], start=True, stop=False,
                              skip_group_check=True)
                    for b in range(NB):
                        for pg in range(PAGES):
                            k0 = (b * PAGES + pg) * P
                            o = pg * NS_TOK + b * TB
                            mm = pe.matmul(PS[:, 7, b * TB:(b + 1) * TB], at_vc[:, k0:k0 + P], at_att[:, o:o + TB],
                                           start=False, stop=b == NB - 1 and pg == PAGES - 1, skip_group_check=True)
                    mm.then_inc(S(L + "o_mm"), 1)
                    ahead(2)
                    pe.wait_ge(S(L + "osq"), h + 1)
                    for hf in range(2):
                        mm = pe.matmul(PS[:, 4 + hf, 0:HALF], const("ones"), at_sq[:, hf * HALF:(hf + 1) * HALF],
                                       start=True, stop=True)
                    mm.then_inc(S(L + "ossq"), 1)
                    ahead(2)
                    pe.wait_ge(S(L + "ob"), h + 1 + 1)
                    out_rows(L, h, base, at_ob, 6 if more else 3, (1, 2, 3))

                project(0, 0, 3 * KC, 0)
                with pe.Fori(0, HEADS - 1) as h:
                    mix(h, True)
                mix(HEADS - 1, False)

            def rwkv(layer):
                L = "rw_"
                base = UB[layer, "mix"]
                norm(norm_name(layer, "m"))
                for n, (lo, w, buf) in enumerate(((0, 64, rw_xk), (64, 64, rw_xv), (128, 128, rw_xk))):
                    pe.wait_ge(S(L + "xm"), n + 1)
                    if n == 0:
                        pe.wait_ge(S(L + "lw_in"), 16)
                    for c in range(KC):
                        for hf in range(2):
                            mm = pe.matmul(PS[0:w, 2 * n + hf, 0:HALF], rw_lw[:, c * 256 + lo:c * 256 + lo + w],
                                           buf[:, c * NT + hf * HALF:c * NT + (hf + 1) * HALF],
                                           start=c == 0, stop=c == KC - 1)
                    mm.then_inc(S(L + "lora_mm"), 1)
                pe.wait_ge(S(L + "hidden"), 3)
                pe.wait_ge(S(L + "xm"), 6)
                ident = const("ident")
                heads = (slice(0, HD), slice(HD, P))

                def rhs_of(buf):
                    return lambda c, hf: buf[:, c * NT + hf * HALF:c * NT + (hf + 1) * HALF]

                inputs = (H, rw_xk, rw_xv)
                before = ("ev_a", "ev_g", "ev_r")

                def project(h, first, last, d):
                    for n in range(first, last):
                        k, c = n // KC, n % KC
                        s = (d + k) % 4
                        if c == 0:
                            pe.wait_ge(S(L + before[k]), h + 1)
                            loaded(s, h, base + d + k - s)
                        for hf in range(2):
                            mm = pe.matmul(PS[:, 2 * (k % 2) + hf, 0:HALF], slot(s, c), rhs_of(inputs[k])(c, hf),
                                           start=c == 0, stop=c == KC - 1)
                        if c == KC - 1:
                            mm.then_inc(S("unit_done"), 1)

                def low_rank(h, n):
                    rows, hid, a, last = ((HD, rw_hw, 1, "ev_k"), (HD, rw_ha, 0, "ev_v"), (P, rw_hg, 1, "ev_w"))[n]
                    pe.wait_ge(S(L + last), h + 1)
                    pe.wait_ge(S(L + "ls_in"), h * 48 + 48)
                    for hf in range(2):
                        mm = pe.matmul(PS[:, 2 * a + hf, 0:HALF], rw_ls[0:rows, n * P:(n + 1) * P],
                                       hid[0:rows, hf * HALF:(hf + 1) * HALF], start=True, stop=True)
                    mm.then_inc(S(L + "lora2_mm"), 1)

                def mix(h, more):
                    done = [0]

                    def ahead(n):
                        if more:
                            project(h + 1, done[0], done[0] + n, -1)
                            done[0] += n

                    pe.wait_ge(S(L + "x"), h * KC + 1)
                    low_rank(h, 2)
                    pe.wait_ge(S(L + "kn_sq"), h + 1)
                    for hf in range(2):
                        mm = pe.matmul(PS[:, 4 + hf, 0:HALF], const("blocks"), rw_rn[:, hf * HALF:(hf + 1) * HALF],
                                       start=True, stop=True)
                    mm.then_inc(S(L + "kn_mm"), 1)
                    pe.wait_ge(S(L + "rk"), h + 1)
                    for hf in range(2):
                        mm = pe.matmul(PS[:, 6 + hf, 0:HALF], const("blocks"), rw_k[:, hf * HALF:(hf + 1) * HALF],
                                       start=True, stop=True)
                    mm.then_inc(S(L + "bonus_mm"), 1)
                    pe.wait_ge(S(L + "ops"), h + 1)
                    pe.wait_ge(S(L + "bonus"), h + 1)
                    settle()
                    for bank, src in enumerate((rw_v, rw_pp, rw_bc, rw_kn)):
                        for n in range(N2):
                            for hd in heads:
                                pe.matmul(PS[hd, 4 + bank, n * C2:(n + 1) * C2], src[hd, n * C2:(n + 1) * C2],
                                          ident[hd, hd], start=True, stop=True)
                        mm = pe.transpose(PS[0:NS_TOK, 0, bank * P:(bank + 1) * P], src[:, NP_TOK:NT], ident)
                    mm.then_inc(S(L + "tm_mm"), 1)
                    pe.wait_ge(S(L + "tm_ev"), h + 1)
                    settle()
                    pairs = ((rw_be, rw_pp), (rw_pp, rw_be), (rw_k2, rw_pp), (rw_be, rw_r), (rw_k2, rw_r))
                    for n_, (a, b) in enumerate(pairs):
                        bank = (4, 5, 6, 7, 0)[n_]
                        for n in range(N2):
                            cs = slice(n * C2, (n + 1) * C2)
                            for hd in heads:
                                pe.matmul(PS[hd, bank, cs], a[hd, cs], b[hd, cs], start=True, stop=True)
                        for i, hd in enumerate(heads):
                            o = n_ * NS_TOK
                            mm = pe.matmul(PS[0:NS_TOK, 1 + i, o:o + NS_TOK], a[hd, NP_TOK:NT], b[hd, NP_TOK:NT],
                                           start=True, stop=True)
                    mm.then_inc(S(L + "mat_mm"), 1)
                    for lv in range(1, 6):
                        pe.wait_ge(S(L + "inv"), h * 6 + lv)
                        settle()
                        for n in range(N2):
                            cs = slice(n * C2, (n + 1) * C2)
                            for hd in heads:
                                mm = pe.matmul(PS[hd, 4, cs], rw_ml[hd, cs], rw_x[hd, cs], start=True, stop=True)
                        if lv == 1:
                            for i in range(2):
                                ss = slice(i * NS_TOK, (i + 1) * NS_TOK)
                                mm = pe.matmul(PS[0:NS_TOK, 5, ss], rw_mls[0:NS_TOK, ss], rw_xs[0:NS_TOK, ss], start=True, stop=True)
                        mm.then_inc(S(L + "y_mm"), 1)
                        ahead(1)
                        pe.wait_ge(S(L + "y_ev"), h * 5 + lv)
                        settle()
                        for n in range(N2):
                            cs = slice(n * C2, (n + 1) * C2)
                            for hd in heads:
                                pe.matmul(PS[hd, 6, cs], rw_xt[hd, cs], rw_y[hd, cs], start=True, stop=True)
                                mm = pe.matmul(PS[hd, 7, cs], rw_y[hd, cs], rw_xt[hd, cs], start=True, stop=True)
                        if lv == 1:
                            for i in range(2):
                                ss = slice(i * NS_TOK, (i + 1) * NS_TOK)
                                s2 = slice(128 + i * NS_TOK, 128 + (i + 1) * NS_TOK)
                                s3 = slice(256 + i * NS_TOK, 256 + (i + 1) * NS_TOK)
                                pe.matmul(PS[0:NS_TOK, 5, s2], rw_xts[0:NS_TOK, ss], rw_ys[0:NS_TOK, ss], start=True, stop=True)
                                mm = pe.matmul(PS[0:NS_TOK, 5, s3], rw_ys[0:NS_TOK, ss], rw_xts[0:NS_TOK, ss], start=True, stop=True)
                        mm.then_inc(S(L + "xy_mm"), 1)
                        ahead(3)
                    pe.wait_ge(S(L + "inv"), h * 6 + 6)
                    settle()
                    for n in range(N2):
                        cs = slice(n * C2, (n + 1) * C2)
                        for hd in heads:
                            pe.matmul(PS[hd, 4, cs], rw_zkt[hd, cs], rw_vtm[hd, cs], start=True, stop=True)
                            pe.matmul(PS[hd, 5, cs], rw_ztm[hd, cs], rw_xt[hd, cs], start=True, stop=True)
                    for i, hd in enumerate(heads):
                        tm = slice(i * HD, (i + 1) * HD)
                        ss = slice(i * NS_TOK, (i + 1) * NS_TOK)
                        pe.matmul(PS[0:NS_TOK, 6, tm], rw_ms[0:NS_TOK, (4 + i) * NS_TOK:(5 + i) * NS_TOK],
                                  rw_tms[0:NS_TOK, tm], start=True, stop=True)
                        mm = pe.matmul(PS[hd, 7, 0:NS_TOK], rw_tms[0:NS_TOK, P + i * HD:P + (i + 1) * HD], rw_xts[0:NS_TOK, ss],
                                       start=True, stop=True)
                    mm.then_inc(S(L + "hw_mm"), 1)
                    ahead(1)
                    pe.wait_ge(S(L + "hw_ev"), h + 1)
                    settle()
                    for n in range(N2):
                        cs = slice(n * C2, (n + 1) * C2)
                        pe.wait_ge(S(L + "st"), h * N2 + n + 1)
                        settle()
                        for hd in heads:
                            pe.matmul(PS[hd, 4 + n % 2, 0:HD], rw_xt[hd, cs], rw_hv[hd, cs], start=True, stop=False)
                            mm = pe.matmul(PS[hd, 4 + n % 2, 0:HD], rw_wt[hd, cs], rw_st[hd, n * HD:(n + 1) * HD],
                                           start=False, stop=True)
                        mm.then_inc(S(L + "u_mm"), 1)
                        if n < 2:
                            ahead(1)
                        pe.wait_ge(S(L + "nu"), h * N2 + n + 1)
                        settle()
                        for hd in heads:
                            pe.matmul(PS[hd, 6 + n % 2, 0:HD], rw_kptm[hd, cs], rw_vtm[hd, cs], start=True, stop=False)
                            mm = pe.matmul(PS[hd, 6 + n % 2, 0:HD], rw_bptm[hd, cs], rw_nu[hd, cs], start=False, stop=True)
                        mm.then_inc(S(L + "ds_mm"), 1)
                        if n == 0:
                            ahead(1)
                        if more and n in (2, 3):
                            low_rank(h + 1, n - 2)
                    if more:
                        pe.wait_ge(S(L + "ev_w"), h + 2)
                        pe.wait_ge(S(L + "ev_a"), h + 2 + 1)
                        settle()
                    for n in range(N2):
                        cs = slice(n * C2, (n + 1) * C2)
                        for hd in heads:
                            pe.matmul(PS[hd, 0, cs], rw_st[hd, n * HD:(n + 1) * HD], rw_r[hd, cs], start=True, stop=False)
                            pe.matmul(PS[hd, 0, cs], rw_vtm[hd, cs], rw_rkt[hd, cs], start=False, stop=False)
                            pe.matmul(PS[hd, 0, cs], rw_nu[hd, cs], rw_rbt[hd, cs], start=False, stop=True)
                    pe.wait_ge(S(L + "s0_in"), h * 16 + 16)
                    pe.wait_ge(S(L + "nu"), (h + 1) * N2)
                    settle()
                    for i, hd in enumerate(heads):
                        ss = slice(i * NS_TOK, (i + 1) * NS_TOK)
                        pe.matmul(PS[hd, 4, 0:NS_TOK], rw_hvs[0:NS_TOK, i * HD:(i + 1) * HD], rw_xts[0:NS_TOK, ss],
                                  start=True, stop=True)
                    for b in range(NB):
                        for hd in heads:
                            mm = pe.matmul(PS[hd, 5, b * TB:(b + 1) * TB], rw_st0[hd, b * HD:(b + 1) * HD],
                                           rw_wts[hd, b * TB:(b + 1) * TB], start=True, stop=True)
                    mm.then_inc(S(L + "us_mm"), 1)
                    pe.wait_ge(S(L + "us_ev"), h + 1)
                    settle()
                    for n in range(2):
                        mm = pe.matmul(PS[0:NS_TOK, 5, 0:P], rw_ufm[:, n * NS_TOK:(n + 1) * NS_TOK], ident, start=n == 0, stop=n == 1)
                    mm.then_inc(S(L + "ut_mm"), 1)
                    pe.wait_ge(S(L + "ut_ev"), h + 1)
                    for i, hd in enumerate(heads):
                        tm = slice(i * HD, (i + 1) * HD)
                        rk = slice((8 + i) * NS_TOK, (9 + i) * NS_TOK)
                        rb = slice((6 + i) * NS_TOK, (7 + i) * NS_TOK)
                        pe.matmul(PS[hd, 1, 0:NS_TOK], rw_tms[0:NS_TOK, tm], rw_ms[0:NS_TOK, rk], start=True, stop=False,
                                  skip_group_check=True)
                        pe.matmul(PS[hd, 1, 0:NS_TOK], rw_nutm[0:NS_TOK, tm], rw_ms[0:NS_TOK, rb], start=False, stop=True,
                                  skip_group_check=True)
                    for b in range(NB):
                        for hd in heads:
                            mm = pe.matmul(PS[hd, 2, b * TB:(b + 1) * TB], rw_st0[hd, b * HD:(b + 1) * HD],
                                           rw_r[hd, NP_TOK + b * TB:NP_TOK + (b + 1) * TB], start=True, stop=True)
                    mm.then_inc(S(L + "o_mm"), 1)
                    pe.wait_ge(S(L + "nux"), h + 1)
                    pe.wait_ge(S(L + "st"), (h + 1) * N2 + 1)
                    for i, hd in enumerate(heads):
                        vx = rw_vxs[0:NS_TOK, :].rearrange("p (b v) -> p b v", b=NB)[:, :, i * HD:(i + 1) * HD]
                        nx = rw_nux[0:NS_TOK, :].rearrange("p (b v) -> p b v", b=NB)[:, :, i * HD:(i + 1) * HD]
                        ps = PS[hd, 6, :].rearrange("p (b v) -> p b v", b=NB)
                        pe.matmul(ps, rw_tms[0:NS_TOK, 2 * P + i * HD:2 * P + (i + 1) * HD], vx, start=True, stop=False)
                        mm = pe.matmul(ps, rw_tms[0:NS_TOK, 3 * P + i * HD:3 * P + (i + 1) * HD], nx, start=False, stop=True)
                    mm.then_inc(S(L + "dss_mm"), 1)
                    pe.wait_ge(S(L + "o_sum"), h + 1)
                    for hf in range(2):
                        mm = pe.matmul(PS[:, 4 + hf, 0:HALF], const("blocks"), rw_o[:, hf * HALF:(hf + 1) * HALF],
                                       start=True, stop=True)
                    mm.then_inc(S(L + "mu_mm"), 1)
                    pe.wait_ge(S(L + "oc_sq"), h + 1)
                    for hf in range(2):
                        mm = pe.matmul(PS[:, 4 + hf, 0:HALF], const("blocks"), rw_o[:, hf * HALF:(hf + 1) * HALF],
                                       start=True, stop=True)
                    mm.then_inc(S(L + "var_mm"), 1)
                    pe.wait_ge(S(L + "ob"), h + 1 + 1)
                    pe.wait_ge(S(L + "state"), h + 1)
                    out_rows(L, h, base, rw_oc, 6 if more else 3, (0, 1, 2, 3))

                project(0, 0, 3 * KC, 0)
                low_rank(0, 0)
                low_rank(0, 1)
                with pe.Fori(0, HEADS - 1) as h:
                    mix(h, True)
                mix(HEADS - 1, False)

            pe.wait_ge(S("consts_in"), 16 * NCONST_LOADS)
            for layer in range(depth):
                (hgrn, attention, rwkv)[layer % 3](layer)
                feed_forward(layer)
            norm("nfin")

        @block.scalar
        def _(act):
            act.dma_start(hg_mask, T["mask"]).then_inc(S("consts_in"), 16)

            def norm(name, src, ready, count):
                act.wait_ge(S(ready), count)
                for c in range(KC):
                    act.activation(h3[:, c, :], src[:, c, :], ACT.Square).then_inc(S("norm_sq"), 1)
                act.wait_ge(S("norm_ssq"), nth(name) + 1)
                act.activation(halves(rstd[:, :]), acc(0), ACT.Sqrt, scale=1.0 / D, bias=scratch[:, 0:1])\
                   .then_inc(S("norm_rms"), 1)

            def done(ubase, i, k):
                act.wait_ge(S("unit_done"), i * 4 + (ubase + k + 1))

            def feed_forward(layer, ready, count):
                act.wait_ge(S(ready), count)
                if layer % 3 == 2:
                    act.wait_ge(S("rw_st_free"), HEADS + 1)
                base = UB[layer, "ff"]

                def split(i, n, width):
                    k = (base + n) % 4
                    act.wait_ge(S(f"slot_in{k}"), i * 16 + (16 * ((base + n) // 4 + 1)))
                    act.activation(wh[n % 2][:, 0:width], ring[:, k * SLOT:k * SLOT + width], ACT.Copy)\
                       .then_inc(S("ff_wh"), 1)

                split(0, 0, D)
                split(0, 1, D)
                norm(norm_name(layer, "f"), x3, ready, count)
                for c in range(KC):
                    act.wait_ge(S("norm_h"), KC * nth(norm_name(layer, "f")) + c + 1)
                    act.activation(hh[:, c * NT:(c + 1) * NT], h3[:, c, :], ACT.Copy).then_inc(S("ff_hh"), 1)
                for s in range(2):
                    block0 = FC * layer + FU * s

                    def up(i, par, width):
                        n = HU * s + 2 * par
                        done(base, i, n)
                        split(i, n + 2, width)
                        act.activation(halves(ff_gate[par]), acc(2 * ((s + par) % 2)), ACT.Silu).then_inc(S("ff_silu"), 1)
                        done(base, i, n + 1)
                        split(i, n + 3, width)
                        act.wait_ge(S("ff_glu"), i * 2 + (par + block0) + 1 + CREDITS["ff_glu"])
                        act.activation(ff_ah[:, bass.ds((i * 2 + par) * NT, NT)], ff_gate[par], ACT.Copy).then_inc(S("ff_ah"), 1)

                    with act.Fori(0, FU // 2) as i:
                        for par in range(2):
                            up(i, par, D)
                    up(FU // 2, 0, SLOT)
                    n0 = HU * s + 2 * FU
                    for m in range(KC):
                        if m < KC - 2 or s == 0:
                            done(base, 0, n0 + m)
                            split(0, n0 + m + 2, SLOT if m < KC - 2 else D)

            def hgrn(layer, ready, count):
                L = "hg_"
                j = layer // 3
                base = UB[layer, "mix"] - 4 * HEADS * j
                act.wait_ge(S(ready), count)

                def split(h, n):
                    k = n % 4
                    act.wait_ge(S(f"slot_in{k}"), h * 16 + (16 * ((base + n) // 4 + 1)))
                    act.activation(wh[n % 2][:, 0:D], ring[:, k * SLOT:k * SLOT + D], ACT.Copy).then_inc(S(L + "wh"), 1)

                def input_split(name):
                    for c in range(KC):
                        act.wait_ge(S("norm_h"), KC * nth(name) + c + 1)
                        act.activation(hh[:, c * NT:(c + 1) * NT], h3[:, c, :], ACT.Copy).then_inc(S(L + "hh"), 1)

                split(j * HEADS, 0)
                split(j * HEADS, 1)
                norm(norm_name(layer, "m"), x3, ready, count)
                input_split(norm_name(layer, "m"))

                def raw(h, k):
                    done(base, h, k)
                    split(h, k + 2)
                    if k == 0:
                        act.wait_ge(S(L + "raw_used"), h + 1)
                        act.activation(halves(hg_sgp), acc(0), ACT.Sigmoid)
                        act.activation(halves(hg_sgn), acc(0), ACT.Sigmoid, scale=-1.0).then_inc(S(L + "ev_f"), 1)
                    if k == 1:
                        act.activation(halves(hg_qs), acc(1), ACT.Sigmoid)
                        act.activation(halves(hg_qr), acc(1), ACT.Copy).then_inc(S(L + "ev_q"), 1)
                    if k == 2:
                        act.wait_ge(S(L + "vt_mm"), h + 1)
                        act.activation(halves(hg_v), acc(0), ACT.Copy).then_inc(S(L + "ev_v"), 1)
                    if k == 3:
                        act.wait_ge(S(L + "out"), h + 1)
                        act.activation(halves(hg_gs), acc(1), ACT.Sigmoid).then_inc(S(L + "ev_g"), 1)

                def mix(h, more):
                    act.wait_ge(S(L + "vt_mm"), h + 1 + 1)
                    act.activation(hg_vt, PS[:, 6, :], ACT.Copy)
                    act.activation(hg_vts[0:NS_TOK, :], PS[0:NS_TOK, 7, 0:P], ACT.Copy).then_inc(S(L + "vt_ev"), 1)
                    if more:
                        raw(h + 1, 0)
                        raw(h + 1, 1)
                    act.wait_ge(S(L + "kt_mm"), h + 1)
                    act.activation(hg_kt, PS[:, 6, :], ACT.Copy)
                    act.activation(hg_kts[0:NS_TOK, :], PS[0:NS_TOK, 7, 0:P], ACT.Copy).then_inc(S(L + "kt_ev"), 1)
                    if more:
                        raw(h + 1, 2)
                        raw(h + 1, 3)

                for k in range(4):
                    raw(j * HEADS, k)
                with act.Fori(j * HEADS, (j + 1) * HEADS - 1) as h:
                    mix(h, True)
                mix((j + 1) * HEADS - 1, False)
                norm(norm_name(layer, "o"), o3, L + "out", HEADS * (j + 1) + 1)
                input_split(norm_name(layer, "o"))
                for m in range(KC - 2):
                    act.wait_ge(S("unit_done"), UB[layer, "out"] + m + 1)
                    split((j + 1) * HEADS, m + 2)

            def attention(layer, ready, count):
                L = "at_"
                base = UB[layer, "mix"]
                act.wait_ge(S(L + "lam_sum"), 1)
                act.activation(c_lam[:, 2:4], c_lam[:, 0:2], ACT.Exp).then_inc(S(L + "lam_exp"), 1)
                norm(norm_name(layer, "m"), x3, ready, count)

                def raw(h, k, d):
                    if k == 0:
                        act.wait_ge(S(L + "kv_free"), h + 1)
                    act.wait_ge(S("unit_done"), h * 4 + (base + d + k + 1))
                    if k == 0:
                        act.activation(halves(at_q), acc(0), ACT.Copy, scale=HD ** -0.5).then_inc(S(L + "ev_q"), 1)
                    if k == 1:
                        act.activation(halves(at_k), acc(1), ACT.Copy).then_inc(S(L + "ev_k"), 1)
                    if k == 2:
                        act.activation(halves(at_v), acc(0), ACT.Copy).then_inc(S(L + "ev_v"), 1)

                def mix(h, more):
                    act.wait_ge(S(L + "vt_mm"), h + 1)
                    act.activation(at_vt, PS[:, 6, :], ACT.Copy)
                    act.activation(at_vts[0:NS_TOK, :], PS[0:NS_TOK, 7, 0:P], ACT.Copy).then_inc(S(L + "vt_ev"), 1)

                    def probs(qb):
                        keys = (qb + 1) * P
                        act.wait_ge(S(L + "maxed"), h * NCH + qb + 1)
                        for c in range(2):
                            last = act.activation(at_p[qb % 2][c][:, 0:keys], at_sb[qb % 2][c][:, 0:keys], ACT.Exp,
                                                  bias=c_nm[qb % 2][:, c:c + 1], accum_out=c_ls[qb % 2][:, c:c + 1])
                        last.then_inc(S(L + "probs"), 1)

                    probs(0)
                    for qb in range(NCH):
                        keys = (qb + 1) * P
                        if qb < NCH - 1:
                            probs(qb + 1)
                        act.wait_ge(S(L + "at_mm"), h * NCH + qb + 1)
                        act.activation(at_at[:, 0:keys], PS[:, 6, 0:keys], ACT.Copy).then_inc(S(L + "at_ev"), 1)
                    act.wait_ge(S(L + "st_mm"), h + 1 + 1)
                    for pg in range(PAGES):
                        act.activation(at_st[:, pg * 64:(pg + 1) * 64].rearrange("p (c t) -> p c t", c=2),
                                       PS[:, 4:6, pg * NS_TOK:(pg + 1) * NS_TOK], ACT.Copy)
                    act.activation(at_stn[0:NS_TOK, :].rearrange("p (c t) -> p c t", c=2),
                                   PS[0:NS_TOK, 4:6, 64:64 + NS_TOK], ACT.Copy).then_inc(S(L + "st_ev"), 1)
                    if more:
                        raw(h + 1, 0, -1)
                        raw(h + 1, 1, -1)
                    act.wait_ge(S(L + "smaxed"), h + 1)
                    act.activation(at_sp[0:64, :], at_ss[0:64, :], ACT.Exp, bias=c_snm[0:64, :],
                                   accum_out=c_sls[0:64, :]).then_inc(S(L + "sprobs"), 1)
                    act.wait_ge(S(L + "sat_mm"), h + 1)
                    act.activation(at_att, PS[:, 6, 0:64], ACT.Copy)
                    act.activation(at_atn[0:NS_TOK, :], PS[0:NS_TOK, 6, 64:96], ACT.Copy).then_inc(S(L + "sat_ev"), 1)
                    act.wait_ge(S(L + "o_ev"), (h + 1) * (NCH + 1) + 1)
                    act.activation(at_sq, at_o, ACT.Square).then_inc(S(L + "osq"), 1)
                    act.wait_ge(S(L + "ossq"), h + 1)
                    act.activation(halves(at_rs), acc(2), ACT.Sqrt, scale=1.0 / P, bias=c_sub).then_inc(S(L + "orms"), 1)
                    if more:
                        raw(h + 1, 2, -1)

                for k in range(3):
                    raw(0, k, 0)
                with act.Fori(0, HEADS - 1) as h:
                    mix(h, True)
                mix(HEADS - 1, False)

            def rwkv(layer, ready, count):
                L = "rw_"
                base = UB[layer, "mix"]
                norm(norm_name(layer, "m"), x3, ready, count)
                act.wait_ge(S(L + "lora_mm"), 1)
                act.activation(halves(rw_hw[0:HD, :]), PS[0:HD, 0:2, 0:HALF], ACT.Tanh).then_inc(S(L + "hidden"), 1)
                act.wait_ge(S(L + "lora_mm"), 2)
                act.activation(halves(rw_ha[0:HD, :]), PS[0:HD, 2:4, 0:HALF], ACT.Copy).then_inc(S(L + "hidden"), 1)
                act.wait_ge(S(L + "lora_mm"), 3)
                act.activation(halves(rw_hg), acc(2), ACT.Sigmoid).then_inc(S(L + "hidden"), 1)

                def raw(h, k, d):
                    if k < 3:
                        act.wait_ge(S("unit_done"), h * 4 + (base + d + k + 1))
                        act.activation(halves((rw_rr, rw_k, rw_v)[k]), acc(k % 2), ACT.Copy)\
                            .then_inc(S(L + ("ev_r", "ev_k", "ev_v")[k]), 1)
                    if k == 3:
                        act.wait_ge(S(L + "cur"), h + 1)
                        act.wait_ge(S(L + "lora2_mm"), h * 3 + 1)
                        act.activation(halves(rw_sg), acc(1), ACT.Sigmoid, bias=c_w0).then_inc(S(L + "ev_w"), 1)
                    if k == 4:
                        act.wait_ge(S(L + "lora2_mm"), h * 3 + 2)
                        act.activation(halves(rw_a), acc(0), ACT.Sigmoid, bias=c_a0).then_inc(S(L + "ev_a"), 1)

                def mix(h, more):
                    act.wait_ge(S(L + "ob"), h + 1)
                    act.wait_ge(S(L + "lora2_mm"), h * 3 + 3)
                    act.activation(halves(rw_g), acc(1), ACT.Copy).then_inc(S(L + "ev_g"), 1)
                    act.wait_ge(S(L + "bc"), h + 1)
                    act.activation(rw_p, rw_bc, ACT.Exp, scale=-KAPPA)
                    act.activation(rw_pi, rw_bc, ACT.Exp, scale=KAPPA)
                    act.drain()
                    act.activation(rw_pp, rw_pp, ACT.Exp, scale=-KAPPA).then_inc(S(L + "exps"), 1)
                    act.wait_ge(S(L + "kn"), h + 1)
                    act.activation(rw_rn, rw_kn, ACT.Square).then_inc(S(L + "kn_sq"), 1)
                    act.wait_ge(S(L + "kn_mm"), h + 1)
                    act.activation(halves(rw_rn), acc(2), ACT.Sqrt).then_inc(S(L + "kn_rt"), 1)
                    act.wait_ge(S(L + "tm_mm"), h + 1)
                    act.activation(rw_vtm, PS[:, 4, :], ACT.Copy)
                    act.activation(rw_ztm, PS[:, 5, :], ACT.Copy)
                    act.activation(rw_kptm, PS[:, 6, :], ACT.Copy)
                    act.activation(rw_bptm, PS[:, 7, :], ACT.Copy)
                    act.activation(rw_tms[0:NS_TOK, :], PS[0:NS_TOK, 0, :], ACT.Copy).then_inc(S(L + "tm_ev"), 1)
                    for lv in range(1, 6):
                        act.wait_ge(S(L + "y_mm"), h * 5 + lv)
                        y = act.activation(rw_y, PS[:, 4, :], ACT.Copy)
                        if lv == 1:
                            y = act.activation(rw_ys[0:NS_TOK, :], PS[0:NS_TOK, 5, 0:2 * NS_TOK], ACT.Copy)
                        y.then_inc(S(L + "y_ev"), 1)
                        if more and lv in (2, 4):
                            raw(h + 1, lv // 2 - 1, -1)
                    act.wait_ge(S(L + "hw_mm"), h + 1)
                    act.activation(rw_hv, PS[:, 4, :], ACT.Copy)
                    act.activation(rw_wt, PS[:, 5, :], ACT.Copy)
                    act.activation(rw_hvs[0:NS_TOK, :], PS[0:NS_TOK, 6, 0:P], ACT.Copy)
                    act.activation(rw_wts, PS[:, 7, 0:NS_TOK], ACT.Copy).then_inc(S(L + "hw_ev"), 1)
                    for n in range(N2):
                        act.wait_ge(S(L + "u_mm"), h * N2 + n + 1)
                        act.activation(rw_nu[:, n * C2:(n + 1) * C2], PS[:, 4 + n % 2, 0:HD], ACT.Copy, scale=-1.0)\
                            .then_inc(S(L + "nu"), 1)
                        if more and n in (1, 2, 3):
                            raw(h + 1, n + 1, -1)
                    act.wait_ge(S(L + "us_mm"), h + 1)
                    act.activation(rw_ufm.rearrange("p (n t) -> p n t", n=2), PS[:, 4:6, 0:NS_TOK], ACT.Copy)\
                        .then_inc(S(L + "us_ev"), 1)
                    act.wait_ge(S(L + "ut_mm"), h + 1)
                    act.activation(rw_nutm[0:NS_TOK, :], PS[0:NS_TOK, 5, 0:P], ACT.Copy, scale=-1.0).then_inc(S(L + "ut_ev"), 1)
                    act.wait_ge(S(L + "o_mm"), h + 1)
                    act.activation(rw_o[:, 0:NP_TOK], PS[:, 0, :], ACT.Copy)
                    act.activation(rw_o[:, NP_TOK:NT], PS[:, 1, 0:NS_TOK], ACT.Copy).then_inc(S(L + "o_ev"), 1)
                    act.wait_ge(S(L + "oc"), h + 1)
                    act.activation(rw_o, rw_oc, ACT.Square).then_inc(S(L + "oc_sq"), 1)
                    act.wait_ge(S(L + "var_mm"), h + 1)
                    act.activation(halves(rw_rn), acc(2), ACT.Sqrt, scale=1.0 / HD, bias=c_gn).then_inc(S(L + "gn_rt"), 1)

                for k in range(5):
                    raw(0, k, 0)
                with act.Fori(0, HEADS - 1) as h:
                    mix(h, True)
                mix(HEADS - 1, False)

            act.wait_ge(S("setup"), 1)
            act.wait_ge(S("lb_sub"), 1)
            act.activation(lbs[:, :], lbs[:, :], ACT.Exp).then_inc(S("lb_exp"), 1)
            ready, count = "consts_in", 16 * NCONST_LOADS
            for layer in range(depth):
                (hgrn, attention, rwkv)[layer % 3](layer, ready, count)
                ready, count = (("hg_x", KC * (layer // 3 + 1) + CREDITS["hg_x"]), ("at_x", KC * HEADS + 1), ("rw_x", KC * HEADS + 1))[layer % 3]
                feed_forward(layer, ready, count)
                ready, count = "ff_x", 2 * KC * (layer + 1) + CREDITS["ff_x"]
            norm("nfin", x3, ready, count)

        @block.vector
        def _(dve):
            def norm(name, src, gain):
                dve.wait_ge(S("norm_rms"), nth(name) + 1)
                dve.reciprocal(rstd[:, :], rstd[:, :])
                dve.drain()
                for c in range(KC):
                    dve.scalar_tensor_tensor(h3[:, c, :], src[:, c, :], vec3[:, gain, c:c + 1], rstd[:, :],
                                             ALU.mult, ALU.mult).then_inc(S("norm_h"), 1)

            def input_rest(L, count):
                for c in range(KC):
                    cs = slice(c * NT, (c + 1) * NT)
                    dve.wait_ge(S(L + "hh"), count + c + 1)
                    dve.tensor_tensor(hl[:, cs], H[:, cs], hh[:, cs].bitcast(F32), ALU.subtract)\
                       .then_inc(S(L + "hl"), 1)

            def feed_forward(layer):
                base, unit0 = UB[layer, "ff"], 2 * HU * layer

                def rest(i, n, width):
                    k = (base + n) % 4
                    dve.wait_ge(S("ff_wh"), i * 4 + (unit0 + n + 1))
                    dve.tensor_tensor(wl[n % 2][:, 0:width], ring[:, k * SLOT:k * SLOT + width],
                                      wh[n % 2][:, 0:width].bitcast(F32), ALU.subtract).then_inc(S("ff_wl"), 1)

                rest(0, 0, D)
                rest(0, 1, D)
                norm(norm_name(layer, "f"), x3, V_FFN + layer)
                input_rest("ff_", KC * layer)
                for s in range(2):
                    block0 = FC * layer + FU * s

                    def up(i, par, width):
                        n = HU * s + 2 * par
                        rest(i, n + 2, width)
                        dve.wait_ge(S("ff_silu"), i * 2 + (par + 1 + block0))
                        dve.wait_ge(S("unit_done"), i * 4 + (base + n + 2))
                        dve.tensor_tensor(halves(ff_gate[par]), halves(ff_gate[par]), acc(2 * ((s + par) % 2) + 1),
                                          ALU.mult).then_inc(S("ff_glu"), 1)
                        rest(i, n + 3, width)
                        dve.wait_ge(S("ff_ah"), i * 2 + (par + 1 + block0))
                        at = bass.ds((i * 2 + par) * NT, NT)
                        dve.tensor_tensor(ff_al[:, at], ff_gate[par], ff_ah[:, at].bitcast(F32), ALU.subtract)\
                           .then_inc(S("ff_al"), 1)

                    with dve.Fori(0, FU // 2) as i:
                        for par in range(2):
                            up(i, par, D)
                    up(FU // 2, 0, SLOT)
                    n0 = HU * s + 2 * FU
                    for m in range(KC):
                        if m < KC - 2 or s == 0:
                            rest(0, n0 + m + 2, SLOT if m < KC - 2 else D)
                        dve.wait_ge(S("unit_done"), base + n0 + m + 1)
                        xm = halves(X[:, m * NT:(m + 1) * NT])
                        dve.tensor_tensor(xm, xm, acc(m % 2), ALU.add).then_inc(S("ff_x"), 1)

            def hgrn(layer):
                L = "hg_"
                j = layer // 3

                def rest(h, n):
                    k = n % 4
                    dve.wait_ge(S(L + "wh"), h * 4 + (KC * j + n + 1))
                    dve.tensor_tensor(wl[n % 2][:, 0:D], ring[:, k * SLOT:k * SLOT + D],
                                      wh[n % 2][:, 0:D].bitcast(F32), ALU.subtract).then_inc(S(L + "wl"), 1)

                rest(j * HEADS, 0)
                rest(j * HEADS, 1)
                norm(norm_name(layer, "m"), x3, V_MIX + layer)
                input_rest(L, 2 * KC * j)
                for n in range(2, 5):
                    rest(j * HEADS, n)
                dve.memset(hg_at, 0.0)
                dve.memset(hg_ats, 0.0)
                lb = lbs[:, layer * KC:(layer + 1) * KC]
                oml = lbt[:, 0:KC]
                dve.tensor_scalar(oml, lb, -1.0, 1.0, ALU.mult, ALU.add)
                dve.drain()

                def mix(h, more):
                    dve.tensor_copy(scratch[:, 1:2], lbt[:, bass.ds(h - j * HEADS, 1)])
                    dve.tensor_copy(scratch[:, 3:4], lbs[:, bass.ds(h + (layer - j) * KC, 1)])
                    dve.drain()
                    dve.wait_ge(S(L + "ev_f"), h + 1)
                    dve.wait_ge(S(L + "ev_q"), h + 1)
                    dve.tensor_scalar(hg_f, hg_sgp, scratch[:, 1:2], scratch[:, 3:4], ALU.mult, ALU.add)
                    dve.tensor_scalar(hg_ks, hg_sgn, scratch[:, 1:2], None, ALU.mult)
                    dve.tensor_tensor(hg_q, hg_qs, hg_qr, ALU.mult).then_inc(S(L + "raw_used"), 1)
                    dve.drain()
                    dve.tensor_scalar(hg_f, hg_f, F_MIN, None, ALU.max).then_inc(S(L + "lvl"), 1)
                    dve.wait_ge(S(L + "vt_ev"), h + 1)
                    dve.tensor_tensor(
                        hg_vx[0:NS_TOK, :].rearrange("p (b v) -> p b v", b=NB),
                        hg_vts[0:NS_TOK, :].unsqueeze(1).to_broadcast([NS_TOK, NB, P]),
                        const("bmask", NS_TOK).unsqueeze(2).to_broadcast([NS_TOK, NB, P]),
                        ALU.mult).then_inc(S(L + "vx"), 1)
                    dprev, doff = hg_f, 0
                    for n in range(LEVELS):
                        dve.drain()
                        dve.wait_ge(S(L + "lvl_mm"), h * LEVELS + n + 1)
                        if n == 0:
                            dve.tensor_tensor(hg_qp, hg_q, hg_f, ALU.mult).then_inc(S(L + "lvl"), 1)
                        else:
                            size = NT if n <= 2 else NP_TOK
                            blk = 1 << (n - 1)
                            m = size // (2 * blk)
                            qv = hg_qp[:, 0:size].rearrange("p (m a b) -> p m a b", a=2, b=blk)
                            kv = hg_ks[:, 0:size].rearrange("p (m a b) -> p m a b", a=2, b=blk)
                            dv = dprev[:, 0:size // blk].rearrange("p (m a) -> p m a", a=2)
                            if n < LEVELS - 1 or True:
                                dn = hg_d[:, doff:doff + m]
                                doff += m
                                dve.tensor_tensor(dn, dv[:, :, 0], dv[:, :, 1], ALU.mult)
                            dve.tensor_tensor(qv[:, :, 1, :], qv[:, :, 1, :],
                                              dv[:, :, 0:1].to_broadcast([P, m, blk]), ALU.mult)
                            dve.tensor_tensor(kv[:, :, 0, :], kv[:, :, 0, :],
                                              dv[:, :, 1:2].to_broadcast([P, m, blk]), ALU.mult).then_inc(S(L + "lvl"), 1)
                            if n == 2:
                                ds_ = dn[:, NP_TOK // 4:NT // 4]
                            dprev = dn
                        if n <= 2:
                            dve.copy_predicated(hg_ats[0:NS_TOK, :], hg_mask[0:NS_TOK, n * P:n * P + NS_TOK],
                                                PS[0:NS_TOK, 7 - n % 2, 0:NS_TOK])
                        cp = dve.copy_predicated(
                            hg_at.rearrange("p (c t) -> p c t", c=NCH),
                            hg_mask[:, n * P:(n + 1) * P].unsqueeze(1).to_broadcast([P, NCH, P]),
                            PS[:, 4 + n % 2, :].rearrange("p (c t) -> p c t", c=NCH))
                        if n == LEVELS - 1:
                            cp.then_inc(S(L + "at"), 1)
                        if n == 0 or more and n in (3, 6):
                            rest(h + 1, 1 + n // 3)
                    dve.wait_ge(S(L + "kv_mm"), h + 1)
                    dve.wait_ge(S(L + "st_free"), h + 1)
                    st = dve.tensor_copy(hg_s[:, 0:P], PS[:, 5, 0:P])
                    for c in range(1, NCH):
                        dve.drain()
                        st = dve.scalar_tensor_tensor(hg_s[:, c * P:(c + 1) * P], hg_s[:, (c - 1) * P:c * P],
                                                      dprev[:, c:c + 1], PS[:, 5, c * P:(c + 1) * P], ALU.mult, ALU.add)
                    st.then_inc(S(L + "s"), 1)
                    dve.wait_ge(S(L + "ev_g"), h + 1 + 1)
                    dve.wait_ge(S(L + "o_mm"), h + 1)
                    dve.tensor_tensor(O[:, bass.ds((h - j * HEADS) * NT, NP_TOK)], PS[:, 4, :], hg_gs[:, 0:NP_TOK], ALU.mult)
                    dve.tensor_tensor(O[:, bass.ds((h - j * HEADS) * NT + NP_TOK, NS_TOK)], PS[:, 5, 0:NS_TOK],
                                      hg_gs[:, NP_TOK:NT], ALU.mult).then_inc(S(L + "out"), 1)
                    for b in range(NB):
                        bs = slice(b * P, (b + 1) * P)
                        st = dve.scalar_tensor_tensor(hg_s0[:, bs], hg_s0[:, bs], ds_[:, b:b + 1],
                                                      PS[:, 6 + b // 4, (b % 4) * P:(b % 4 + 1) * P], ALU.mult, ALU.add)
                    st.then_inc(S(L + "state"), 1)
                    if more:
                        rest(h + 1, 4)

                with dve.Fori(j * HEADS, (j + 1) * HEADS - 1) as h:
                    mix(h, True)
                mix((j + 1) * HEADS - 1, False)
                norm(norm_name(layer, "o"), o3, V_HG + layer // 3)
                input_rest(L, 2 * KC * j + KC)
                dve.wait_ge(S(L + "st_free"), HEADS * (j + 1) + 1)
                base = UB[layer, "out"]
                for m in range(KC):
                    if m < KC - 2:
                        rest((j + 1) * HEADS, m + 2)
                    dve.wait_ge(S("unit_done"), base + m + 1)
                    xm = halves(X[:, m * NT:(m + 1) * NT])
                    dve.tensor_tensor(xm, xm, acc(m % 4), ALU.add).then_inc(S(L + "x"), 1)

            def add_rows(L, h, base, d, accs):
                for m in range(KC):
                    if m < KC - 1:
                        dve.wait_ge(S(L + "out_mm"), h * (KC - 1) + m + 1)
                    else:
                        dve.wait_ge(S("unit_done"), h * 4 + (base + d + 1))
                    xm = halves(X[:, m * NT:(m + 1) * NT])
                    dve.tensor_tensor(xm, xm, acc(accs[m % len(accs)]), ALU.add).then_inc(S(L + "x"), 1)

            def attention(layer):
                L = "at_"
                base = UB[layer, "mix"]
                lv = lamv[:, :].rearrange("p (n e) -> p n e", n=4)
                for n in range(2):
                    dve.tensor_tensor(lv[:, 2 * n, :], lv[:, 2 * n, :], lv[:, 2 * n + 1, :], ALU.mult)
                dve.drain()
                dve.reduce_sum(c_lam[:, 0:1], lv[:, 0, :], AX.X)
                dve.reduce_sum(c_lam[:, 1:2], lv[:, 2, :], AX.X).then_inc(S(L + "lam_sum"), 1)
                dve.memset(c_sub, SUBLN_EPS)
                dve.tensor_scalar(c_gain, subln[:, :], 1.0 - LAM_INIT, None, ALU.mult)
                dve.wait_ge(S(L + "lam_exp"), 1)
                dve.tensor_tensor(c_nlam, c_lam[:, 3:4], c_lam[:, 2:3], ALU.subtract)
                dve.drain()
                dve.tensor_scalar(c_nlam, c_nlam, -LAM_INIT, None, ALU.add)
                dve.memset(c_sign, 1.0)
                dve.drain()
                dve.tensor_copy(c_sign[NS_TOK:2 * NS_TOK, :], c_nlam[NS_TOK:2 * NS_TOK, :])
                norm(norm_name(layer, "m"), x3, V_MIX + layer)
                dist = const("dist")

                def mix(h, more):
                    dve.tensor_copy(c_slope, consts[:, bass.ds(h + CO["slopes"][0], 1)])

                    def biased(qb):
                        keys, par = (qb + 1) * P, qb % 2
                        dve.drain()
                        dve.wait_ge(S(L + "score_mm"), h * NCH + qb + 1)
                        for c in range(2):
                            last = dve.scalar_tensor_tensor(at_sb[par][c][:, 0:keys], dist[:, NP_TOK - keys:], c_slope,
                                                            PS[:, 4 + c, 0:keys], ALU.mult, ALU.add)
                        last.then_inc(S(L + "scored"), 1)
                        dve.drain()
                        for c in range(2):
                            dve.reduce_max(c_nm[par][:, c:c + 1], at_sb[par][c][:, 0:keys], AX.X)
                        dve.drain()
                        dve.tensor_scalar(c_nm[par], c_nm[par], -1.0, None, ALU.mult).then_inc(S(L + "maxed"), 1)

                    biased(0)
                    for qb in range(NCH):
                        par = qb % 2
                        if qb < NCH - 1:
                            biased(qb + 1)
                        dve.wait_ge(S(L + "probs"), h * NCH + qb + 1)
                        dve.reciprocal(c_rl[par], c_ls[par])
                        dve.drain()
                        dve.tensor_tensor(c_rl[par][:, 1:2], c_rl[par][:, 1:2], c_nlam, ALU.mult)
                        dve.drain()
                        for c in range(2):
                            last = dve.tensor_scalar(at_diag[par][c], const("ident"), c_rl[par][:, c:c + 1], None, ALU.mult)
                        last.then_inc(S(L + "diag"), 1)
                        dve.wait_ge(S(L + "o_mm"), h * (NCH + 1) + qb + 1)
                        dve.tensor_copy(at_o[:, qb * P:(qb + 1) * P], PS[:, 7, 0:P]).then_inc(S(L + "o_ev"), 1)
                    dve.wait_ge(S(L + "ss_mm"), h + 1)
                    dve.scalar_tensor_tensor(at_ss[0:64, :], const("bs", 64), c_slope[0:64, :], PS[0:64, 5, 0:PAST + NS_TOK],
                                             ALU.mult, ALU.add)
                    dve.drain()
                    dve.reduce_max(c_snm[0:64, :], at_ss[0:64, :], AX.X)
                    dve.drain()
                    dve.tensor_scalar(c_snm[0:64, :], c_snm[0:64, :], -1.0, None, ALU.mult).then_inc(S(L + "smaxed"), 1)
                    dve.wait_ge(S(L + "sprobs"), h + 1)
                    dve.reciprocal(c_srl[0:64, :], c_sls[0:64, :])
                    dve.drain()
                    dve.tensor_tensor(c_sco[0:64, :], c_srl[0:64, :], c_sign[0:64, :], ALU.mult)
                    dve.drain()
                    dve.tensor_scalar(at_selc[0:64, :], const("sel", 64), c_sco[0:64, :], None, ALU.mult)\
                        .then_inc(S(L + "selc"), 1)
                    dve.wait_ge(S(L + "o_mm"), (h + 1) * (NCH + 1))
                    dve.tensor_copy(at_o[:, NP_TOK:NT], PS[:, 7, 0:NS_TOK]).then_inc(S(L + "o_ev"), 1)
                    dve.wait_ge(S(L + "orms"), h + 1)
                    dve.reciprocal(at_rs, at_rs)
                    dve.drain()
                    dve.scalar_tensor_tensor(at_ob, at_o, c_gain, at_rs, ALU.mult, ALU.mult).then_inc(S(L + "ob"), 1)
                    add_rows(L, h, base, 6 if more else 3, (1, 2, 3))

                with dve.Fori(0, HEADS - 1) as h:
                    mix(h, True)
                mix(HEADS - 1, False)
                dve.wait_ge(S(L + "kv_free"), HEADS + 1)

            def rwkv(layer):
                L = "rw_"
                base = UB[layer, "mix"]
                dve.memset(c_gn, GN_EPS)
                norm(norm_name(layer, "m"), x3, V_MIX + layer)
                dve.drain()
                dve.tensor_tensor(o3[:, :, 1:NP_TOK], h3[:, :, 0:NP_TOK - 1], h3[:, :, 1:NP_TOK], ALU.subtract)
                dve.tensor_scalar(o3[:, :, 0:1], h3[:, :, 0:1], -1.0, None, ALU.mult)
                for c in range(KC):
                    hs = h3[:, c, NP_TOK:NT].rearrange("p (b t) -> p b t", t=TB)
                    os_ = o3[:, c, NP_TOK:NT].rearrange("p (b t) -> p b t", t=TB)
                    dve.tensor_tensor(os_[:, :, 1:TB], hs[:, :, 0:TB - 1], hs[:, :, 1:TB], ALU.subtract)
                    dve.tensor_tensor(os_[:, :, 0], vec3[:, V_SHIFT:V_SHIFT + NB, c], hs[:, :, 0], ALU.subtract)
                sh = rw_sh.rearrange("p (c n) -> p c n", c=KC)
                dve.tensor_copy(sh[:, :, 0:1], h3[:, :, NP_TOK - 1:NP_TOK])
                dve.tensor_copy(sh[:, :, 1:9], h3[:, :, NP_TOK + TB - 1:NT:TB]).then_inc(S(L + "shift"), 1)
                dve.drain()
                for n, (mix, dst, mm) in enumerate(((3, rw_xk, 0), (4, rw_xv, 0), (5, rw_xk, 1), (1, rw_xk, 3),
                                                    (2, rw_xv, 3), (0, H, 3))):
                    if mm:
                        dve.wait_ge(S(L + "lora_mm"), mm)
                    for c in range(KC):
                        last = dve.scalar_tensor_tensor(dst[:, c * NT:(c + 1) * NT], o3[:, c, :],
                                                        vec3[:, V_RWMIX + mix, c:c + 1], h3[:, c, :], ALU.mult, ALU.add)
                    last.then_inc(S(L + "xm"), 1)
                dve.wait_ge(S(L + "hidden"), 3)
                dve.memset(rw_st[:, 0:HD], 0.0)
                cur = lambda v: rw_cur[:, v:v + 1]

                def chunks(ap, n, c):
                    return ap.rearrange("p (n c) -> p n c", c=c)

                def pair(mask):
                    return mask.unsqueeze(1).to_broadcast([P, N2, C2])

                def pair32(mask):
                    return mask.unsqueeze(1).to_broadcast([NS_TOK, 2, NS_TOK])

                def mat(ap):
                    return ap.rearrange("p (n c) -> p n c", c=C2)

                def mat32(ap):
                    return ap[0:NS_TOK].rearrange("p (n c) -> p n c", c=NS_TOK)

                def level(n, upper):
                    o = CO["lvl64"][0] + (2 * n + upper) * C2
                    return consts[:, o:o + C2], consts[0:NS_TOK, o:o + NS_TOK]

                def biases(col):
                    dve.tensor_copy(c_w0a0.unsqueeze(2), vec3[:, V_W0:V_A0 + 1, col]).then_inc(S(L + "cur"), 1)

                def mix(h, more):
                    dve.drain()
                    dve.tensor_copy(rw_cur.unsqueeze(2), vec3[:, :, bass.ds(h, 1)])
                    dve.drain()
                    dve.wait_ge(S(L + "ev_k"), h + 1)
                    dve.tensor_scalar(rw_kn, rw_k, cur(V_KK), None, ALU.mult).then_inc(S(L + "kn"), 1)
                    dve.wait_ge(S(L + "ev_w"), h + 1)
                    dve.tensor_tensor_scan(rw_bc, const("reset"), rw_sg, 0.0, ALU.mult, ALU.add)
                    dve.drain()
                    dve.tensor_tensor(rw_pp, rw_bc, rw_sg, ALU.subtract).then_inc(S(L + "bc"), 1)
                    dve.wait_ge(S(L + "ev_a"), h + 1 + 1)
                    if more:
                        biases(bass.ds(h + 1, 1))
                    dve.tensor_scalar(rw_be, rw_a, -1.0, cur(V_KA), ALU.add, ALU.mult)
                    dve.drain()
                    dve.scalar_tensor_tensor(rw_k2, rw_be, 1.0, rw_k, ALU.add, ALU.mult)
                    dve.drain()
                    dve.scalar_tensor_tensor(rw_k, rw_rr, cur(V_RK), rw_k2, ALU.mult, ALU.mult).then_inc(S(L + "rk"), 1)
                    dve.wait_ge(S(L + "kn_rt"), h + 1)
                    dve.tensor_scalar(rw_rn, rw_rn, 1e-12, None, ALU.max)
                    dve.drain()
                    dve.reciprocal(rw_rn, rw_rn)
                    dve.drain()
                    dve.tensor_tensor(rw_kn, rw_kn, rw_rn, ALU.mult)
                    dve.drain()
                    dve.tensor_tensor(rw_be, rw_kn, rw_a, ALU.mult)
                    dve.wait_ge(S(L + "exps"), h + 1)
                    dve.tensor_tensor(rw_pp, rw_pp, rw_kn, ALU.mult)
                    dve.tensor_tensor(rw_k2, rw_k2, rw_pi, ALU.mult)
                    dve.tensor_tensor(rw_r, rw_rr, rw_p, ALU.mult)
                    dve.drain()
                    dve.tensor_tensor(rw_be, rw_be, rw_pi, ALU.mult)
                    dve.drain()
                    pc = chunks(rw_p[:, 0:NP_TOK], N2, C2)[:, :, C2 - 1:C2]
                    pcs = chunks(rw_p[:, NP_TOK:NT], NB, TB)[:, :, TB - 1:TB]
                    for dst, src in ((rw_bc, rw_k2), (rw_kn, rw_be)):
                        dve.tensor_tensor(chunks(dst[:, 0:NP_TOK], N2, C2), chunks(src[:, 0:NP_TOK], N2, C2),
                                          pc.to_broadcast([P, N2, C2]), ALU.mult)
                        last = dve.tensor_tensor(chunks(dst[:, NP_TOK:NT], NB, TB), chunks(src[:, NP_TOK:NT], NB, TB),
                                                 pcs.to_broadcast([P, NB, TB]), ALU.mult)
                    last.then_inc(S(L + "ops"), 1)
                    dve.wait_ge(S(L + "bonus_mm"), h + 1)
                    dve.wait_ge(S(L + "ev_v"), h + 1)
                    dve.tensor_tensor(halves(rw_pi), acc(3), halves(rw_v), ALU.mult).then_inc(S(L + "bonus"), 1)
                    dve.wait_ge(S(L + "mat_mm"), h + 1)
                    for bank, dst, mask in ((4, rw_mt, "strict"), (5, rw_m, "low"), (6, rw_zkt, "strict"),
                                            (7, rw_rbt, "incl"), (0, rw_rkt, "incl")):
                        dve.tensor_tensor(mat(dst), mat(PS[:, bank, :]), pair(const(mask)), ALU.mult)
                    for i in range(2):
                        dve.tensor_tensor(rw_ms[0:NS_TOK, :].rearrange("p (m i c) -> p m i c", m=5, i=2)[:, :, i, :],
                                          PS[0:NS_TOK, 1 + i, 0:5 * NS_TOK].rearrange("p (m c) -> p m c", m=5),
                                          const("masks32", NS_TOK).rearrange("p (m c) -> p m c", m=5), ALU.mult)
                    dve.drain()
                    mts, ms = rw_ms[0:NS_TOK, 0:2 * NS_TOK], rw_ms[0:NS_TOK, 2 * NS_TOK:4 * NS_TOK]
                    for src, src32, dst, dst32, upper in ((rw_m, ms, rw_x, rw_xs, 0), (rw_mt, mts, rw_xt, rw_xts, 1)):
                        big, small = level(0, upper)
                        dve.tensor_tensor(mat(rw_tmp), mat(src), pair(big), ALU.mult)
                        dve.tensor_tensor(mat32(rw_tmps), mat32(src32), pair32(small), ALU.mult)
                        dve.drain()
                        dve.tensor_tensor(mat(dst), pair(const("eye64")), mat(rw_tmp), ALU.subtract)
                        dve.tensor_tensor(mat32(dst32), pair32(const("eye64", NS_TOK)[:, 0:NS_TOK]), mat32(rw_tmps), ALU.subtract)
                        dve.drain()
                    for lv in range(1, 6):
                        big, small = level(lv, 1)
                        if lv == 1:
                            dve.tensor_tensor(mat32(rw_mls), mat32(mts), pair32(small), ALU.mult)
                        dve.tensor_tensor(mat(rw_ml), mat(rw_mt), pair(big), ALU.mult).then_inc(S(L + "inv"), 1)
                        dve.wait_ge(S(L + "xy_mm"), h * 5 + lv)
                        if lv == 1:
                            dve.tensor_tensor(rw_xs[0:NS_TOK, :], rw_xs[0:NS_TOK, :], PS[0:NS_TOK, 5, 128:128 + 2 * NS_TOK], ALU.subtract)
                            dve.tensor_tensor(rw_xts[0:NS_TOK, :], rw_xts[0:NS_TOK, :], PS[0:NS_TOK, 5, 256:256 + 2 * NS_TOK], ALU.subtract)
                        dve.tensor_tensor(rw_x, rw_x, PS[:, 6, :], ALU.subtract)
                        last = dve.tensor_tensor(rw_xt, rw_xt, PS[:, 7, :], ALU.subtract)
                    last.then_inc(S(L + "inv"), 1)
                    def spread(dst, src):
                        return dve.tensor_tensor(dst[0:NS_TOK, :].rearrange("p (b v) -> p b v", b=NB),
                                                 src[0:NS_TOK, 0:P].unsqueeze(1).to_broadcast([NS_TOK, NB, P]),
                                                 const("bmask", NS_TOK).unsqueeze(2).to_broadcast([NS_TOK, NB, P]), ALU.mult)
                    spread(rw_vxs, rw_tms)
                    dve.drain()
                    dve.wait_ge(S(L + "st_free"), h + 1)
                    for n in range(N2):
                        if n:
                            dve.drain()
                        dve.wait_ge(S(L + "ds_mm"), h * N2 + n + 1)
                        dve.scalar_tensor_tensor(rw_st[:, (n + 1) * HD:(n + 2) * HD], rw_st[:, n * HD:(n + 1) * HD],
                                                 rw_p[:, n * C2 + C2 - 1:n * C2 + C2], PS[:, 6 + n % 2, 0:HD],
                                                 ALU.mult, ALU.add).then_inc(S(L + "st"), 1)
                    dve.wait_ge(S(L + "ut_ev"), h + 1)
                    spread(rw_nux, rw_nutm).then_inc(S(L + "nux"), 1)
                    dve.wait_ge(S(L + "o_ev"), h + 1)
                    dve.tensor_tensor(rw_o[:, NP_TOK:NT], rw_o[:, NP_TOK:NT], PS[:, 2, 0:NS_TOK], ALU.add)\
                        .then_inc(S(L + "o_sum"), 1)
                    dve.wait_ge(S(L + "dss_mm"), h + 1)
                    st3 = rw_st0.rearrange("p (b v) -> p b v", b=NB)
                    dve.tensor_tensor(st3, st3, pcs.to_broadcast([P, NB, HD]), ALU.mult)
                    dve.drain()
                    dve.tensor_tensor(rw_st0, rw_st0, PS[:, 6, :], ALU.add).then_inc(S(L + "state"), 1)
                    dve.wait_ge(S(L + "mu_mm"), h + 1)
                    dve.scalar_tensor_tensor(halves(rw_oc), acc(2), -1.0 / HD, halves(rw_o), ALU.mult, ALU.add)\
                        .then_inc(S(L + "oc"), 1)
                    dve.wait_ge(S(L + "gn_rt"), h + 1)
                    dve.reciprocal(rw_rn, rw_rn)
                    dve.drain()
                    dve.tensor_tensor(rw_oc, rw_oc, rw_rn, ALU.mult)
                    dve.drain()
                    dve.tensor_scalar(rw_oc, rw_oc, cur(V_LNW), cur(V_LNB), ALU.mult, ALU.add)
                    dve.drain()
                    dve.tensor_tensor(rw_oc, rw_oc, rw_pi, ALU.add)
                    dve.drain()
                    dve.wait_ge(S(L + "ev_g"), h + 1 + 1)
                    dve.tensor_tensor(rw_oc, rw_oc, rw_g, ALU.mult).then_inc(S(L + "ob"), 1)
                    add_rows(L, h, base, 6 if more else 3, (0, 1, 2, 3))

                biases(slice(0, 1))
                with dve.Fori(0, HEADS - 1) as h:
                    mix(h, True)
                mix(HEADS - 1, False)
                dve.wait_ge(S(L + "st_free"), HEADS + 1)
                dve.wait_ge(S(L + "sh_out"), 16)

            def lower_bounds():
                raw = vec[:, V_LB * KC:(V_LB + 4) * KC]
                mx, sm, rs = lbt[:, 0:KC], lbt[:, KC:2 * KC], lbt[:, 2 * KC:3 * KC]
                dve.tensor_tensor(mx, raw[:, 0:KC], raw[:, KC:2 * KC], ALU.max)
                for n in (2, 3):
                    dve.drain()
                    dve.tensor_tensor(mx, mx, raw[:, n * KC:(n + 1) * KC], ALU.max)
                dve.drain()
                dve.tensor_tensor(lbs[:, :].rearrange("p (l c) -> p l c", l=4), raw.rearrange("p (l c) -> p l c", l=4),
                                  mx.unsqueeze(1).to_broadcast([P, 4, KC]), ALU.subtract).then_inc(S("lb_sub"), 1)
                dve.wait_ge(S("lb_exp"), 1)
                dve.tensor_tensor(sm, lbs[:, 0:KC], lbs[:, KC:2 * KC], ALU.add)
                for n in (2, 3):
                    dve.drain()
                    dve.tensor_tensor(sm, sm, lbs[:, n * KC:(n + 1) * KC], ALU.add)
                dve.drain()
                dve.reciprocal(rs, sm)
                dve.drain()
                dve.tensor_tensor(lbs[:, :].rearrange("p (l c) -> p l c", l=4), lbs[:, :].rearrange("p (l c) -> p l c", l=4),
                                  rs.unsqueeze(1).to_broadcast([P, 4, KC]), ALU.mult)
                dve.drain()
                dve.memset(lbs[:, 0:KC], 0.0)
                for n in (2, 3):
                    dve.drain()
                    dve.tensor_tensor(lbs[:, n * KC:(n + 1) * KC], lbs[:, n * KC:(n + 1) * KC],
                                      lbs[:, (n - 1) * KC:n * KC], ALU.add)
                dve.drain()

            dve.memset(scratch[:, 0:1], RMS_EPS).then_inc(S("setup"), 1)
            dve.wait_ge(S("consts_in"), 16 * NCONST_LOADS)
            lower_bounds()
            for layer in range(depth):
                (hgrn, attention, rwkv)[layer % 3](layer)
                feed_forward(layer)
            norm("nfin", x3, V_FIN)

        @block.gpsimd
        def _(pool):
            for name, count in CREDITS.items():
                pool.sem_inc(S(name), count)

            def settle():
                pool.sem_inc(S("pool_settled"), 1)

            def hgrn(layer):
                L = "hg_"
                j = layer // 3
                with pool.Fori(j * HEADS, (j + 1) * HEADS) as h:
                    pool.dma_start(hg_s0, T["hg_s0"][bass.ds(h, 1), :, :].rearrange("a p n -> (a p) n"))\
                        .then_inc(S(L + "s0_in"), 16)
                    pool.wait_ge(S(L + "state"), h + 1 + 1)
                    settle()
                    pool.dma_start(T["hg_so"][bass.ds(h, 1), :, :].rearrange("a p n -> (a p) n"), hg_s0)\
                        .then_inc(S(L + "st_out"), 16)
                    pool.dma_start(T["hg_po"][bass.ds(h, 1), :, :].rearrange("a p n -> (a p) n"),
                                   hg_s[:, (NCH - 1) * P:NCH * P]).then_inc(S(L + "st_out"), 16)
                    pool.wait_ge(S(L + "st_out"), h * 32 + 32)
                    pool.sem_inc(S(L + "st_free"), 1)

            def head(t, i):
                return t[bass.ds(i, 1), :, :].rearrange("a p n -> (a p) n")

            def attention(layer):
                L = "at_"
                with pool.Fori(0, HEADS) as h:
                    pool.wait_ge(S(L + "st_mm"), h + 1)
                    settle()
                    for n in range(NB * PAGES):
                        page = pool.value_load(pages[0:1, n:n + 1], min_val=0, max_val=NPOOL - 1)
                        pool.dma_start(at_kc[:, n * P:(n + 1) * P], head(T["cache_k"], page * HEADS + h)).then_inc(S(L + "kc_in"), 16)
                    pool.wait_ge(S(L + "ob"), h + 1)
                    settle()
                    for n in range(NB * PAGES):
                        page = pool.value_load(pages[0:1, n:n + 1], min_val=0, max_val=NPOOL - 1)
                        pool.dma_start(at_vc[:, n * P:(n + 1) * P], head(T["cache_v"], page * HEADS + h)).then_inc(S(L + "vc_in"), 16)
                    pool.wait_ge(S(L + "ev_k"), h + 1)
                    settle()
                    pool.dma_start(head(T["k_out"], h), at_k).then_inc(S(L + "kv_out"), 16)
                    pool.wait_ge(S(L + "ev_v"), h + 1 + 1)
                    settle()
                    pool.dma_start(head(T["v_out"], h), at_v).then_inc(S(L + "kv_out"), 16)
                    pool.wait_ge(S(L + "kv_out"), h * 32 + 32)
                    pool.sem_inc(S(L + "kv_free"), 1)

            def rwkv(layer):
                L = "rw_"
                pool.wait_ge(S("norm_sq"), nth(norm_name(layer, "m")) * KC + 1)
                pool.dma_start(rw_lw, T["lora1"]).then_inc(S(L + "lw_in"), 16)
                pool.wait_ge(S(L + "shift"), 1)
                pool.dma_start(T["sh_out"], rw_sh).then_inc(S(L + "sh_out"), 16)

                def low_rank(h):
                    pool.dma_start(rw_ls[0:HD, 0:P], head(T["rw_w2"], h)).then_inc(S(L + "ls_in"), 16)
                    pool.dma_start(rw_ls[0:HD, P:2 * P], head(T["rw_a2"], h)).then_inc(S(L + "ls_in"), 16)
                    pool.dma_start(rw_ls[:, 2 * P:3 * P], head(T["rw_g2"], h)).then_inc(S(L + "ls_in"), 16)

                def states(h, more):
                    pool.dma_start(rw_st0, head(T["rw_s0"], h)).then_inc(S(L + "s0_in"), 16)
                    if more:
                        pool.wait_ge(S(L + "ev_a"), h + 1 + 1)
                        pool.wait_ge(S(L + "ev_g"), h + 1 + 1)
                        settle()
                        low_rank(h + 1)
                    pool.wait_ge(S(L + "state"), h + 1)
                    settle()
                    pool.dma_start(head(T["rw_so"], h), rw_st0).then_inc(S(L + "st_out"), 16)
                    pool.dma_start(head(T["rw_po"], h), rw_st[:, N2 * HD:(N2 + 1) * HD]).then_inc(S(L + "st_out"), 16)
                    pool.wait_ge(S(L + "st_out"), h * 32 + 32)
                    pool.sem_inc(S(L + "st_free"), 1)

                low_rank(0)
                pool.wait_ge(S(L + "lora_mm"), 3)
                with pool.Fori(0, HEADS - 1) as h:
                    states(h, True)
                states(HEADS - 1, False)
                pool.wait_ge(S(L + "sh_out"), 16)

            for layer in range(depth):
                if layer == 1:
                    pool.wait_ge(S("ff_x"), 2 * KC * layer + CREDITS["ff_x"])
                    attention(layer)
                if layer == 2:
                    pool.wait_ge(S("ff_x"), 2 * KC * layer + CREDITS["ff_x"])
                    rwkv(layer)
                if layer == 3:
                    pool.wait_ge(S("ff_x"), 2 * KC * layer + CREDITS["ff_x"])
                if layer % 3 == 0:
                    hgrn(layer)


def column_units(w):
    k, m = w.shape
    return w.reshape(k // P, P, m // P, P).transpose(2, 1, 0, 3).reshape(m // P, P, k)


AHEAD_ORDER = [0, 1, 2] + [4 * h + n for h in range(1, HEADS) for n in (0, 1, 2, -1)] + [4 * HEADS - 1]


def layout(a, depth):
    arr = {}
    x = np.concatenate([a["x_prompt"].reshape(-1, D), a["x_sample"].reshape(-1, D)])
    arr["x"] = x.T.reshape(KC, P, NT).transpose(1, 0, 2).reshape(P, -1)
    rows = [a["norm_mix"], a["norm_ffn"], a["final_norm"][None], a["hg_norm"], a["rw_mix"][0]]
    rows += [a[n].reshape(1, D) for n in ("rw_w0", "rw_a0", "rw_k_k", "rw_k_a", "rw_r_k", "rw_ln_w", "rw_ln_b")]
    rows += [a["hg_lb_raw"], a["state_shift"][0]]
    v = np.concatenate(rows)
    assert v.shape[0] == NV
    arr["vec"] = v.reshape(NV, KC, P).transpose(2, 0, 1).reshape(P, -1)
    arr["subln"] = a["at_subln"].reshape(P, 1)
    arr["consts"], arr["mask"] = constants()
    for layer in range(depth):
        kind, j = layer % 3, layer // 3
        if kind == 0:
            u = column_units(a["hg_w_in"][j]).reshape(4, HEADS, P, D)
            arr[f"w_mix{layer}"] = u[[1, 0, 2, 3]].transpose(1, 0, 2, 3).reshape(4 * HEADS, P, D)
            arr[f"w_hgout{layer}"] = column_units(a["hg_w_out"][j])
        if kind == 1:
            u = column_units(a["at_w_in"][j]).reshape(3, HEADS, P, D)
            u = np.concatenate([u, a["at_w_out"][j].reshape(1, HEADS, P, D)])
            u = u.transpose(1, 0, 2, 3).reshape(4 * HEADS, P, D)
            arr[f"w_mix{layer}"] = u[AHEAD_ORDER]
        if kind == 2:
            u = np.stack([column_units(w) for w in a["rw_w_rkv"][j]] + [a["rw_w_o"][j].reshape(HEADS, P, D)])
            u = u.transpose(1, 0, 2, 3).reshape(4 * HEADS, P, D)
            arr[f"w_mix{layer}"] = u[AHEAD_ORDER]
        up = column_units(a["ffn_w_in"][layer]).reshape(2, FC, P, D).transpose(1, 0, 2, 3)
        arr[f"w_up{layer}"] = up.reshape(2 * FC, P, D)
        down = column_units(a["ffn_w_out"][layer]).reshape(KC, P, 2, SLOT).transpose(2, 0, 1, 3)
        arr[f"w_down{layer}"] = down.reshape(2 * KC, P, SLOT)
    nh = len(a["state_hgrn"])
    arr["hg_s0"] = a["state_hgrn"].transpose(0, 2, 3, 1, 4).reshape(nh * HEADS, P, NB * P)
    arr["lam"] = np.tile(a["at_lam"].reshape(1, -1), (P, 1))
    arr["pages"] = a["page_table"].reshape(1, -1).astype(np.int32)
    arr["cache_k"] = a["cache_k"][0].transpose(0, 2, 3, 1).reshape(NPOOL * HEADS, P, P)
    arr["cache_v"] = a["cache_v"][0].transpose(0, 2, 1, 3).reshape(NPOOL * HEADS, P, P)
    lora = np.concatenate([a["rw_w1"][0], a["rw_a1"][0], a["rw_g1"][0]], 1)
    arr["lora1"] = lora.reshape(KC, P, 256).transpose(1, 0, 2).reshape(P, -1)
    for n in ("w2", "a2", "g2"):
        w = a[f"rw_{n}"][0]
        arr[f"rw_{n}"] = w.reshape(len(w), KC, P).transpose(1, 0, 2)
    st = a["state_rwkv"][0].reshape(NB, HEADS, 2, HD, HD)
    arr["rw_s0"] = st.transpose(1, 2, 4, 0, 3).reshape(HEADS, P, NB * HD)
    return arr


OUTS = {"y": (P, KC * NT), "hg_so": (2 * HEADS, P, NB * P), "hg_po": (2 * HEADS, P, P),
        "k_out": (HEADS, P, NT), "v_out": (HEADS, P, NT), "rw_so": (HEADS, P, NB * HD), "rw_po": (HEADS, P, HD),
        "sh_out": (P, KC * 9)}


def unpack(o):
    y = o["y"].reshape(P, KC, NT).transpose(2, 1, 0).reshape(NT, D)
    so = o["hg_so"].reshape(2, HEADS, P, NB, P).transpose(0, 3, 1, 2, 4)
    po = o["hg_po"].reshape(2, 1, HEADS, P, P)
    k, v = (o[n].transpose(2, 0, 1) for n in ("k_out", "v_out"))
    rs = o["rw_so"].reshape(HEADS, 2, HD, NB, HD).transpose(3, 0, 1, 4, 2).reshape(1, NB, 2 * HEADS, HD, HD)
    rp = o["rw_po"].reshape(HEADS, 2, HD, HD).transpose(0, 1, 3, 2).reshape(1, 1, 2 * HEADS, HD, HD)
    sh = o["sh_out"].reshape(P, KC, 9).transpose(2, 1, 0).reshape(9, D)
    sample = (1, NB, TB, HEADS, P)
    return (y[None, :NP_TOK], y[NP_TOK:].reshape(NB, TB, D), po, so, k[None, None, :NP_TOK], v[None, None, :NP_TOK],
            k[NP_TOK:].reshape(sample), v[NP_TOK:].reshape(sample), rp, sh[None, 0:1], rs, sh[None, 1:])


def kernel(**inputs):
    import concourse.bacc as bacc
    from concourse.bass_utils import run_bass_kernel_spmd

    a = {k: np.asarray(v) for k, v in inputs.items()}
    nc = bacc.Bacc("TRN2", target_bir_lowering=False, num_devices=1)
    arrays = {f"in_{k}": np.ascontiguousarray(v) for k, v in layout(a, DEPTH).items()}
    T = {k[3:]: nc.dram_tensor(k, v.shape, mybir.dt.from_np(v.dtype), kind="ExternalInput").ap()
         for k, v in arrays.items()}
    for k, shape in OUTS.items():
        T[k] = nc.dram_tensor(f"out_{k}", shape, F32, kind="ExternalOutput").ap()
    build(nc, T, DEPTH)
    r = run_bass_kernel_spmd(nc, [arrays], core_ids=[0]).results[0]
    return unpack({k: r[f"out_{k}"] for k in OUTS})
```
